# Optimizing a Trainium2 kernel written in Bass

```python
import jax
import jax.numpy as jnp
from jax import lax
import numpy as np
import math, functools
import jax, jax.numpy as jnp

D_MODEL = 1024
BATCH = 1
SEQ = 512
DEPTH = 2

GRID_W = 64
CTX_LEN = 256
HEAD_DIM = 64
SCALE = HEAD_DIM ** -0.5
ROPE_HALF = HEAD_DIM // 2
ROPE_FREQS = HEAD_DIM // 4
ROPE_THETA = 10000.0
Q_BLOCK = 128
A_HEADS = 8
A_KV_HEADS = 2
B_HEADS = 8
B_KV_HEADS = 2
WINDOW = 128
C_HEADS = 8
NA_ROWS = 8
NA_COLS = 16
D_HEADS = 8
DECAY_LORA = 64
ICLR_LORA = 64
GATE_LORA = 128
GN_EPS = 64e-5
RMS_EPS = 1e-6
NEG_INF = -1e30
FFN_HIDDEN = -(-8 * D_MODEL // (3 * 256)) * 256

A_Q = A_HEADS * HEAD_DIM
A_KV = A_KV_HEADS * HEAD_DIM
B_Q = B_HEADS * HEAD_DIM
B_KV = B_KV_HEADS * HEAD_DIM
C_W = C_HEADS * HEAD_DIM
D_W = D_HEADS * HEAD_DIM
EVEN_WIDTHS = (A_Q, A_KV, A_KV, B_Q, B_KV, B_KV)
EVEN_IN = A_Q + 2 * A_KV + B_Q + 2 * B_KV
EVEN_MIX = A_Q + B_Q
D_SHIFT_W = 3 * D_W + DECAY_LORA + ICLR_LORA + GATE_LORA
ODD_IN = 3 * C_W + D_SHIFT_W
ODD_MIX = C_W + D_W
N_EVEN = (DEPTH + 1) // 2
N_ODD = DEPTH // 2


def _split(t, widths):
    return jnp.split(t, [int(o) for o in np.cumsum(widths)[:-1]], axis=-1)

def rms_norm(t, gain):
    tf = t.astype(jnp.float32)
    tf = tf * lax.rsqrt(jnp.mean(tf * tf, axis=-1, keepdims=True) + RMS_EPS)
    return (tf * gain.astype(jnp.float32)).astype(t.dtype)

def modulate(t, shift, scale):
    return t * (1 + scale) + shift

def heads(t, n):
    return t.reshape(t.shape[:-1] + (n, HEAD_DIM))

def group(q, n_kv):
    return q.reshape(q.shape[:2] + (n_kv, q.shape[2] // n_kv, HEAD_DIM))

def axial_rope_tables(n_tokens):
    t = jnp.arange(n_tokens, dtype=jnp.int32)
    row = (t // GRID_W).astype(jnp.float32)
    col = (t % GRID_W).astype(jnp.float32)
    inv = ROPE_THETA ** (-jnp.arange(ROPE_FREQS, dtype=jnp.float32) / ROPE_FREQS)
    ang = jnp.concatenate([row[:, None] * inv, col[:, None] * inv], axis=-1)
    return jnp.cos(ang), jnp.sin(ang)

def apply_rope(t, cos, sin):
    c = cos[None, :, None, :].astype(t.dtype)
    s = sin[None, :, None, :].astype(t.dtype)
    t1, t2 = t[..., :ROPE_HALF], t[..., ROPE_HALF:]
    return jnp.concatenate([t1 * c - t2 * s, t1 * s + t2 * c], axis=-1)

def _sink_column(sink, shape):
    col = sink.astype(jnp.float32).reshape(1, shape[1], shape[2], 1, 1)
    return jnp.broadcast_to(col, shape[:-1] + (1,))

def dense_attention(q, k, v, sink=None):
    B, L, HKV, G, _ = q.shape
    n = k.shape[1]
    s = jnp.einsum('bqkgd,bnkd->bkgqn', q, k, preferred_element_type=jnp.float32) * SCALE
    if sink is not None:
        s = jnp.concatenate([s, _sink_column(sink, s.shape)], axis=-1)
    p = jax.nn.softmax(s, axis=-1)[..., :n].astype(v.dtype)
    return jnp.einsum('bkgqn,bnkd->bqkgd', p, v).reshape(B, L, HKV * G * HEAD_DIM)

def global_attention(q, k, v, kc, vc):
    B, S, HKV, G, _ = q.shape
    nblk = S // Q_BLOCK
    keys = jnp.concatenate([k, kc], axis=1)
    vals = jnp.concatenate([v, vc], axis=1)
    qb = jnp.moveaxis(q.reshape(B, nblk, Q_BLOCK, HKV, G, HEAD_DIM), 1, 0)

    def block(qblk):
        s = jnp.einsum('bqkgd,bnkd->bkgqn', qblk, keys, preferred_element_type=jnp.float32) * SCALE
        p = jax.nn.softmax(s, axis=-1).astype(vals.dtype)
        return jnp.einsum('bkgqn,bnkd->bqkgd', p, vals)

    o = lax.map(block, qb)
    return jnp.moveaxis(o, 0, 1).reshape(B, S, HKV * G * HEAD_DIM)

def window_attention(q, k, v, kc, vc, sink):
    B, S, HKV, G, _ = q.shape
    nblk = S // Q_BLOCK
    span = Q_BLOCK + 2 * WINDOW
    n_ctx = kc.shape[1]
    pad = ((0, 0), (WINDOW, WINDOW), (0, 0), (0, 0))
    kp, vp = jnp.pad(k, pad), jnp.pad(v, pad)
    qb = jnp.moveaxis(q.reshape(B, nblk, Q_BLOCK, HKV, G, HEAD_DIM), 1, 0)
    qi = jnp.arange(Q_BLOCK)[:, None]
    kj = jnp.arange(span)[None, :]
    band = jnp.abs(kj - WINDOW - qi) <= WINDOW

    def block(args):
        qblk, start = args
        ks = lax.dynamic_slice_in_dim(kp, start, span, axis=1)
        vs = lax.dynamic_slice_in_dim(vp, start, span, axis=1)
        pos = start - WINDOW + kj
        valid = band & (pos >= 0) & (pos < S)
        s_loc = jnp.einsum('bqkgd,bnkd->bkgqn', qblk, ks, preferred_element_type=jnp.float32) * SCALE
        s_loc = jnp.where(valid, s_loc, NEG_INF)
        s_ctx = jnp.einsum('bqkgd,bnkd->bkgqn', qblk, kc, preferred_element_type=jnp.float32) * SCALE
        s = jnp.concatenate([s_loc, s_ctx, _sink_column(sink, s_loc.shape)], axis=-1)
        p = jax.nn.softmax(s, axis=-1).astype(v.dtype)
        return (jnp.einsum('bkgqn,bnkd->bqkgd', p[..., :span], vs)
                + jnp.einsum('bkgqn,bnkd->bqkgd', p[..., span:span + n_ctx], vc))

    o = lax.map(block, (qb, jnp.arange(nblk) * Q_BLOCK))
    return jnp.moveaxis(o, 0, 1).reshape(B, S, HKV * G * HEAD_DIM)

def neighborhood_attention(q, k, v, kc, vc, rpb):
    B, S, H, _ = q.shape
    rows = S // GRID_W
    kr = min(NA_ROWS, rows)
    n_loc = kr * NA_COLS
    qg = jnp.moveaxis(q.reshape(B, rows, GRID_W, H, HEAD_DIM), 1, 0)
    kg = k.reshape(B, rows, GRID_W, H, HEAD_DIM)
    vg = v.reshape(B, rows, GRID_W, H, HEAD_DIM)
    col = jnp.arange(GRID_W)
    col_idx = jnp.clip(col - NA_COLS // 2, 0, GRID_W - NA_COLS)[:, None] + jnp.arange(NA_COLS)[None, :]
    dcol = col_idx - col[:, None] + NA_COLS - 1
    row_start = jnp.clip(jnp.arange(rows) - kr // 2, 0, rows - kr)

    def block(args):
        q_row, r, rs = args
        ks = lax.dynamic_slice_in_dim(kg, rs, kr, axis=1)[:, :, col_idx]
        vs = lax.dynamic_slice_in_dim(vg, rs, kr, axis=1)[:, :, col_idx]
        drow = rs + jnp.arange(kr) - r + NA_ROWS - 1
        bias = rpb[:, drow[None, :, None], dcol[:, None, :]].astype(jnp.float32)
        s_loc = jnp.einsum('bchd,bicjhd->bhcij', q_row, ks, preferred_element_type=jnp.float32) * SCALE + bias
        s_ctx = jnp.einsum('bchd,bnhd->bhcn', q_row, kc, preferred_element_type=jnp.float32) * SCALE
        s = jnp.concatenate([s_loc.reshape(B, H, GRID_W, n_loc), s_ctx], axis=-1)
        p = jax.nn.softmax(s, axis=-1).astype(v.dtype)
        p_loc = p[..., :n_loc].reshape(B, H, GRID_W, kr, NA_COLS)
        return (jnp.einsum('bhcij,bicjhd->bchd', p_loc, vs)
                + jnp.einsum('bhcn,bnhd->bchd', p[..., n_loc:], vc))

    o = lax.map(block, (qg, jnp.arange(rows), row_start))
    return jnp.moveaxis(o, 0, 1).reshape(B, S, H * HEAD_DIM)

def centred_shift_mix(z, mu):
    zp = jnp.pad(z, ((0, 0), (1, 1), (0, 0)))
    return z + (0.5 * (zp[:, :-2] + zp[:, 2:]) - z) * mu

def rwkv7_inputs(zd, w0, w2, a0, a2, g2, k_k, k_a):
    r, k, v, wd, ad, gd = _split(zd, (D_W, D_W, D_W, DECAY_LORA, ICLR_LORA, GATE_LORA))
    g = jax.nn.sigmoid(gd) @ g2
    kk = heads(k * k_k, D_HEADS).astype(jnp.float32)
    kk = kk / jnp.maximum(jnp.sqrt(jnp.sum(kk * kk, axis=-1, keepdims=True)), 1e-12)
    decay, kd, av = [], [], []
    for d in range(2):
        w = -jax.nn.softplus(-(w0[d] + jnp.tanh(wd) @ w2[d])) - 0.5
        a = jax.nn.sigmoid(a0[d] + ad @ a2[d])
        decay.append(heads(jnp.exp(-jnp.exp(w.astype(jnp.float32))), D_HEADS))
        kd.append(heads(k * (1 + (a - 1) * k_a), D_HEADS))
        av.append(heads(a, D_HEADS))
    return {"r": heads(r, D_HEADS), "v": heads(v, D_HEADS), "kk": kk, "g": g,
            "decay": decay, "k": kd, "a": av}

def wkv7_scan(state0, p, d, reverse, emit):
    seq = [p["decay"][d], p["k"][d], p["v"], p["kk"], p["a"][d]] + ([p["r"]] if emit else [])
    xs = tuple(jnp.moveaxis(t.astype(jnp.float32), 1, 0) for t in seq)

    def step(S, inp):
        w_t, k_t, v_t, kk_t, a_t = inp[:5]
        sa = jnp.einsum('bhvk,bhk->bhv', S, kk_t)
        S = (S * w_t[:, :, None, :] - sa[..., None] * (kk_t * a_t)[:, :, None, :]
             + v_t[..., None] * k_t[:, :, None, :])
        return S, (jnp.einsum('bhvk,bhk->bhv', S, inp[5]) if emit else None)

    S, ys = lax.scan(step, state0, xs, reverse=reverse)
    return S, (jnp.moveaxis(ys, 0, 1) if emit else None)

def rwkv7_readout(y, p, r_k, ln_w, ln_b):
    B, L, H, N = y.shape
    mean = jnp.mean(y, axis=-1, keepdims=True)
    var = jnp.mean(jnp.square(y - mean), axis=-1, keepdims=True)
    yn = ((y - mean) * lax.rsqrt(var + GN_EPS)).reshape(B, L, H * N)
    yn = yn * ln_w.astype(jnp.float32) + ln_b.astype(jnp.float32)
    r = p["r"].astype(jnp.float32)
    ksum = (p["k"][0] + p["k"][1]).astype(jnp.float32)
    bonus = jnp.sum(r * ksum * r_k.astype(jnp.float32), axis=-1, keepdims=True) * p["v"].astype(jnp.float32)
    return (yn + bonus.reshape(B, L, H * N)) * p["g"].astype(jnp.float32)

def even_mixer(h, hc, w_in, w_out, q_gain, k_gain, sink, cos, sin, need_ctx):
    qa, ka, va, qb, kb, vb = _split(h @ w_in, EVEN_WIDTHS)
    qca, kca, vca, qcb, kcb, vcb = _split(hc @ w_in, EVEN_WIDTHS)
    qa = apply_rope(rms_norm(heads(qa, A_HEADS), q_gain), cos, sin)
    ka = apply_rope(rms_norm(heads(ka, A_KV_HEADS), k_gain), cos, sin)
    kca = rms_norm(heads(kca, A_KV_HEADS), k_gain)
    va, vca = heads(va, A_KV_HEADS), heads(vca, A_KV_HEADS)
    qb = apply_rope(heads(qb, B_HEADS), cos, sin)
    kb = apply_rope(heads(kb, B_KV_HEADS), cos, sin)
    kcb, vb, vcb = heads(kcb, B_KV_HEADS), heads(vb, B_KV_HEADS), heads(vcb, B_KV_HEADS)
    y_a = global_attention(group(qa, A_KV_HEADS), ka, va, kca, vca)
    y_b = window_attention(group(qb, B_KV_HEADS), kb, vb, kcb, vcb, sink)
    y = jnp.concatenate([y_a, y_b], axis=-1) @ w_out
    if not need_ctx:
        return y, None
    qca = rms_norm(heads(qca, A_HEADS), q_gain)
    yc_a = dense_attention(group(qca, A_KV_HEADS), kca, vca)
    yc_b = dense_attention(group(heads(qcb, B_HEADS), B_KV_HEADS), kcb, vcb, sink)
    return y, jnp.concatenate([yc_a, yc_b], axis=-1) @ w_out

def odd_mixer(h, hc, w_in, w_out, rpb, mu, w0, w2, a0, a2, g2, k_k, k_a, r_k, ln_w, ln_b, need_ctx):
    q, k, v, zd = _split(h @ w_in, (C_W, C_W, C_W, D_SHIFT_W))
    qc, kc, vc, zdc = _split(hc @ w_in, (C_W, C_W, C_W, D_SHIFT_W))
    kc, vc = heads(kc, C_HEADS), heads(vc, C_HEADS)
    y_c = neighborhood_attention(heads(q, C_HEADS), heads(k, C_HEADS), heads(v, C_HEADS), kc, vc, rpb)
    lat = rwkv7_inputs(centred_shift_mix(zd, mu), w0, w2, a0, a2, g2, k_k, k_a)
    cx = rwkv7_inputs(centred_shift_mix(zdc, mu), w0, w2, a0, a2, g2, k_k, k_a)
    zero = jnp.zeros((h.shape[0], D_HEADS, HEAD_DIM, HEAD_DIM), jnp.float32)
    s_fwd, yc_fwd = wkv7_scan(zero, cx, 0, False, need_ctx)
    s_bwd, yc_bwd = wkv7_scan(zero, cx, 1, True, need_ctx)
    _, y_fwd = wkv7_scan(s_fwd, lat, 0, False, True)
    _, y_bwd = wkv7_scan(s_bwd, lat, 1, True, True)
    y_d = rwkv7_readout(y_fwd + y_bwd, lat, r_k, ln_w, ln_b).astype(h.dtype)
    y = jnp.concatenate([y_c, y_d], axis=-1) @ w_out
    if not need_ctx:
        return y, None
    yc_c = dense_attention(heads(qc, C_HEADS)[:, :, :, None], kc, vc)
    yc_d = rwkv7_readout(yc_fwd + yc_bwd, cx, r_k, ln_w, ln_b).astype(hc.dtype)
    return y, jnp.concatenate([yc_c, yc_d], axis=-1) @ w_out

def swiglu(h, w_in, w_out):
    gate, up = jnp.split(h @ w_in, 2, axis=-1)
    return (jax.nn.silu(gate) * up) @ w_out

def first_inputs(seed: int = 0) -> dict:
    key = jax.random.key(seed)
    ks = iter(jax.random.split(key, 40))

    def nrm(shape, scale):
        return scale * jax.random.normal(next(ks), shape, jnp.float32)

    D = D_MODEL
    return {
        "x": nrm((BATCH, SEQ, D), 1.0),
        "c": nrm((BATCH, D), 1.0),
        "ctx": nrm((BATCH, CTX_LEN, D), 1.0),
        "c_ctx": nrm((D,), 1.0),
        "w_mod": nrm((DEPTH, D, 6 * D), 0.5 * D ** -0.5),
        "b_mod": nrm((DEPTH, 6 * D), 0.02),
        "norm_mix": 1.0 + nrm((DEPTH, D), 0.02),
        "norm_ffn": 1.0 + nrm((DEPTH, D), 0.02),
        "w_in_even": nrm((N_EVEN, D, EVEN_IN), D ** -0.5),
        "w_out_even": nrm((N_EVEN, EVEN_MIX, D), EVEN_MIX ** -0.5),
        "q_norm_a": 1.0 + nrm((N_EVEN, HEAD_DIM), 0.02),
        "k_norm_a": 1.0 + nrm((N_EVEN, HEAD_DIM), 0.02),
        "sink_b": nrm((N_EVEN, B_HEADS), 0.5),
        "w_in_odd": nrm((N_ODD, D, ODD_IN), D ** -0.5),
        "w_out_odd": nrm((N_ODD, ODD_MIX, D), ODD_MIX ** -0.5),
        "rpb_c": nrm((N_ODD, C_HEADS, 2 * NA_ROWS - 1, 2 * NA_COLS - 1), 0.2),
        "shift_mu": jax.random.uniform(next(ks), (N_ODD, D_SHIFT_W), jnp.float32),
        "decay_w0": -1.0 + nrm((N_ODD, 2, D_W), 0.3),
        "decay_w2": nrm((N_ODD, 2, DECAY_LORA, D_W), 0.1),
        "iclr_a0": nrm((N_ODD, 2, D_W), 0.3),
        "iclr_a2": nrm((N_ODD, 2, ICLR_LORA, D_W), 0.1),
        "gate_g2": nrm((N_ODD, GATE_LORA, D_W), GATE_LORA ** -0.5),
        "k_k": 0.85 + nrm((N_ODD, D_W), 0.05),
        "k_a": 1.0 + nrm((N_ODD, D_W), 0.05),
        "r_k": nrm((N_ODD, D_HEADS, HEAD_DIM), 0.1),
        "ln_x_w": 1.0 + nrm((N_ODD, D_W), 0.02),
        "ln_x_b": nrm((N_ODD, D_W), 0.02),
        "w_ffn_in": nrm((DEPTH, D, 2 * FFN_HIDDEN), D ** -0.5),
        "w_ffn_out": nrm((DEPTH, FFN_HIDDEN, D), FFN_HIDDEN ** -0.5),
        "norm_out": 1.0 + nrm((D,), 0.02),
    }

def first_block(x, c, ctx, c_ctx, w_mod, b_mod, norm_mix, norm_ffn, w_in_even, w_out_even, q_norm_a, k_norm_a,
              sink_b, w_in_odd, w_out_odd, rpb_c, shift_mu, decay_w0, decay_w2, iclr_a0, iclr_a2, gate_g2,
              k_k, k_a, r_k, ln_x_w, ln_x_b, w_ffn_in, w_ffn_out, norm_out):
    cos, sin = axial_rope_tables(x.shape[1])
    silu_c = jax.nn.silu(c)
    silu_cc = jax.nn.silu(c_ctx)
    for layer in range(DEPTH):
        need_ctx = layer < DEPTH - 1
        mod = (silu_c @ w_mod[layer] + b_mod[layer])[:, None, :]
        modc = silu_cc @ w_mod[layer] + b_mod[layer]
        sh1, sc1, g1, sh2, sc2, g2 = jnp.split(mod, 6, axis=-1)
        csh1, csc1, cg1, csh2, csc2, cg2 = jnp.split(modc, 6, axis=-1)
        h = modulate(rms_norm(x, norm_mix[layer]), sh1, sc1)
        hc = modulate(rms_norm(ctx, norm_mix[layer]), csh1, csc1)
        i = layer // 2
        if layer % 2 == 0:
            y, yc = even_mixer(h, hc, w_in_even[i], w_out_even[i], q_norm_a[i], k_norm_a[i], sink_b[i],
                               cos, sin, need_ctx)
        else:
            y, yc = odd_mixer(h, hc, w_in_odd[i], w_out_odd[i], rpb_c[i], shift_mu[i], decay_w0[i], decay_w2[i],
                              iclr_a0[i], iclr_a2[i], gate_g2[i], k_k[i], k_a[i], r_k[i], ln_x_w[i], ln_x_b[i],
                              need_ctx)
        x = x + g1 * y
        x = x + g2 * swiglu(modulate(rms_norm(x, norm_ffn[layer]), sh2, sc2), w_ffn_in[layer], w_ffn_out[layer])
        if need_ctx:
            ctx = ctx + cg1 * yc
            ctx = ctx + cg2 * swiglu(modulate(rms_norm(ctx, norm_ffn[layer]), csh2, csc2),
                                     w_ffn_in[layer], w_ffn_out[layer])
    return rms_norm(x, norm_out)


_first_inputs = first_inputs


def first_inputs(seed=0):
    import zlib

    import numpy as np

    out = dict(_first_inputs(seed))
    spreads = {}
    factors = {'norm_mix': 8.0,
     'norm_ffn': 6.502,
     'q_norm_a': 8.0,
     'k_norm_a': 8.0,
     'sink_b': 8.0,
     'rpb_c': 64.0,
     'decay_w0': 30.288,
     'decay_w2': 33.528,
     'iclr_a0': 4.053,
     'k_k': 64.0,
     'k_a': 7.039,
     'ln_x_w': 64.0,
     'ln_x_b': 64.0,
     'norm_out': 8.87}
    for name, (base, spread) in spreads.items():
        noise = np.random.default_rng([zlib.crc32(name.encode()), seed]).standard_normal(out[name].shape)
        drawn = base * np.exp(spread * noise) if base else spread * noise
        out[name] = jnp.asarray(drawn.astype(out[name].dtype))
    for name, factor in factors.items():
        out[name] = (out[name] * factor).astype(out[name].dtype)
    return out


_narrow_inputs = first_inputs


def first_inputs(seed=0):

    out = dict(_narrow_inputs(seed))
    wider = {'rpb_c': 10.28, 'k_k': 12.0, 'ln_x_w': 12.0, 'ln_x_b': 12.0, 'norm_out': 3.41}
    for name, times in wider.items():
        mean = out[name].mean()
        out[name] = (mean + times * (out[name] - mean)).astype(out[name].dtype)
    return out


N_MOD = 6
NORM_EPS = 1e-6
D_FF = -(-8 * D_MODEL // (3 * 256)) * 256

D_MIX = D_MODEL
GLA_HEADS = 4
GLA_DV = D_MIX // 2 // GLA_HEADS
GLA_DK = GLA_DV // 2
GLA_LR = 16
GLA_TAU = 16.0
GLA_CHUNK = 64
GLA_HK = GLA_HEADS * GLA_DK
GLA_HV = GLA_HEADS * GLA_DV
GMLP_GROUPS = 4
GMLP_WIDTH = D_MIX // 2
GMLP_GC = GMLP_WIDTH // GMLP_GROUPS
GMLP_CHUNK = 128
AB_STATE_SPLITS = (GLA_HK, GLA_HV, GLA_LR, GLA_LR)
AB_OUT_SPLITS = (GLA_HK, GLA_HV, GMLP_WIDTH, GMLP_WIDTH)
AB_IN = sum(AB_STATE_SPLITS + AB_OUT_SPLITS)

SSD_INNER = 2 * D_MODEL
SSD_HEADDIM = 64
SSD_HEADS = SSD_INNER // SSD_HEADDIM
SSD_GROUPS = 4
SSD_HPG = SSD_HEADS // SSD_GROUPS
SSD_STATE = 128
SSD_CHUNK = 128
SSD_CONV = 5
SSD_GS = SSD_GROUPS * SSD_STATE
SSD_CONV_DIM = SSD_INNER + 2 * SSD_GS
SSD_IN = SSD_CONV_DIM + 2 * SSD_HEADS + SSD_INNER


def rms_norm_2(x, g):
    xf = x.astype(jnp.float32)
    y = xf * lax.rsqrt(jnp.mean(xf * xf, axis=-1, keepdims=True) + NORM_EPS)
    return y.astype(x.dtype) * g

def group_rms_norm(x, g, groups):
    shp = x.shape
    xf = x.astype(jnp.float32).reshape(shp[:-1] + (groups, shp[-1] // groups))
    y = xf * lax.rsqrt(jnp.mean(xf * xf, axis=-1, keepdims=True) + NORM_EPS)
    return y.reshape(shp).astype(x.dtype) * g

def layer_norm(x, g):
    xf = x.astype(jnp.float32)
    mu = jnp.mean(xf, axis=-1, keepdims=True)
    var = jnp.mean(jnp.square(xf - mu), axis=-1, keepdims=True)
    return ((xf - mu) * lax.rsqrt(var + NORM_EPS)).astype(x.dtype) * g

def modulate_2(h, shift, scale):
    return h * (1 + scale) + shift

def split_cols(a, sizes):
    idx = [int(i) for i in np.cumsum(sizes)[:-1]]
    return jnp.split(a, idx, axis=-1)

def swiglu_2(h, w_in, w_out):
    g, u = jnp.split(h @ w_in, 2, axis=-1)
    return (jax.nn.silu(g) * u) @ w_out

def to_col_major(x):
    bsz, t, d = x.shape
    rows = t // GRID_W
    return x.reshape(bsz, rows, GRID_W, d).transpose(0, 2, 1, 3).reshape(bsz, t, d)

def to_row_major(x):
    bsz, t, d = x.shape
    rows = t // GRID_W
    return x.reshape(bsz, GRID_W, rows, d).transpose(0, 2, 1, 3).reshape(bsz, t, d)

def dwconv_centred(x, w, b):
    pad = (w.shape[0] - 1) // 2
    y = lax.conv_general_dilated(x, w.astype(x.dtype)[:, None, :], window_strides=(1,),
                                 padding=[(pad, pad)], dimension_numbers=('NWC', 'WIO', 'NWC'),
                                 feature_group_count=x.shape[-1])
    return y + b

def bidir_prefix_scan(scan_f, scan_b, ctx_f, ctx_b, lat_f, lat_b, s0, ctx_out):
    flip = lambda a: None if a is None else jnp.flip(a, axis=1)
    y_cf, s_cf = scan_f(*ctx_f, s0, ctx_out)
    y_xf, _ = scan_f(*lat_f, s_cf, True)
    y_cb, s_cb = scan_b(*[flip(a) for a in ctx_b], s0, ctx_out)
    y_xb, _ = scan_b(*[flip(a) for a in lat_b], s_cb, True)
    y_x = y_xf + flip(y_xb)
    y_c = y_cf + flip(y_cb) if ctx_out else None
    return y_x, y_c

def gla_chunked(k, v, log_a, q, s0, with_output):
    bsz, t, h, dk = k.shape
    dv = v.shape[-1]
    n = t // GLA_CHUNK
    chunks = lambda a: a.astype(jnp.float32).reshape(bsz, n, GLA_CHUNK, h, a.shape[-1])
    k, v, log_a = chunks(k), chunks(v), chunks(log_a)
    b = jnp.cumsum(log_a, axis=2)
    b_last = b[:, :, -1]
    d_state = jnp.einsum('bnlhk,bnlhv->bnhkv', k * jnp.exp(b_last[:, :, None] - b), v)

    def step(s, inp):
        decay, ds = inp
        return decay[..., None] * s + ds, s

    s_final, s_prev = lax.scan(step, s0, (jnp.moveaxis(jnp.exp(b_last), 1, 0), jnp.moveaxis(d_state, 1, 0)))
    if not with_output:
        return None, s_final
    q = chunks(q)
    s_prev = jnp.moveaxis(s_prev, 0, 1)
    q_dec = q * jnp.exp(b)
    o_inter = jnp.einsum('bnlhk,bnhkv->bnlhv', q_dec, s_prev)
    scores = jnp.einsum('bnlhk,bnshk->bnhls', q_dec, k * jnp.exp(-b))
    tri = jnp.tril(jnp.ones((GLA_CHUNK, GLA_CHUNK), dtype=bool))
    scores = jnp.where(tri, scores, 0.0)
    o_intra = jnp.einsum('bnhls,bnshv->bnlhv', scores, v)
    return (o_inter + o_intra).reshape(bsz, t, h, dv), s_final

def ssd_chunked(x, bm, dt, cm, s0, with_output, a_coef):
    bsz, t = x.shape[:2]
    n = t // SSD_CHUNK
    f = lambda z: z.astype(jnp.float32).reshape((bsz, n, SSD_CHUNK) + z.shape[2:])
    x, bm, dt = f(x), f(bm), f(dt)
    acum = jnp.cumsum(dt * a_coef, axis=2)
    a_last = acum[:, :, -1]
    xdt = x * dt[..., None]
    states = jnp.einsum('bclgn,bclgh,bclghp->bcghpn', bm, jnp.exp(a_last[:, :, None] - acum), xdt)

    def step(s, inp):
        decay, st = inp
        return decay[..., None, None] * s + st, s

    s_final, s_prev = lax.scan(step, s0, (jnp.moveaxis(jnp.exp(a_last), 1, 0), jnp.moveaxis(states, 1, 0)))
    if not with_output:
        return None, s_final
    cm = f(cm)
    s_prev = jnp.moveaxis(s_prev, 0, 1)
    y_off = jnp.einsum('bclgn,bcghpn->bclghp', cm, s_prev) * jnp.exp(acum)[..., None]
    at = jnp.moveaxis(acum, 2, -1)
    seg = at[..., :, None] - at[..., None, :]
    tri = jnp.tril(jnp.ones((SSD_CHUNK, SSD_CHUNK), dtype=bool))
    decay = jnp.exp(jnp.where(tri, seg, -jnp.inf))
    cb = jnp.einsum('bclgn,bcsgn->bcgls', cm, bm)
    y_diag = jnp.einsum('bcgls,bcghls,bcsghp->bclghp', cb, decay, xdt)
    return (y_diag + y_off).reshape((bsz, t) + x.shape[3:]), s_final

def ab_project(h, w_in, gate_w, gate_b, full):
    bsz, t, _ = h.shape
    sizes = AB_STATE_SPLITS + AB_OUT_SPLITS if full else AB_STATE_SPLITS
    parts = split_cols(h @ w_in[:, :sum(sizes)], sizes)
    heads = lambda a: a.reshape(bsz, t, GLA_HEADS, -1)
    k, v, lr_f, lr_b = parts[:4]
    la_f = jax.nn.log_sigmoid((lr_f @ gate_w[0] + gate_b[0]).astype(jnp.float32)) / GLA_TAU
    la_b = jax.nn.log_sigmoid((lr_b @ gate_w[1] + gate_b[1]).astype(jnp.float32)) / GLA_TAU
    state = (heads(k), heads(v), heads(la_f), heads(la_b))
    if not full:
        return state, None
    q, r, u, g = parts[4:]
    return state, (heads(q) * GLA_DK ** -0.5, r, u, g)

def gmlp_chunk_mix(u, v, vnorm_g, spatial_w, spatial_b):
    bsz, t, _ = u.shape
    n = t // GMLP_CHUNK
    u = jax.nn.gelu(u)
    v = layer_norm(jax.nn.gelu(v), vnorm_g).reshape(bsz, n, GMLP_CHUNK, GMLP_GROUPS, GMLP_GC)
    s = jnp.einsum('gts,bnsgc->bntgc', spatial_w, v) + spatial_b.T[:, :, None]
    return u * s.reshape(bsz, t, GMLP_WIDTH)

def mixer_gla_gmlp(hx, hc, w_in, gate_w, gate_b, gla_norm_g, vnorm_g, spatial_w, spatial_b, w_out, ctx_out):
    (kx, vx, lfx, lbx), (qx, rx, ux, gx) = ab_project(hx, w_in, gate_w, gate_b, True)
    (kc, vc, lfc, lbc), rest_c = ab_project(hc, w_in, gate_w, gate_b, ctx_out)
    qc = rest_c[0] if ctx_out else None
    s0 = jnp.zeros((hx.shape[0], GLA_HEADS, GLA_DK, GLA_DV), jnp.float32)
    ox, oc = bidir_prefix_scan(gla_chunked, gla_chunked,
                               [kc, vc, lfc, qc], [kc, vc, lbc, qc],
                               [kx, vx, lfx, qx], [kx, vx, lbx, qx], s0, ctx_out)

    def merge(o, r, u, g):
        bsz, t = o.shape[:2]
        a = group_rms_norm(o.reshape(bsz, t, GLA_HV), gla_norm_g, GLA_HEADS) * jax.nn.silu(r)
        b = gmlp_chunk_mix(u, g, vnorm_g, spatial_w, spatial_b)
        return jnp.concatenate([a.astype(b.dtype), b], axis=-1) @ w_out

    yx = merge(ox, rx, ux, gx)
    yc = merge(oc, rest_c[1], rest_c[2], rest_c[3]) if ctx_out else None
    return yx, yc

def ssd_project(h, w_in, conv_w, conv_b, dt_bias, full):
    bsz, t, _ = h.shape
    if full:
        p = h @ w_in
        xbc = jax.nn.silu(dwconv_centred(p[..., :SSD_CONV_DIM], conv_w, conv_b))
        xs, bm, cm = split_cols(xbc, (SSD_INNER, SSD_GS, SSD_GS))
        dt_raw = p[..., SSD_CONV_DIM:SSD_CONV_DIM + 2 * SSD_HEADS]
        z = p[..., SSD_CONV_DIM + 2 * SSD_HEADS:]
        cm = cm.reshape(bsz, t, SSD_GROUPS, SSD_STATE)
    else:
        nxb = SSD_INNER + SSD_GS
        xb = jax.nn.silu(dwconv_centred(h @ w_in[:, :nxb], conv_w[:, :nxb], conv_b[:nxb]))
        xs, bm = split_cols(xb, (SSD_INNER, SSD_GS))
        dt_raw = h @ w_in[:, SSD_CONV_DIM:SSD_CONV_DIM + 2 * SSD_HEADS]
        cm = None
        z = None
    dt = jax.nn.softplus(dt_raw.astype(jnp.float32).reshape(bsz, t, 2, SSD_HEADS) + dt_bias)
    dt = dt.reshape(bsz, t, 2, SSD_GROUPS, SSD_HPG)
    xs = xs.reshape(bsz, t, SSD_GROUPS, SSD_HPG, SSD_HEADDIM)
    bm = bm.reshape(bsz, t, SSD_GROUPS, SSD_STATE)
    return xs, bm, cm, dt[:, :, 0], dt[:, :, 1], z

def mixer_ssd(hx, hc, w_in, conv_w, conv_b, dt_bias, a_log, d_skip, norm_g, w_out, ctx_out):
    xx, bx, cx, dfx, dbx, zx = ssd_project(hx, w_in, conv_w, conv_b, dt_bias, True)
    xc, bc, cc, dfc, dbc, zc = ssd_project(hc, w_in, conv_w, conv_b, dt_bias, ctx_out)
    a = -jnp.exp(a_log.astype(jnp.float32)).reshape(2, SSD_GROUPS, SSD_HPG)
    s0 = jnp.zeros((hx.shape[0], SSD_GROUPS, SSD_HPG, SSD_HEADDIM, SSD_STATE), jnp.float32)
    yx, yc = bidir_prefix_scan(functools.partial(ssd_chunked, a_coef=a[0]),
                               functools.partial(ssd_chunked, a_coef=a[1]),
                               [xc, bc, dfc, cc], [xc, bc, dbc, cc],
                               [xx, bx, dfx, cx], [xx, bx, dbx, cx], s0, ctx_out)
    d_h = d_skip.reshape(SSD_GROUPS, SSD_HPG)[..., None]

    def finish(y, xs, z):
        bsz, t = y.shape[:2]
        y = (y + d_h * xs).reshape(bsz, t, SSD_INNER)
        y = group_rms_norm(y * jax.nn.silu(z), norm_g, SSD_GROUPS)
        return y.astype(z.dtype) @ w_out

    out_x = finish(yx, xx, zx)
    out_c = finish(yc, xc, zc) if ctx_out else None
    return out_x, out_c

def second_inputs(seed: int = 0) -> dict:
    key = jax.random.key(seed)
    ks = iter(jax.random.split(key, 40))

    def nrm(shape, scale):
        return jax.random.normal(next(ks), shape, jnp.float32) * scale

    ne, no = (DEPTH + 1) // 2, DEPTH // 2
    dt0 = jnp.exp(jax.random.uniform(next(ks), (no, 2, SSD_HEADS), jnp.float32, math.log(1e-3), math.log(1e-1)))
    return {
        'x': nrm((BATCH, SEQ, D_MODEL), 1.0),
        'c': nrm((BATCH, D_MODEL), 1.0),
        'ctx': nrm((BATCH, CTX_LEN, D_MODEL), 1.0),
        'c_ctx': nrm((D_MODEL,), 1.0),
        'mod_w': nrm((DEPTH, D_MODEL, N_MOD * D_MODEL), D_MODEL ** -0.5),
        'mod_b': nrm((DEPTH, N_MOD * D_MODEL), 0.02),
        'norm_g': 1.0 + nrm((DEPTH, 2, D_MODEL), 0.02),
        'ffn_w_in': nrm((DEPTH, D_MODEL, 2 * D_FF), D_MODEL ** -0.5),
        'ffn_w_out': nrm((DEPTH, D_FF, D_MODEL), D_FF ** -0.5),
        'ab_w_in': nrm((ne, D_MODEL, AB_IN), D_MODEL ** -0.5),
        'ab_gate_w': nrm((ne, 2, GLA_LR, GLA_HK), GLA_LR ** -0.5),
        'ab_gate_b': nrm((ne, 2, GLA_HK), 0.1),
        'ab_gla_norm_g': 1.0 + nrm((ne, GLA_HV), 0.02),
        'ab_vnorm_g': 1.0 + nrm((ne, GMLP_WIDTH), 0.02),
        'ab_spatial_w': nrm((ne, GMLP_GROUPS, GMLP_CHUNK, GMLP_CHUNK), GMLP_CHUNK ** -0.5),
        'ab_spatial_b': 1.0 + nrm((ne, GMLP_GROUPS, GMLP_CHUNK), 0.02),
        'ab_w_out': nrm((ne, D_MIX, D_MODEL), D_MIX ** -0.5),
        'ssd_w_in': nrm((no, D_MODEL, SSD_IN), D_MODEL ** -0.5),
        'ssd_conv_w': nrm((no, SSD_CONV, SSD_CONV_DIM), SSD_CONV ** -0.5),
        'ssd_conv_b': nrm((no, SSD_CONV_DIM), 0.02),
        'ssd_dt_bias': dt0 + jnp.log(-jnp.expm1(-dt0)),
        'ssd_a_log': jnp.log(jax.random.uniform(next(ks), (no, 2, SSD_HEADS), jnp.float32, 1.0, 16.0)),
        'ssd_d': 1.0 + nrm((no, SSD_HEADS), 0.02),
        'ssd_norm_g': 1.0 + nrm((no, SSD_INNER), 0.02),
        'ssd_w_out': nrm((no, SSD_INNER, D_MODEL), SSD_INNER ** -0.5),
        'final_norm_g': 1.0 + nrm((D_MODEL,), 0.02),
    }

def second_block(x, c, ctx, c_ctx, mod_w, mod_b, norm_g, ffn_w_in, ffn_w_out,
              ab_w_in, ab_gate_w, ab_gate_b, ab_gla_norm_g, ab_vnorm_g, ab_spatial_w, ab_spatial_b, ab_w_out,
              ssd_w_in, ssd_conv_w, ssd_conv_b, ssd_dt_bias, ssd_a_log, ssd_d, ssd_norm_g, ssd_w_out,
              final_norm_g):
    sc = jax.nn.silu(c)
    sc_ctx = jax.nn.silu(c_ctx)
    for i in range(DEPTH):
        ctx_out = i < DEPTH - 1
        j = i // 2
        mx = jnp.split((sc @ mod_w[i] + mod_b[i])[:, None, :], N_MOD, axis=-1)
        mc = jnp.split(sc_ctx @ mod_w[i] + mod_b[i], N_MOD, axis=-1)
        hx = modulate_2(rms_norm_2(x, norm_g[i, 0]), mx[0], mx[1])
        hc = modulate_2(rms_norm_2(ctx, norm_g[i, 0]), mc[0], mc[1])
        if i % 2 == 0:
            yx, yc = mixer_gla_gmlp(hx, hc, ab_w_in[j], ab_gate_w[j], ab_gate_b[j], ab_gla_norm_g[j],
                                    ab_vnorm_g[j], ab_spatial_w[j], ab_spatial_b[j], ab_w_out[j], ctx_out)
        else:
            yx_cm, yc = mixer_ssd(to_col_major(hx), hc, ssd_w_in[j], ssd_conv_w[j], ssd_conv_b[j],
                                  ssd_dt_bias[j], ssd_a_log[j], ssd_d[j], ssd_norm_g[j], ssd_w_out[j], ctx_out)
            yx = to_row_major(yx_cm)
        x = x + mx[2] * yx
        x = x + mx[5] * swiglu_2(modulate_2(rms_norm_2(x, norm_g[i, 1]), mx[3], mx[4]), ffn_w_in[i], ffn_w_out[i])
        if ctx_out:
            ctx = ctx + mc[2] * yc
            ctx = ctx + mc[5] * swiglu_2(modulate_2(rms_norm_2(ctx, norm_g[i, 1]), mc[3], mc[4]), ffn_w_in[i], ffn_w_out[i])
    return rms_norm_2(x, final_norm_g)


_first_inputs_2 = second_inputs


def second_inputs(seed=0):
    import zlib

    import numpy as np

    out = dict(_first_inputs_2(seed))
    spreads = {}
    factors = {'ab_gate_b': 2.797,
     'ab_gla_norm_g': 7.166,
     'ab_vnorm_g': 7.544,
     'ab_spatial_b': 7.102,
     'ssd_conv_b': 6.366,
     'ssd_d': 8.0,
     'ssd_norm_g': 6.925,
     'final_norm_g': 2.785}
    for name, (base, spread) in spreads.items():
        noise = np.random.default_rng([zlib.crc32(name.encode()), seed]).standard_normal(out[name].shape)
        drawn = base * np.exp(spread * noise) if base else spread * noise
        out[name] = __import__('jax').numpy.asarray(drawn.astype(out[name].dtype))
    for name, factor in factors.items():
        out[name] = (out[name] * factor).astype(out[name].dtype)
    return out


_narrow_inputs_2 = second_inputs


def second_inputs(seed=0):
    out = dict(_narrow_inputs_2(seed))
    wider = {'ab_gla_norm_g': 5.07,
     'ab_vnorm_g': 5.09,
     'ab_spatial_b': 5.17,
     'ssd_d': 10.05,
     'ssd_norm_g': 5.33,
     'final_norm_g': 3.08}
    for name, times in wider.items():
        mean = out[name].mean()
        out[name] = (mean + times * (out[name] - mean)).astype(out[name].dtype)
    return out


def setup_inputs(seed=0):
    out = dict(first_inputs(seed))
    for name, value in second_inputs(seed + 1).items():
        if name != "x":
            out[name + "_2"] = value
    return out


def reference(
    x, c, ctx, c_ctx, w_mod, b_mod, norm_mix, norm_ffn, w_in_even, w_out_even, q_norm_a,
    k_norm_a, sink_b, w_in_odd, w_out_odd, rpb_c, shift_mu, decay_w0, decay_w2, iclr_a0,
    iclr_a2, gate_g2, k_k, k_a, r_k, ln_x_w, ln_x_b, w_ffn_in, w_ffn_out, norm_out, c_2, ctx_2,
    c_ctx_2, mod_w_2, mod_b_2, norm_g_2, ffn_w_in_2, ffn_w_out_2, ab_w_in_2, ab_gate_w_2,
    ab_gate_b_2, ab_gla_norm_g_2, ab_vnorm_g_2, ab_spatial_w_2, ab_spatial_b_2, ab_w_out_2,
    ssd_w_in_2, ssd_conv_w_2, ssd_conv_b_2, ssd_dt_bias_2, ssd_a_log_2, ssd_d_2, ssd_norm_g_2,
    ssd_w_out_2, final_norm_g_2,
):
    x = first_block(
        x, c, ctx, c_ctx, w_mod, b_mod, norm_mix, norm_ffn, w_in_even, w_out_even, q_norm_a,
        k_norm_a, sink_b, w_in_odd, w_out_odd, rpb_c, shift_mu, decay_w0, decay_w2, iclr_a0,
        iclr_a2, gate_g2, k_k, k_a, r_k, ln_x_w, ln_x_b, w_ffn_in, w_ffn_out, norm_out,
    )
    return second_block(
        x, c_2, ctx_2, c_ctx_2, mod_w_2, mod_b_2, norm_g_2, ffn_w_in_2, ffn_w_out_2, ab_w_in_2,
        ab_gate_w_2, ab_gate_b_2, ab_gla_norm_g_2, ab_vnorm_g_2, ab_spatial_w_2, ab_spatial_b_2,
        ab_w_out_2, ssd_w_in_2, ssd_conv_w_2, ssd_conv_b_2, ssd_dt_bias_2, ssd_a_log_2, ssd_d_2,
        ssd_norm_g_2, ssd_w_out_2, final_norm_g_2,
    )


_drawn_inputs = setup_inputs


def setup_inputs(seed=0):
    import zlib

    import numpy as np

    out = dict(_drawn_inputs(seed))
    spreads = {}
    factors = {'rpb_c': 3.354, 'ln_x_b': 2.758, 'norm_g_2': 3.632, 'ssd_conv_b_2': 7.589, 'ssd_d_2': 8.0}
    for name, (base, spread) in spreads.items():
        noise = np.random.default_rng([zlib.crc32(name.encode()), seed]).standard_normal(out[name].shape)
        drawn = base * np.exp(spread * noise) if base else spread * noise
        out[name] = jnp.asarray(drawn.astype(out[name].dtype))
    for name, factor in factors.items():
        out[name] = (out[name] * factor).astype(out[name].dtype)
    return out
```

```python
from contextlib import ExitStack, contextmanager

import numpy as np

import concourse.bass as bass
from concourse import mybir

F32 = mybir.dt.float32
ALU = mybir.AluOpType
ACT = mybir.ActivationFunctionType
AX = mybir.AxisListType.X

P = 128
D = 1024
KD = D // P
CTX = 256
LAT = 512
TOK = CTX + LAT
FF = 2816
FT = FF // P
HD = 64
EPS = 1e-6
NEG = -1e30
SPANS = ((CTX, LAT), (0, CTX))
SILU_STREAM, CTX_STREAM = 0, 1


@contextmanager
def stage(nc, *names):
    sems = [nc.alloc_semaphore(f"{n}_{nc.next_id()}") for n in names]
    with nc.Block() as block:
        yield (block, *sems)
    nc.clear_and_free_semaphores(sems)
    nc.all_engine_barrier()


def memory(nc, ctx):
    def sb(name, shape):
        return ctx.enter_context(nc.sbuf_tensor(f"{name}_{nc.next_id()}", shape, F32))

    def ps(name, shape):
        return ctx.enter_context(nc.psum_tensor(f"{name}_{nc.next_id()}", shape, F32))
    return sb, ps


def steps_of(eng, n, body):
    for i in range(min(n, 2)):
        body(i, i, True)
    if n // 2 > 1:
        with eng.Fori(1, n // 2) as t:
            for slot in range(2):
                body(2 * t + slot, slot, False)
    if n % 2 and n > 2:
        body(n - 1, 0, False)


def linear(nc, hT, w, col0, ncols, emit, spans=SPANS):
    KT = hT.shape[1]
    kind = emit[0]
    steps = ncols // 256
    halves = ncols // 2
    wr = w.rearrange("(k p) n -> p k n", p=P)
    lo = min(t0 for t0, _ in spans)
    with ExitStack() as ctx:
        sb, ps = memory(nc, ctx)
        wbuf = [sb(f"w{s}", [P, KT, 256]) for s in range(2)]
        out = [sb(f"out{s}", [P, TOK]) for s in range(2)]
        acc = [[ps(f"acc{s}{j}", [P, 512]) for j in range(2)] for s in range(4)]
        with stage(nc, "w_ready0", "w_ready1", "tile_ready", "tile_used", "silu_ready", "stored0", "stored1") as (
                block, w_ready0, w_ready1, tile_ready, tile_used, silu_ready, stored0, stored1):
            w_ready, stored = (w_ready0, w_ready1), (stored0, stored1)

            @block.sync
            def _(sp):
                def load(i, s, first):
                    if not first:
                        sp.wait_ge(tile_ready, 2 * i - 2)
                    if kind == "swiglu":
                        for j in range(2):
                            sp.dma_start(wbuf[s][:, :, j * P:(j + 1) * P],
                                         wr[:, :, bass.ds(i * P + (col0 + j * halves), P)]).then_inc(w_ready[s], 16)
                    else:
                        sp.dma_start(wbuf[s][:], wr[:, :, bass.ds(i * 256 + col0, 256)]).then_inc(w_ready[s], 16)
                steps_of(sp, steps, load)

            loads = 2 if kind == "swiglu" else 1

            @block.tensor
            def _(pe):
                def products(i, s, first):
                    pe.wait_ge(w_ready[s], 16 * loads if first else (i - s) * (8 * loads) + 16 * loads)
                    for j in range(2):
                        if not first:
                            pe.wait_ge(tile_used, 2 * i + (j - 3))
                        for b, (t0, tn) in enumerate(spans):
                            for k in range(KT):
                                mm = nc.tensor.matmul(acc[2 * s + j][b][:, 0:tn], wbuf[s][:, k, j * P:(j + 1) * P],
                                                      hT[:, k, t0:t0 + tn], start=(k == 0), stop=(k == KT - 1))
                        mm.then_inc(tile_ready, 1)
                steps_of(pe, steps, products)

            @block.vector
            def _(dve):
                def finish(i, s, first):
                    for j in range(2):
                        if kind == "swiglu" and j == 0:
                            continue
                        dve.wait_ge(tile_ready, 2 * i + (j + 1))
                        if kind == "swiglu":
                            dve.wait_ge(silu_ready, i + 1)
                        if kind == "store" and not (first and s == 0):
                            dve.wait_ge(stored[j], 16 * i)
                        for b, (t0, tn) in enumerate(spans):
                            a = acc[2 * s + j][b][:, 0:tn]
                            if kind == "store":
                                op = nc.vector.tensor_copy(out[j][:, t0:t0 + tn], a)
                            elif kind == "swiglu":
                                op = nc.vector.tensor_tensor(emit[1][:, bass.ds(i, 1), t0:t0 + tn],
                                                             a, out[s][:, t0:t0 + tn], ALU.mult)
                            else:
                                x = emit[1][:, bass.ds(2 * i + j, 1), t0:t0 + tn]
                                op = nc.vector.scalar_tensor_tensor(
                                    out=x, in0=a, scalar=emit[2][:, bass.ds(2 * i + j, 1), b], in1=x,
                                    op0=ALU.mult, op1=ALU.add)
                        op.then_inc(tile_used, 2 if kind == "swiglu" else 1)
                steps_of(dve, steps, finish)

            @block.scalar
            def _(act):
                def store(i, s, first):
                    for j in range(2):
                        act.wait_ge(tile_used, 2 * i + (j + 1))
                        act.dma_start(emit[1][bass.ds(i * 256 + (emit[2] + j * P), P), lo:TOK],
                                      out[j][:, lo:TOK]).then_inc(stored[j], 16)

                def silu(i, s, first):
                    act.wait_ge(tile_ready, 2 * i + 1)
                    if not first:
                        act.wait_ge(tile_used, 2 * i - 2)
                    for b, (t0, tn) in enumerate(spans):
                        op = nc.scalar.activation(out[s][:, t0:t0 + tn], acc[2 * s][b][:, 0:tn], ACT.Silu)
                    op.then_inc(silu_ready, 1)
                if kind == "store":
                    steps_of(act, steps, store)
                    for j in range(2):
                        act.wait_ge(stored[j], 16 * steps)
                if kind == "swiglu":
                    steps_of(act, steps, silu)


def swiglu(nc, xT, hT, w_in, w_out, gates, spans):
    with ExitStack() as ctx:
        sb, _ = memory(nc, ctx)
        hidden = sb("hidden", [P, FT, TOK])
        linear(nc, hT, w_in, 0, 2 * FF, ("swiglu", hidden), spans)
        linear(nc, hidden, w_out, 0, D, ("residual", xT, gates), spans)

def load_tokens(nc, xT, ident, parts):
    jobs = [(src, t, c0 + t) for src, c0 in parts for t in range(0, src.shape[0], P)]
    with ExitStack() as ctx:
        sb, ps = memory(nc, ctx)
        rows = [sb(f"rows{i}", [P, D]) for i in range(len(jobs))]
        turned = [ps(f"turned{i}", [P, 4, P]) for i in range(4)]
        with stage(nc, "rows_ready", "turned_ready", "turned_used") as (
                block, rows_ready, turned_ready, turned_used):
            @block.sync
            def _(sp):
                for i, (src, t, _) in enumerate(jobs):
                    sp.dma_start(rows[i][:], src[t:t + P, :]).then_inc(rows_ready, 16)

            @block.tensor
            def _(pe):
                pe.wait_ge(rows_ready, 16 * len(jobs))
                for i in range(len(jobs)):
                    for g in range(2):
                        n = 2 * i + g
                        if n >= 4:
                            pe.wait_ge(turned_used, n - 3)
                        for k in range(4):
                            tr = nc.tensor.transpose(turned[n % 4][:, k, :], rows[i][:, (4 * g + k) * P:(4 * g + k + 1) * P],
                                                     ident[:])
                        tr.then_inc(turned_ready, 1)

            @block.vector
            def _(dve):
                for i, (_, _, c) in enumerate(jobs):
                    for g in range(2):
                        n = 2 * i + g
                        dve.wait_ge(turned_ready, n + 1)
                        nc.vector.tensor_copy(xT[:, 4 * g:4 * g + 4, c:c + P], turned[n % 4][:]).then_inc(turned_used, 1)


def columns(nc, ident, jobs):
    jobs = [(dst, vec, w) for dst, vec, *rest in jobs for w in [rest[0] if rest else P]]
    with ExitStack() as ctx:
        sb, ps = memory(nc, ctx)
        rows = [sb(f"rows{i}", [64, P]) for i in range(len(jobs))]
        turned = [ps(f"turned{i}", [P, 64]) for i in range(2)]
        with stage(nc, "rows_ready", "turned_ready", "turned_used") as (
                block, rows_ready, turned_ready, turned_used):
            @block.sync
            def _(sp):
                for i, (dst, vec, w) in enumerate(jobs):
                    sp.dma_start(rows[i][0:dst.shape[1], 0:w], vec.rearrange("(n p) -> n p", p=w)).then_inc(rows_ready, 16)

            @block.tensor
            def _(pe):
                pe.wait_ge(rows_ready, 16 * len(jobs))
                for i, (dst, _, w) in enumerate(jobs):
                    n = dst.shape[1]
                    if i >= 2:
                        pe.wait_ge(turned_used, i - 1)
                    nc.tensor.transpose(turned[i % 2][0:w, 0:n], rows[i][0:n, 0:w], ident[0:n, 0:n]).then_inc(turned_ready, 1)

            @block.vector
            def _(dve):
                for i, (dst, _, w) in enumerate(jobs):
                    n = dst.shape[1]
                    dve.wait_ge(turned_ready, i + 1)
                    nc.vector.tensor_copy(dst[0:w, :], turned[i % 2][0:w, 0:n]).then_inc(turned_used, 1)


def modulation(nc, ident, cond, w, b_cols, modT):
    NC = 512
    steps = 6 * D // NC
    wr = w.rearrange("(k p) n -> p k n", p=P)
    with ExitStack() as ctx:
        sb, ps = memory(nc, ctx)
        wbuf = [sb(f"w{s}", [P, KD, NC]) for s in range(2)]
        row = [sb(f"row{s}", [P, NC]) for s in range(2)]
        acc = [ps(f"acc{s}", [2, NC]) for s in range(2)]
        turned = [ps(f"turned{s}", [P, 4, P]) for s in range(2)]
        with stage(nc, "w_ready0", "w_ready1", "zeroed", "row_ready", "row_copied", "turned_ready", "mod_ready") as (
                block, w_ready0, w_ready1, zeroed, row_ready, row_copied, turned_ready, mod_ready):
            w_ready = (w_ready0, w_ready1)

            @block.gpsimd
            def _(pool):
                for s in range(2):
                    nc.gpsimd.memset(row[s][:], 0.0).then_inc(zeroed, 1)

            @block.sync
            def _(sp):
                def load(i, s, first):
                    if not first:
                        sp.wait_ge(row_ready, i - 1)
                    sp.dma_start(wbuf[s][:], wr[:, :, bass.ds(i * NC, NC)]).then_inc(w_ready[s], 16)
                steps_of(sp, steps, load)

            @block.tensor
            def _(pe):
                def step(i, s, first):
                    pe.wait_ge(w_ready[s], 16 if first else (i - s) * 8 + 16)
                    if not first:
                        pe.wait_ge(row_copied, i - 1)
                    for k in range(KD):
                        mm = nc.tensor.matmul(acc[s][:], cond[:, k, :], wbuf[s][:, k, :], start=(k == 0), stop=(k == KD - 1))
                    mm.then_inc(row_ready, 1)
                    pe.wait_ge(row_copied, i + 1)
                    if not first:
                        pe.wait_ge(mod_ready, i - 1)
                    for j in range(4):
                        tr = nc.tensor.transpose(turned[s][:, j, :], row[s][:, j * P:(j + 1) * P], ident[:])
                    tr.then_inc(turned_ready, 1)
                steps_of(pe, steps, step)

            @block.scalar
            def _(act):
                def copy(i, s, first):
                    act.wait_ge(row_ready, i + 1)
                    if not first:
                        act.wait_ge(turned_ready, i - 1)
                    if first:
                        act.wait_ge(zeroed, 2)
                    nc.scalar.copy(row[s][0:2, :], acc[s][:]).then_inc(row_copied, 1)
                steps_of(act, steps, copy)

            @block.vector
            def _(dve):
                def add(i, s, first):
                    dve.wait_ge(turned_ready, i + 1)
                    for j in range(4):
                        op = nc.vector.tensor_scalar(modT[:, bass.ds(4 * i + j, 1), :], turned[s][:, j, 0:2],
                                                     b_cols[:, bass.ds(4 * i + j, 1)], None, ALU.add)
                    op.then_inc(mod_ready, 1)
                steps_of(dve, steps, add)


def rms_modulate(nc, xT, dst, ones, gain, modT=None, shift=0, scale=0, spans=SPANS, by_column=False):
    with ExitStack() as ctx:
        sb, ps = memory(nc, ctx)
        square = sb("square", [P, KD, TOK])
        rstd = sb("rstd", [P, TOK])
        std = sb("std", [P, TOK])
        eps = sb("eps", [P, 1])
        factor = sb("factor", [P, KD, 2])
        held = square if by_column else dst
        total = [ps(f"total{b}", [P, 512]) for b in range(2)]
        with stage(nc, "squared", "eps_set", "summed", "std_ready", "rstd_ready", "one_plus", "factor_ready",
                   "scaled") as (block, squared, eps_set, summed, std_ready, rstd_ready, one_plus,
                                 factor_ready, scaled):
            @block.gpsimd
            def _(pool):
                nc.gpsimd.memset(eps[:], EPS).then_inc(eps_set, 1)

            @block.scalar
            def _(act):
                for b, (t0, tn) in enumerate(spans):
                    for k in range(KD):
                        nc.scalar.activation(square[:, k, t0:t0 + tn], xT[:, k, t0:t0 + tn], ACT.Square
                                             ).then_inc(squared, 1)
                act.wait_ge(eps_set, 1)
                for b, (t0, tn) in enumerate(spans):
                    act.wait_ge(summed, b + 1)
                    nc.scalar.activation(std[:, t0:t0 + tn], total[b][:, 0:tn], ACT.Sqrt, bias=eps[:, 0:1],
                                         scale=1.0 / D).then_inc(std_ready, 1)
                if modT is not None:
                    n = 0
                    for b, (t0, tn) in enumerate(spans):
                        for k in range(KD):
                            n += 1
                            act.wait_ge(scaled, n)
                            into = dst[:, k, t0:t0 + tn]
                            if by_column and t0 == CTX:
                                into = into.rearrange("p (c r) -> p r c", c=64)
                                source = held[:, k, t0:t0 + tn].rearrange("p (r c) -> p r c", c=64)
                            else:
                                source = held[:, k, t0:t0 + tn]
                            nc.scalar.activation(into, source, ACT.Identity, bias=modT[:, KD * shift + k, b:b + 1])

            @block.tensor
            def _(pe):
                for b, (t0, tn) in enumerate(spans):
                    for k in range(KD):
                        pe.wait_ge(squared, b * KD + k + 1)
                        mm = nc.tensor.matmul(total[b][:, 0:tn], ones[:], square[:, k, t0:t0 + tn],
                                              start=(k == 0), stop=(k == KD - 1))
                    mm.then_inc(summed, 1)

            @block.vector
            def _(dve):
                if modT is not None:
                    nc.vector.tensor_scalar(factor[:], modT[:, KD * scale:KD * (scale + 1), :], 1.0, None, ALU.add
                                            ).then_inc(one_plus, 1)
                    dve.wait_ge(one_plus, 1)
                    for b in range(2):
                        f = nc.vector.tensor_tensor(factor[:, :, b], factor[:, :, b], gain[:], ALU.mult)
                else:
                    for b in range(2):
                        f = nc.vector.tensor_copy(factor[:, :, b], gain[:])
                f.then_inc(factor_ready, 1)
                dve.wait_ge(factor_ready, 1)
                for b, (t0, tn) in enumerate(spans):
                    dve.wait_ge(std_ready, b + 1)
                    nc.vector.reciprocal(rstd[:, t0:t0 + tn], std[:, t0:t0 + tn]).then_inc(rstd_ready, 1)
                    dve.wait_ge(rstd_ready, b + 1)
                    for k in range(KD):
                        nc.vector.scalar_tensor_tensor(
                            out=held[:, k, t0:t0 + tn], in0=xT[:, k, t0:t0 + tn], scalar=factor[:, k, b:b + 1],
                            in1=rstd[:, t0:t0 + tn], op0=ALU.mult, op1=ALU.mult).then_inc(scaled, 1)


def load_columns(nc, hT, dram, lo=0):
    with stage(nc, "loaded") as (block, loaded):
        @block.sync
        def _(sp):
            sp.dma_start(hT[:, :, lo:TOK], dram.rearrange("(k p) t -> p k t", p=P)[:, :, lo:TOK]).then_inc(loaded, 16)
            sp.wait_ge(loaded, 16)


def store_tokens(nc, xT, ident, out):
    with ExitStack() as ctx:
        sb, ps = memory(nc, ctx)
        rows = [sb(f"rows{i}", [P, D]) for i in range(LAT // P)]
        turned = [ps(f"turned{i}", [P, 4, P]) for i in range(4)]
        with stage(nc, "turned_ready", "turned_used", "stored") as (block, turned_ready, turned_used, stored):
            @block.tensor
            def _(pe):
                for n in range(2 * LAT // P):
                    if n >= 4:
                        pe.wait_ge(turned_used, n - 3)
                    c = CTX + n // 2 * P
                    for k in range(4):
                        tr = nc.tensor.transpose(turned[n % 4][:, k, :], xT[:, n % 2 * 4 + k, c:c + P], ident[:])
                    tr.then_inc(turned_ready, 1)

            @block.vector
            def _(dve):
                for n in range(2 * LAT // P):
                    dve.wait_ge(turned_ready, n + 1)
                    nc.vector.tensor_copy(rows[n // 2][:, n % 2 * 512:n % 2 * 512 + 512], turned[n % 4][:]
                                          ).then_inc(turned_used, 1)

            @block.sync
            def _(sp):
                for i in range(LAT // P):
                    sp.wait_ge(turned_used, 2 * i + 2)
                    sp.dma_start(out[i * P:(i + 1) * P, :], rows[i][:]).then_inc(stored, 16)
                sp.wait_ge(stored, 16 * LAT // P)

def rope(nc, src, dst, row0, tiles, consts, gains=None):
    block_ones, cos, sin = consts
    with ExitStack() as ctx:
        sb, ps = memory(nc, ctx)
        plain = [sb(f"plain{s}", [P, TOK]) for s in range(2)]
        swapped = [sb(f"swapped{s}", [P, TOK]) for s in range(2)]
        square = [sb(f"square{s}", [P, TOK]) for s in range(2)]
        std = [sb(f"std{s}", [P, TOK]) for s in range(2)]
        rstd = [sb(f"rstd{s}", [P, TOK]) for s in range(2)]
        turned = [sb(f"turned{s}", [P, TOK]) for s in range(2)]
        other = [sb(f"other{s}", [P, TOK]) for s in range(2)]
        eps = sb("eps", [P, 1])
        total = [ps(f"total{s}", [P, 1024]) for s in range(2)]
        with stage(nc, "loaded0", "loaded1", "eps_set", "squared", "summed", "std_ready", "rstd_ready", "parts",
                   "joined", "ready", "stored0", "stored1") as (
                block, loaded0, loaded1, eps_set, squared, summed, std_ready, rstd_ready, parts, joined, ready,
                stored0, stored1):
            loaded, stored = (loaded0, loaded1), (stored0, stored1)

            @block.sync
            def _(sp):
                def load(i, s, first):
                    if not first:
                        sp.wait_ge(ready, i - 1)
                    sp.dma_start(plain[s][:], src[bass.ds(i * P + row0, P), :]).then_inc(loaded[s], 16)
                    for h in range(4):
                        sp.dma_start(swapped[s][32 * h:32 * h + 32, :],
                                     src[bass.ds(i * P + (row0 + 32 * (h ^ 1)), 32), :]).then_inc(loaded[s], 16)
                steps_of(sp, tiles, load)

            @block.gpsimd
            def _(pool):
                nc.gpsimd.memset(eps[:], EPS).then_inc(eps_set, 1)

            @block.scalar
            def _(act):
                def norm(i, s, first):
                    act.wait_ge(loaded[s], 80 if first else (i - s) * 40 + 80)
                    if not first:
                        act.wait_ge(summed, i - 1)
                    nc.scalar.activation(square[s][:], plain[s][:], ACT.Square).then_inc(squared, 1)
                    act.wait_ge(summed, i + 1)
                    nc.scalar.activation(std[s][:], total[s][:, 0:TOK], ACT.Sqrt, bias=eps[:, 0:1], scale=1.0 / HD
                                         ).then_inc(std_ready, 1)
                if gains is not None:
                    act.wait_ge(eps_set, 1)
                    steps_of(act, tiles, norm)

            @block.tensor
            def _(pe):
                def norm(i, s, first):
                    pe.wait_ge(squared, i + 1)
                    if not first:
                        pe.wait_ge(std_ready, i - 1)
                    for t0, tn in ((0, 512), (512, 256)):
                        mm = nc.tensor.matmul(total[s][:, t0:t0 + tn], block_ones[:], square[s][:, t0:t0 + tn],
                                              start=True, stop=True)
                    mm.then_inc(summed, 1)
                if gains is not None:
                    steps_of(pe, tiles, norm)

            @block.vector
            def _(dve):
                def rotate(i, s, first):
                    dve.wait_ge(loaded[s], 80 if first else (i - s) * 40 + 80)
                    if not first:
                        dve.wait_ge(stored[s], (i - s) * 8)
                    for n, (t, table, into) in enumerate(((plain[s], cos, turned[s]), (swapped[s], sin, other[s]))):
                        if gains is not None:
                            op = nc.vector.scalar_tensor_tensor(out=into[:], in0=t[:], scalar=gains[:, bass.ds(i, 1), n],
                                                                in1=table[:], op0=ALU.mult, op1=ALU.mult)
                        else:
                            op = nc.vector.tensor_tensor(into[:], t[:], table[:], ALU.mult)
                        op.then_inc(parts, 1)
                    dve.wait_ge(parts, 2 * i + 2)
                    op = nc.vector.tensor_tensor(turned[s][:], turned[s][:], other[s][:], ALU.add)
                    if gains is not None:
                        op.then_inc(joined, 1)
                        dve.wait_ge(std_ready, i + 1)
                        nc.vector.reciprocal(rstd[s][:], std[s][:]).then_inc(rstd_ready, 1)
                        dve.wait_ge(joined, i + 1)
                        dve.wait_ge(rstd_ready, i + 1)
                        op = nc.vector.tensor_tensor(turned[s][:], turned[s][:], rstd[s][:], ALU.mult)
                    op.then_inc(ready, 1)
                steps_of(dve, tiles, rotate)

            @block.gpsimd
            def _(pool):
                def store(i, s, first):
                    pool.wait_ge(ready, i + 1)
                    pool.dma_start(dst[bass.ds(i * P + row0, P), :], turned[s][:]).then_inc(stored[s], 16)
                steps_of(pool, tiles, store)
                for s in range(2):
                    pool.wait_ge(stored[s], 16 * ((tiles + 1 - s) // 2))


def attention(nc, ident, heads, qk, q_row, k_row, per_kv, v, v_row, mix, mix_row, queries, scale,
              mask=None, sinks=None, rpb=None, q_from=0):
    QT = len(queries)
    every = sum(n // P for _, n, _ in queries)
    q_min = min(c for c, _, _ in queries)
    with ExitStack() as ctx:
        sb, ps = memory(nc, ctx)
        qT = [sb(f"qT{s}", [HD, TOK]) for s in range(2)]
        kT = [sb(f"kT{s}", [HD, TOK]) for s in range(2)]
        vT = [sb(f"vT{s}", [HD, TOK]) for s in range(2)]
        vrow = sb("vrow", [P, 6, HD])
        scores = [sb(f"scores{s}", [P, TOK]) for s in range(2)]
        probs = [sb(f"probs{s}", [P, TOK]) for s in range(2)]
        probsT = [sb(f"probsT{s}", [P, 6, P]) for s in range(2)]
        outT = [sb(f"outT{s}", [HD, TOK]) for s in range(2)]
        stats = [[sb(f"{n}{s}", [P, 1]) for s in range(2)] for n in ("top", "ntop", "esink", "sum", "den", "rden")]
        top, ntop, esink, total, den, rden = stats
        hankel = [sb(f"hankel{s}", [P, 14, HD]) for s in range(2)] if rpb else None
        raw = [ps(f"raw{s}", [P, 1024]) for s in range(2)]
        probsT_ps = ps("probsT_ps", [P, 1024])
        v_ps = ps("v_ps", [P, 6, HD])
        out_ps = ps("out_ps", [HD, P])
        with stage(nc, "loaded0", "loaded1", "v_turned", "v_ready", "raw_ready", "masked", "top_ready", "ntop_ready",
                   "sum_ready", "den_ready", "rden_ready", "probs_ready", "probsT_ready",
                   "probsT_copied", "out_ready", "out_copied", "stored0", "stored1") as (
                block, loaded0, loaded1, v_turned, v_ready, raw_ready, masked, top_ready, ntop_ready,
                sum_ready, den_ready, rden_ready, probs_ready, probsT_ready, probsT_copied, out_ready,
                out_copied, stored0, stored1):
            loaded, stored = (loaded0, loaded1), (stored0, stored1)
            loads = 5 if rpb else 3
            full = 16 * loads

            @block.sync
            def _(sp):
                def load(h, s, first):
                    if not first:
                        sp.wait_ge(out_ready, (h - 1) * QT)
                    kv = h if per_kv == 1 else h // per_kv
                    sp.dma_start(qT[s][:, q_from:TOK], qk[bass.ds(h * HD + q_row, HD), q_from:TOK]).then_inc(loaded[s], 16)
                    sp.dma_start(kT[s][:], qk[bass.ds(kv * HD + k_row, HD), :]).then_inc(loaded[s], 16)
                    sp.dma_start(vT[s][:], v[bass.ds(kv * HD + v_row, HD), :]).then_inc(loaded[s], 16)
                    if rpb:
                        for r in range(2):
                            sp.dma_start(hankel[s][64 * r:64 * r + 64, :, :],
                                         bass.AP(rpb[0].tensor, h * (15 * 127) + (1 - r) * 127,
                                                 [[1, 64], [127, 14], [1, 64]])).then_inc(loaded[s], 16)
                steps_of(sp, heads, load)

            def arrived(eng, h, s, first):
                eng.wait_ge(loaded[s], full if first else (h - s) * (full // 2) + full)

            @block.tensor
            def _(pe):
                def head(h, s, first):
                    arrived(pe, h, s, first)

                    def score(q):
                        c, nk, m = queries[q]
                        n = h * QT + q
                        b = raw[q % 2]
                        if not (first and s == 0 and q < 2):
                            pe.wait_ge(sum_ready, n - 1)
                        for t0, tn in ((0, min(nk, 512)), (512, nk - 512)):
                            if tn > 0:
                                last = t0 + tn >= nk
                                mm = nc.tensor.matmul(b[:, t0:t0 + tn], qT[s][:, c:c + P], kT[s][:, t0:t0 + tn],
                                                      start=True, stop=not rpb)
                        if rpb:
                            w = hankel[s][:, 6 - 2 * q:14 - 2 * q, :].rearrange("p a b -> p (a b)")
                            nc.tensor.matmul(b[:, 256:512], rpb[1][:], w[:, 0:256], start=False, stop=True)
                            mm = nc.tensor.matmul(b[:, 512:768], rpb[1][:], w[:, 256:512], start=False, stop=True)
                        mm.then_inc(raw_ready, 1)

                    def turn(q):
                        _, nk, _ = queries[q]
                        n = h * QT + q
                        pe.wait_ge(probs_ready, n + 1)
                        if not (first and s == 0 and q < 1):
                            pe.wait_ge(probsT_copied, n)
                        for k in range(nk // P):
                            tr = nc.tensor.transpose(probsT_ps[:, k * P:(k + 1) * P], probs[q % 2][:, k * P:(k + 1) * P],
                                                     ident[:])
                        tr.then_inc(probsT_ready, 1)

                    def values(q):
                        _, nk, _ = queries[q]
                        n = h * QT + q
                        if q == 0:
                            pe.wait_ge(v_ready, h + 1)
                        pe.wait_ge(probsT_copied, n + 1)
                        if not (first and s == 0 and q < 1):
                            pe.wait_ge(out_copied, n)
                        for k in range(nk // P):
                            mm = nc.tensor.matmul(out_ps[:], vrow[:, k, :], probsT[q % 2][:, k, :],
                                                  start=(k == 0), stop=(k == nk // P - 1))
                        mm.then_inc(out_ready, 1)
                    if not (first and s == 0):
                        pe.wait_ge(v_ready, h)
                    score(0)
                    for k in range(6):
                        tr = nc.tensor.transpose(v_ps[:, k, :], vT[s][:, k * P:(k + 1) * P], ident[0:HD, 0:HD])
                    tr.then_inc(v_turned, 1)
                    for q in range(QT):
                        if q + 1 < QT:
                            score(q + 1)
                        if q:
                            values(q - 1)
                        turn(q)
                    values(QT - 1)
                steps_of(pe, heads, head)

            @block.vector
            def _(dve):
                def head(h, s, first):
                    def softmax_top(q):
                        c, nk, m = queries[q]
                        n = h * QT + q
                        p = q % 2
                        new = first and s == 0 and q < 2
                        dve.wait_ge(raw_ready, n + 1)
                        if not new:
                            dve.wait_ge(sum_ready, n - 1)
                        if m is not None:
                            nc.vector.tensor_tensor(scores[p][:, 0:nk], raw[p][:, 0:nk], mask[:, m, 0:nk], ALU.add
                                                    ).then_inc(masked, 1)
                            dve.wait_ge(masked, h * n_masked + sum(x[2] is not None for x in queries[:q + 1]))
                            src = scores[p]
                        else:
                            src = raw[p]
                        nc.vector.tensor_reduce(top[p][:], src[:, 0:nk], AX, ALU.max).then_inc(top_ready, 1)
                        dve.wait_ge(top_ready, n + 1)
                        if sinks is not None:
                            nc.vector.tensor_scalar(ntop[p][:], top[p][:], -scale, sinks[:, bass.ds(h, 1)], ALU.mult, ALU.min
                                                    ).then_inc(ntop_ready, 1)
                        else:
                            nc.vector.tensor_scalar(ntop[p][:], top[p][:], -scale, None, ALU.mult).then_inc(ntop_ready, 1)

                    def normalise(q):
                        _, nk, _ = queries[q]
                        n = h * QT + q
                        p = q % 2
                        dve.wait_ge(sum_ready, n + 1)
                        if sinks is not None:
                            nc.vector.tensor_tensor(den[p][:], total[p][:], esink[p][:], ALU.add).then_inc(den_ready, 1)
                            dve.wait_ge(den_ready, n + 1)
                            nc.vector.reciprocal(rden[p][:], den[p][:]).then_inc(rden_ready, 1)
                        else:
                            nc.vector.reciprocal(rden[p][:], total[p][:]).then_inc(rden_ready, 1)
                        dve.wait_ge(rden_ready, n + 1)
                        nc.vector.tensor_scalar(probs[p][:, 0:nk], probs[p][:, 0:nk], rden[p][:, 0:1], None, ALU.mult
                                                ).then_inc(probs_ready, 1)

                    def output(q):
                        c, _, _ = queries[q]
                        n = h * QT + q
                        dve.wait_ge(out_ready, n + 1)
                        if q == 0 and not first:
                            dve.wait_ge(stored[s], (h - s) * 8)
                        nc.vector.tensor_copy(outT[s][:, c:c + P], out_ps[:]).then_inc(out_copied, 1)
                    softmax_top(0)
                    dve.wait_ge(v_turned, h + 1)
                    if not (first and s == 0):
                        dve.wait_ge(out_ready, h * QT)
                    nc.vector.tensor_copy(vrow[:], v_ps[:]).then_inc(v_ready, 1)
                    for q in range(QT):
                        if q + 1 < QT:
                            softmax_top(q + 1)
                        if q:
                            output(q - 1)
                        normalise(q)
                    output(QT - 1)
                n_masked = sum(m is not None for _, _, m in queries)
                steps_of(dve, heads, head)

            @block.scalar
            def _(act):
                def head(h, s, first):
                    def exponent(q):
                        _, nk, m = queries[q]
                        n = h * QT + q
                        p = q % 2
                        act.wait_ge(ntop_ready, n + 1)
                        if not (first and s == 0 and q < 2):
                            act.wait_ge(probsT_ready, n - 1)
                        src = raw[p] if m is None else scores[p]
                        op = nc.scalar.activation(probs[p][:, 0:nk], src[:, 0:nk], ACT.Exp, bias=ntop[p][:, 0:1],
                                                  scale=scale, accum_out=total[p][:, 0:1])
                        if sinks is not None:
                            op = nc.scalar.activation(esink[p][:], sinks[:, bass.ds(h, 1)], ACT.Exp,
                                                      bias=ntop[p][:, 0:1], scale=-1.0)
                        op.then_inc(sum_ready, 1)

                    def copy(q):
                        _, nk, _ = queries[q]
                        n = h * QT + q
                        act.wait_ge(probsT_ready, n + 1)
                        if not (first and s == 0 and q < 2):
                            act.wait_ge(out_ready, n - 1)
                        nc.scalar.copy(probsT[q % 2][:, 0:nk // P, :], probsT_ps[:, 0:nk]).then_inc(probsT_copied, 1)
                    exponent(0)
                    for q in range(QT):
                        if q + 1 < QT:
                            exponent(q + 1)
                        copy(q)
                steps_of(act, heads, head)

            @block.gpsimd
            def _(pool):
                def store(h, s, first):
                    pool.wait_ge(out_copied, (h + 1) * QT)
                    pool.dma_start(mix[bass.ds(h * HD + mix_row, HD), q_min:TOK], outT[s][:, q_min:TOK]
                                   ).then_inc(stored[s], 16)
                steps_of(pool, heads, store)
                for s in range(2):
                    pool.wait_ge(stored[s], 16 * ((heads + 1 - s) // 2))


QUERIES_LAT = [(CTX + P * i, TOK, None) for i in range(LAT // P)]
QUERIES_CTX = [(P * i, CTX, None) for i in range(CTX // P)]
QUERIES_MASKED = [(CTX + P * i, TOK, i) for i in range(LAT // P)]


def even_mixer(nc, ident, proj, rot, mix, consts, gains, window, sinks):
    rope(nc, proj, rot, 0, 5, consts, gains)
    rope(nc, proj, rot, 768, 5, consts)
    attention(nc, ident, 8, rot, 0, 512, 4, proj, 640, mix, 0, QUERIES_CTX + QUERIES_LAT, HD ** -0.5)
    attention(nc, ident, 8, rot, 768, 1280, 4, proj, 1408, mix, 512, QUERIES_CTX + QUERIES_MASKED, HD ** -0.5,
              mask=window, sinks=sinks)

class Chain:

    def __init__(self, eng, sem, per):
        self.eng, self.sem, self.per, self.k, self.i = eng, sem, per, 0, 0

    def start(self, i):
        assert self.k in (0, self.per), (self.k, self.per)
        self.i, self.k = i, 0

    def __call__(self, ins):
        self.k += 1
        ins.then_inc(self.sem, 1)
        self.eng.wait_ge(self.sem, self.i * self.per + self.k)


RW = 512
CH = 64
NCH = TOK // CH


def shift_mix(nc, proj, row0, tiles, mu, mixed):
    W = TOK + 4
    with ExitStack() as ctx:
        sb, _ = memory(nc, ctx)
        z = [sb(f"z{s}", [P, W]) for s in range(2)]
        around = [sb(f"around{s}", [P, W - 2]) for s in range(2)]
        out = [sb(f"out{s}", [P, W - 2]) for s in range(2)]
        with stage(nc, "zeroed", "loaded0", "loaded1", "added", "centred", "ready", "stored0", "stored1") as (
                block, zeroed, loaded0, loaded1, added, centred, ready, stored0, stored1):
            loaded, stored = (loaded0, loaded1), (stored0, stored1)

            @block.sync
            def _(sp):
                sp.wait_ge(zeroed, 2)
                def load(i, s, first):
                    if not first:
                        sp.wait_ge(ready, i - 1)
                    rows = proj[bass.ds(i * P + row0, P), :]
                    sp.dma_start(z[s][:, 1:1 + CTX], rows[:, 0:CTX]).then_inc(loaded[s], 16)
                    sp.dma_start(z[s][:, CTX + 3:CTX + 3 + LAT], rows[:, CTX:TOK]).then_inc(loaded[s], 16)
                steps_of(sp, tiles, load)

            @block.gpsimd
            def _(pool):
                for s in range(2):
                    nc.gpsimd.memset(z[s][:], 0.0).then_inc(zeroed, 1)

                def store(i, s, first):
                    pool.wait_ge(ready, i + 1)
                    rows = mixed[bass.ds(i * P, P), :]
                    pool.dma_start(rows[:, 0:CTX], out[s][:, 0:CTX]).then_inc(stored[s], 16)
                    pool.dma_start(rows[:, CTX:TOK], out[s][:, CTX + 2:CTX + 2 + LAT]).then_inc(stored[s], 16)
                steps_of(pool, tiles, store)
                for s in range(2):
                    pool.wait_ge(stored[s], 32 * ((tiles + 1 - s) // 2))

            @block.vector
            def _(dve):
                def step(i, s, first):
                    dve.wait_ge(loaded[s], 32 if first else (i - s) * 16 + 32)
                    nc.vector.tensor_tensor(around[s][:], z[s][:, 0:W - 2], z[s][:, 2:W], ALU.add).then_inc(added, 1)
                    dve.wait_ge(added, i + 1)
                    nc.vector.scalar_tensor_tensor(out=around[s][:], in0=around[s][:], scalar=0.5, in1=z[s][:, 1:W - 1],
                                                   op0=ALU.mult, op1=ALU.subtract).then_inc(centred, 1)
                    dve.wait_ge(centred, i + 1)
                    if not first:
                        dve.wait_ge(stored[s], (i - s) * 16)
                    nc.vector.scalar_tensor_tensor(out=out[s][:], in0=around[s][:], scalar=mu[:, bass.ds(i, 1)],
                                                   in1=z[s][:, 1:W - 1], op0=ALU.mult, op1=ALU.add).then_inc(ready, 1)
                steps_of(dve, tiles, step)


def rwkv_features(nc, mixed, w2, a2, g2, cols, block_ones, reset, arrays, dec, bonus, gate):
    (kk_c, ka_c, rk_c, w0_c, a0_c) = cols
    with ExitStack() as ctx:
        sb, ps = memory(nc, ctx)
        tw, ad, sg = sb("tanh_w", [HD, TOK]), sb("ad", [HD, TOK]), sb("sig_g", [P, TOK])
        r, k, v = sb("r", [P, TOK]), sb("k", [P, TOK]), sb("v", [P, TOK])
        ws, asl, gs = sb("w2", [HD, 2, P]), sb("a2", [HD, 2, P]), sb("g2", [P, P])
        kk, sq, nrm, rr = sb("kk", [P, TOK]), sb("sq", [P, TOK]), sb("nrm", [P, TOK]), sb("rr", [P, TOK])
        ksum, bon, gat = sb("ksum", [P, TOK]), sb("bon", [P, TOK]), sb("gat", [P, TOK])
        lw = [sb(f"lw{d}", [P, TOK]) for d in range(2)]
        a = [sb(f"a{d}", [P, TOK]) for d in range(2)]
        c, e, kd = sb("c", [P, TOK]), sb("e", [P, TOK]), sb("kd", [P, TOK])
        up, down, excl = (sb(n, [P, TOK]) for n in ("exp_c", "exp_minus_c", "exp_e"))
        outs = [sb(f"o{n}", [P, TOK]) for n in range(4)]
        wc = sb("wc", [P, NCH])
        bias_now = sb("bias_now", [P, 4])
        X, Y, Z = (ps(n, [P, 1024]) for n in ("X", "Y", "Z"))
        parts = ((0, 512), (512, 256))
        with stage(nc, "lora_loaded", "lora_ready", "loaded", "zw_ready", "za_ready", "sig_ready", "kk_squared",
                   "kk_summed", "kk_root", "feature_step", "sums_ready", "exps_ready", "four_ready", "stored",
                   "tail_ready", "bonus_in", "bonus_summed", "gate_ready", "tail_stored") as (
                block, lora_loaded, lora_ready, loaded, zw_ready, za_ready, sig_ready, kk_squared, kk_summed,
                kk_root, feature_step, sums_ready, exps_ready, four_ready, stored, tail_ready, bonus_in,
                bonus_summed, gate_ready, tail_stored):
            TILES = RW // P

            def tiles(eng, body):
                body(0, True)
                with eng.Fori(1, TILES) as m:
                    body(m, False)

            def last_of_chunk(t, d):
                return t[:].rearrange("p (n c) -> p n c", c=CH)[:, :, (CH - 1) * (1 - d)]

            @block.sync
            def _(sp):
                sp.dma_start(tw[:], mixed[3 * RW:3 * RW + 64, :]).then_inc(lora_loaded, 16)
                sp.dma_start(ad[:], mixed[3 * RW + 64:3 * RW + 128, :]).then_inc(lora_loaded, 16)
                sp.dma_start(sg[:], mixed[3 * RW + 128:3 * RW + 256, :]).then_inc(lora_loaded, 16)

                def load(m, first):
                    if not first:
                        sp.wait_ge(tail_ready, m)
                        sp.wait_ge(gate_ready, m)
                    for n, t in enumerate((r, k, v)):
                        sp.dma_start(t[:], mixed[bass.ds(m * P + n * RW, P), :]).then_inc(loaded, 16)
                    sp.dma_start(ws[:], w2.rearrange("d l n -> l d n")[:, :, bass.ds(m * P, P)]).then_inc(loaded, 16)
                    sp.dma_start(asl[:], a2.rearrange("d l n -> l d n")[:, :, bass.ds(m * P, P)]).then_inc(loaded, 16)
                    sp.dma_start(gs[:], g2[:, bass.ds(m * P, P)]).then_inc(loaded, 16)
                tiles(sp, load)

            @block.scalar
            def _(act):
                act.wait_ge(lora_loaded, 48)
                nc.scalar.activation(tw[:], tw[:], ACT.Tanh).then_inc(lora_ready, 1)
                nc.scalar.activation(sg[:], sg[:], ACT.Sigmoid).then_inc(lora_ready, 1)

                def step(m, first):
                    act.wait_ge(sums_ready, 3 * m + 1)
                    nc.scalar.activation(sq[:], kk[:], ACT.Square).then_inc(kk_squared, 1)
                    act.wait_ge(kk_summed, m + 1)
                    nc.scalar.activation(nrm[:], Z[:, 0:TOK], ACT.Sqrt).then_inc(kk_root, 1)
                    for d in range(2):
                        act.wait_ge(zw_ready, 2 * m + d + 1)
                        nc.scalar.activation(lw[d][:], X[:, 0:TOK], ACT.Sigmoid, bias=bias_now[:, 2 * d:2 * d + 1])
                        act.wait_ge(za_ready, 2 * m + d + 1)
                        nc.scalar.activation(a[d][:], Y[:, 0:TOK], ACT.Sigmoid, bias=bias_now[:, 2 * d + 1:2 * d + 2]
                                             ).then_inc(sig_ready, 1)
                    for d in range(2):
                        act.wait_ge(sums_ready, 3 * m + (2 + d))
                        nc.scalar.activation(up[:], c[:], ACT.Exp)
                        nc.scalar.activation(down[:], c[:], ACT.Exp, scale=-1.0)
                        nc.scalar.activation(excl[:], e[:], ACT.Exp)
                        if not (first and d == 0):
                            act.wait_ge(stored, 80 * (2 * m + d))
                        nc.scalar.activation(wc[:], last_of_chunk(c, d), ACT.Exp).then_inc(exps_ready, 1)
                tiles(act, step)

            @block.tensor
            def _(pe):
                pe.wait_ge(lora_ready, 2)

                def step(m, first):
                    pe.wait_ge(loaded, m * 96 + 96)
                    for d in range(2):
                        if not (first and d == 0):
                            pe.wait_ge(sig_ready, 2 * m + d)
                        if d == 0 and not first:
                            pe.wait_ge(tail_ready, m)
                        for t0, tn in parts:
                            mm = nc.tensor.matmul(X[:, t0:t0 + tn], ws[:, d, :], tw[:, t0:t0 + tn], start=True, stop=True)
                        mm.then_inc(zw_ready, 1)
                        for t0, tn in parts:
                            mm = nc.tensor.matmul(Y[:, t0:t0 + tn], asl[:, d, :], ad[:, t0:t0 + tn], start=True, stop=True)
                        mm.then_inc(za_ready, 1)
                        if d == 0:
                            pe.wait_ge(kk_squared, m + 1)
                            for t0, tn in parts:
                                mm = nc.tensor.matmul(Z[:, t0:t0 + tn], block_ones[:], sq[:, t0:t0 + tn], start=True, stop=True)
                            mm.then_inc(kk_summed, 1)
                    pe.wait_ge(sig_ready, 2 * m + 2)
                    for t0, tn in parts:
                        mm = nc.tensor.matmul(Y[:, t0:t0 + tn], gs[:], sg[:, t0:t0 + tn], start=True, stop=True)
                    mm.then_inc(gate_ready, 1)
                    pe.wait_ge(bonus_in, m + 1)
                    for t0, tn in parts:
                        mm = nc.tensor.matmul(X[:, t0:t0 + tn], block_ones[:], rr[:, t0:t0 + tn], start=True, stop=True)
                    mm.then_inc(bonus_summed, 1)
                tiles(pe, step)

            @block.vector
            def _(dve):
                done = Chain(dve, feature_step, 23)

                def step(m, first):
                    done.start(m)
                    dve.wait_ge(loaded, m * 96 + 96)
                    if not first:
                        dve.wait_ge(tail_ready, m)
                    for d in range(2):
                        nc.vector.tensor_copy(bias_now[:, 2 * d:2 * d + 1], w0_c[:, bass.ds(m + TILES * d, 1)])
                        nc.vector.tensor_copy(bias_now[:, 2 * d + 1:2 * d + 2], a0_c[:, bass.ds(m + TILES * d, 1)])
                    nc.vector.tensor_scalar(kk[:], k[:], kk_c[:, bass.ds(m, 1)], None, ALU.mult).then_inc(sums_ready, 1)
                    dve.wait_ge(kk_root, m + 1)
                    done(nc.vector.tensor_scalar(nrm[:], nrm[:], 1e-12, None, ALU.max))
                    done(nc.vector.reciprocal(nrm[:], nrm[:]))
                    done(nc.vector.tensor_tensor(kk[:], kk[:], nrm[:], ALU.mult))
                    for d in range(2):
                        dve.wait_ge(sig_ready, 2 * m + d + 1)
                        done(nc.vector.tensor_scalar(lw[d][:], lw[d][:], -float(np.exp(-0.5)), None, ALU.mult))
                        if d == 1:
                            dve.wait_ge(exps_ready, 2 * m + 1)
                        elif not first:
                            dve.wait_ge(exps_ready, 2 * m)
                        done(nc.vector.tensor_tensor_scan(c[:], reset[:], lw[d][:], 0.0, ALU.mult, ALU.add))
                        if d == 0:
                            nc.vector.tensor_tensor(e[:], c[:], lw[d][:], ALU.subtract).then_inc(sums_ready, 1)
                        else:
                            cv, ev = (t[:].rearrange("p (n c) -> p n c", c=CH) for t in (c, e))
                            done(nc.vector.tensor_tensor(ev, cv[:, :, CH - 1:CH].to_broadcast([P, NCH, CH]), cv, ALU.subtract))
                            nc.vector.tensor_tensor(c[:], e[:], lw[d][:], ALU.add).then_inc(sums_ready, 1)
                        done(nc.vector.tensor_scalar(kd[:], a[d][:], -1.0, ka_c[:, bass.ds(m, 1)], ALU.add, ALU.mult))
                        done(nc.vector.scalar_tensor_tensor(out=kd[:], in0=kd[:], scalar=1.0, in1=k[:], op0=ALU.add, op1=ALU.mult))
                        if d == 0:
                            nc.vector.tensor_copy(ksum[:], kd[:])
                        else:
                            done(nc.vector.tensor_tensor(ksum[:], ksum[:], kd[:], ALU.add))
                        done(nc.vector.tensor_tensor(a[d][:], a[d][:], kk[:], ALU.mult))
                        dve.wait_ge(exps_ready, 2 * m + d + 1)
                        if not (first and d == 0):
                            dve.wait_ge(stored, 80 * (2 * m + d))
                        done(nc.vector.tensor_tensor(outs[0][:], kk[:], excl[:], ALU.mult))
                        done(nc.vector.tensor_tensor(outs[1][:], a[d][:], down[:], ALU.mult))
                        done(nc.vector.tensor_tensor(outs[2][:], kd[:], down[:], ALU.mult))
                        nc.vector.tensor_tensor(outs[3][:], r[:], up[:], ALU.mult).then_inc(four_ready, 1)
                        dve.wait_ge(four_ready, 2 * m + d + 1)
                    done(nc.vector.tensor_scalar(rr[:], r[:], rk_c[:, bass.ds(m, 1)], None, ALU.mult))
                    nc.vector.tensor_tensor(rr[:], rr[:], ksum[:], ALU.mult).then_inc(bonus_in, 1)
                    if not first:
                        dve.wait_ge(tail_stored, 32 * m)
                    dve.wait_ge(gate_ready, m + 1)
                    done(nc.vector.tensor_copy(gat[:], Y[:, 0:TOK]))
                    dve.wait_ge(bonus_summed, m + 1)
                    nc.vector.tensor_tensor(bon[:], X[:, 0:TOK], v[:], ALU.mult).then_inc(tail_ready, 1)
                tiles(dve, step)

            @block.gpsimd
            def _(pool):
                def store(m, first):
                    for d in range(2):
                        pool.wait_ge(four_ready, 2 * m + d + 1)
                        pool.wait_ge(exps_ready, 2 * m + d + 1)
                        for n in range(4):
                            pool.dma_start(arrays[d, n, bass.ds(m * P, P), :], outs[n][:]).then_inc(stored, 16)
                        pool.dma_start(dec[d, bass.ds(m * P, P), :], wc[:]).then_inc(stored, 16)
                    pool.wait_ge(tail_ready, m + 1)
                    pool.dma_start(bonus[bass.ds(m * P, P), :], bon[:, CTX:TOK]).then_inc(tail_stored, 16)
                    pool.dma_start(gate[bass.ds(m * P, P), :], gat[:, CTX:TOK]).then_inc(tail_stored, 16)
                tiles(pool, store)
                pool.wait_ge(stored, 160 * TILES)
                pool.wait_ge(tail_stored, 32 * TILES)


def rwkv_chunks(nc, ident, masks, arrays, mixed, chunks):
    H = 8
    LEV = 5
    with ExitStack() as ctx:
        sb, ps = memory(nc, ctx)
        ar = [[sb(f"ar{s}{d}", [HD, H, 2, CH]) for d in range(2)] for s in range(2)]
        be = [[sb(f"be{s}{d}", [HD, H, CH]) for d in range(2)] for s in range(2)]
        ka = [[sb(f"ka{s}{d}", [HD, H, CH]) for d in range(2)] for s in range(2)]
        vf = [sb(f"vf{s}", [HD, H, CH]) for s in range(2)]
        two = lambda n, shape: [sb(f"{n}{d}", shape) for d in range(2)]
        mp = two("mp", [CH, H, 2, CH])
        lt = two("lt", [CH, H, CH])
        bq = two("bq", [CH, H, 2, CH])
        kt = two("kt", [CH, H, HD])
        am = two("am", [CH, H, 2, CH])
        vt = two("vt", [CH, H, HD])
        lev = [[sb(f"lev{d}{n}", [CH, H, CH]) for n in range(LEV + 1)] for d in range(2)]
        z = two("z", [CH, H, CH])
        x = two("x", [CH, H, CH])
        lx = two("lx", [CH, H, CH])
        au = two("au", [CH, H, 2, CH])
        res = [sb(f"res{d}", [CH, 4, H, CH]) for d in range(2)]
        big = [ps(f"big{d}", [CH, H, 2, CH]) for d in range(2)]
        one = [ps(f"one{d}", [CH, H, CH]) for d in range(2)]
        six = [ps(f"six{d}", [CH, H, CH]) for d in range(2)]
        names = ["loaded0", "loaded1", "kar", "mp_ready", "bar", "lt_ready", "q_ready", "beta_t", "beta_c", "kappa_t",
                 "kappa_c", "alpha_t", "alpha_c", "v_t", "v_c", "levels", "z1a", "z1", "x1_t", "x1", "lx_p", "lx_c", "x_p", "x_c",
                 "z_p", "z_c", "mv_p", "mv_c", "au_p", "au_c", "gf_p", "g_c", "f_c", "h_p", "h_c", "y_p", "y_c",
                 "stored0", "stored1", "passed"]
        with stage(nc, *names) as (block, *sems):
            S = dict(zip(names, sems))
            loaded = (S["loaded0"], S["loaded1"])
            stored = (S["stored0"], S["stored1"])
            I64 = ident[0:HD, 0:HD]

            def wide(t):
                return t.rearrange("p (o c) -> p o c", o=1).to_broadcast([CH, H, CH])

            def wait(eng, name, i, d, n=0, per=1):
                eng.wait_ge(S[name], i * (2 * per) + (2 * n + d + 1))

            def wait_last(eng, name, i, d, per=1):
                eng.wait_ge(S[name], i * (2 * per) + (d - 1))

            def dv(name, d):
                return arrays[d, {"alpha": 0, "beta": 1, "kappa": 2, "rho": 3}[name]].rearrange("(h k) t -> k h t", k=HD)

            @block.sync
            def _(sp):
                def load(i, s, first):
                    if not first:
                        sp.wait_ge(S["y_c"], 2 * i - 2)
                        sp.wait_ge(S["f_c"], 2 * i - 2)
                    cols = bass.ds(i * CH, CH)
                    for d in range(2):
                        for dst, name in ((ar[s][d][:, :, 0, :], "alpha"), (ar[s][d][:, :, 1, :], "rho"),
                                          (be[s][d][:], "beta"), (ka[s][d][:], "kappa")):
                            sp.dma_start(dst, dv(name, d)[:, :, cols]).then_inc(loaded[s], 16)
                    sp.dma_start(vf[s][:], mixed[2 * RW:3 * RW, :].rearrange("(h k) t -> k h t", k=HD)[:, :, cols]
                                 ).then_inc(loaded[s], 16)
                steps_of(sp, NCH, load)

            def arrived(eng, i, s, first):
                eng.wait_ge(loaded[s], 144 if first else (i - s) * 72 + 144)

            @block.tensor
            def _(pe):
                def step(i, s, first):
                    fresh = first and s == 0
                    arrived(pe, i, s, first)

                    def apart():
                        pe.sem_inc(S["passed"], 1)

                    def each(out, lhs, rhs, name, start=True, stop=True):
                        apart()
                        for h in range(H):
                            mm = nc.tensor.matmul(out[:, h], lhs[:, h], rhs[:, h], start=start, stop=stop)
                        if name:
                            mm.then_inc(S[name], 1)

                    def turn(out, src, name):
                        apart()
                        for h in range(H):
                            tr = nc.tensor.transpose(out[:, h], src[:, h], I64)
                        tr.then_inc(S[name], 1)
                    both = lambda t: t.rearrange("p h a c -> p h (a c)") if hasattr(t, "rearrange") else t[:].rearrange("p h a c -> p h (a c)")
                    for d in range(2):
                        if not fresh:
                            wait_last(pe, "f_c", i, d)
                            wait_last(pe, "g_c", i, d)
                        each(both(big[d][:]), ka[s][d], both(ar[s][d][:]), "kar")
                    for d in range(2):
                        if not fresh:
                            wait_last(pe, "h_c", i, d)
                        turn(one[d], be[s][d], "beta_t")
                    for d in range(2):
                        if not fresh:
                            wait_last(pe, "y_c", i, d)
                        turn(six[d], ka[s][d], "kappa_t")
                    for d in range(2):
                        wait(pe, "mp_ready", i, d)
                        each(both(big[d][:]), be[s][d], both(ar[s][d][:]), "bar")
                    for d in range(2):
                        wait(pe, "beta_c", i, d)
                        turn(one[d], ar[s][d][:, :, 0, :], "alpha_t")
                    for d in range(2):
                        wait(pe, "kappa_c", i, d)
                        turn(six[d], vf[s], "v_t")
                    for d in range(2):
                        wait(pe, "alpha_c", i, d)
                        wait(pe, "z1", i, d)
                        turn(one[d], z[d], "x1_t")
                    for d in range(2):
                        wait(pe, "v_c", i, d)
                        each(six[d], mp[d][:, :, 0, :], vt[d], "mv_p")
                    for n in range(LEV):
                        for d in range(2):
                            if n == 0:
                                wait(pe, "x1", i, d)
                            else:
                                wait(pe, "x_c", i, d, n - 1, LEV)
                                wait(pe, "z_c", i, d, n - 1, LEV)
                            wait(pe, "levels", i, d, 0)
                            each(one[d], lev[d][n + 1], x[d], "lx_p")
                        for d in range(2):
                            if n == 0:
                                wait(pe, "mv_c", i, d)
                            wait(pe, "lx_c", i, d, n, LEV)
                            each(six[d], z[d], lx[d], "x_p")
                        for d in range(2):
                            wait(pe, "x_c", i, d, n, LEV)
                            turn(one[d], x[d], "z_p")
                    for d in range(2):
                        wait(pe, "lt_ready", i, d)
                        wait(pe, "q_ready", i, d)
                        wait(pe, "z_c", i, d, LEV - 1, LEV)
                        each(both(big[d][:]), z[d], both(am[d][:]), "au_p")
                    for d in range(2):
                        wait(pe, "au_c", i, d)
                        apart()
                        for h in range(H):
                            nc.tensor.matmul(one[d][:, h], kt[d][:, h], vt[d][:, h], start=True, stop=False)
                            mm = nc.tensor.matmul(one[d][:, h], bq[d][:, h, 0, :], au[d][:, h, 1, :], start=False, stop=True)
                        mm.then_inc(S["h_p"], 1)
                        each(both(big[d][:]), au[d][:, :, 0, :], both(bq[d][:]), "gf_p")
                        for h in range(H):
                            nc.tensor.matmul(six[d][:, h], vt[d][:, h], mp[d][:, h, 1, :], start=True, stop=False)
                            mm = nc.tensor.matmul(six[d][:, h], au[d][:, h, 1, :], bq[d][:, h, 1, :], start=False, stop=True)
                        mm.then_inc(S["y_p"], 1)
                steps_of(pe, NCH, step)

            @block.vector
            def _(dve):
                def step(i, s, first):
                    fresh = first and s == 0
                    V = nc.vector
                    for d in range(2):
                        wait(dve, "kar", i, d)
                        if not fresh:
                            wait_last(dve, "y_p", i, d)
                        m = masks[:, d, 0:2, :].rearrange("p (o a) c -> p o (a c)", o=1).to_broadcast([CH, H, 2 * CH])
                        V.tensor_tensor(mp[d][:].rearrange("p h a c -> p h (a c)"), big[d][:].rearrange("p h a c -> p h (a c)"),
                                        m, ALU.mult).then_inc(S["mp_ready"], 1)
                    for d in range(2):
                        wait(dve, "bar", i, d)
                        if not fresh:
                            wait_last(dve, "y_p", i, d)
                        V.tensor_tensor(bq[d][:, :, 1, :], big[d][:, :, 1, :], wide(masks[:, d, 2, :]), ALU.mult
                                        ).then_inc(S["q_ready"], 1)
                        if not fresh:
                            wait_last(dve, "levels", i, d)
                        V.tensor_copy(lt[d][:], big[d][:, :, 0, :]).then_inc(S["lt_ready"], 1)
                        wait(dve, "lt_ready", i, d)
                        if not fresh:
                            wait_last(dve, "au_p", i, d)
                        V.tensor_tensor(z[d][:], lt[d][:], wide(masks[:, d, 3, :]), ALU.mult).then_inc(S["z1a"], 1)
                        wait(dve, "z1a", i, d)
                        V.tensor_tensor(z[d][:], z[d][:], wide(I64), ALU.add).then_inc(S["z1"], 1)
                    for d in range(2):
                        wait(dve, "x1_t", i, d)
                        V.tensor_copy(x[d][:], one[d][:]).then_inc(S["x1"], 1)
                    for n in range(LEV):
                        for d in range(2):
                            wait(dve, "x_p", i, d, n, LEV)
                            wait(dve, "x1", i, d)
                            if n:
                                wait(dve, "x_c", i, d, n - 1, LEV)
                            V.tensor_tensor(x[d][:], x[d][:], six[d][:], ALU.add).then_inc(S["x_c"], 1)
                    for d in range(2):
                        wait(dve, "au_p", i, d)
                        if not fresh:
                            wait_last(dve, "y_p", i, d)
                        V.tensor_copy(au[d][:], big[d][:]).then_inc(S["au_c"], 1)
                    for d in range(2):
                        wait(dve, "h_p", i, d)
                        if not fresh:
                            dve.wait_ge(stored[d], i * 16)
                        V.tensor_copy(res[d][:, 2], one[d][:]).then_inc(S["h_c"], 1)
                        wait(dve, "gf_p", i, d)
                        V.tensor_tensor(res[d][:, 0], big[d][:, :, 0, :], wide(I64), ALU.add).then_inc(S["g_c"], 1)
                        V.tensor_tensor(res[d][:, 1], big[d][:, :, 1, :], ar[s][d][:, :, 1, :], ALU.add).then_inc(S["f_c"], 1)
                steps_of(dve, NCH, step)

            @block.scalar
            def _(act):
                def step(i, s, first):
                    fresh = first and s == 0
                    A = nc.scalar
                    for d in range(2):
                        wait(act, "beta_t", i, d)
                        if not fresh:
                            wait_last(act, "y_p", i, d)
                        A.mul(bq[d][:, :, 0, :], one[d][:], -1.0).then_inc(S["beta_c"], 1)
                    for d in range(2):
                        wait(act, "kappa_t", i, d)
                        A.copy(kt[d][:], six[d][:]).then_inc(S["kappa_c"], 1)
                    for d in range(2):
                        wait(act, "alpha_t", i, d)
                        A.copy(am[d][:, :, 0, :], one[d][:]).then_inc(S["alpha_c"], 1)
                    for d in range(2):
                        wait(act, "v_t", i, d)
                        A.copy(vt[d][:], six[d][:]).then_inc(S["v_c"], 1)
                    for d in range(2):
                        wait(act, "mv_p", i, d)
                        A.copy(am[d][:, :, 1, :], six[d][:]).then_inc(S["mv_c"], 1)
                    for n in range(LEV):
                        for d in range(2):
                            wait(act, "lx_p", i, d, n, LEV)
                            A.copy(lx[d][:], one[d][:]).then_inc(S["lx_c"], 1)
                        for d in range(2):
                            wait(act, "z_p", i, d, n, LEV)
                            A.copy(z[d][:], one[d][:]).then_inc(S["z_c"], 1)
                    for d in range(2):
                        wait(act, "y_p", i, d)
                        if not fresh:
                            act.wait_ge(stored[d], i * 16)
                        A.copy(res[d][:, 3], six[d][:]).then_inc(S["y_c"], 1)
                steps_of(act, NCH, step)

            @block.gpsimd
            def _(pool):
                def step(i, s, first):
                    fresh = first and s == 0
                    for d in range(2):
                        wait(pool, "lt_ready", i, d)
                        if not fresh:
                            wait_last(pool, "lx_p", i, d, LEV)
                        for n in range(1, LEV + 1):
                            op = nc.gpsimd.tensor_tensor(lev[d][n][:], lt[d][:], wide(masks[:, d, 3 + n, :]), ALU.mult)
                        op.then_inc(S["levels"], 1)
                    for d in range(2):
                        wait(pool, "y_c", i, d)
                        wait(pool, "f_c", i, d)
                        wait(pool, "h_c", i, d)
                        wait(pool, "g_c", i, d)
                        pool.dma_start(chunks[d, bass.ds(i, 1)].rearrange("o p a n -> (o p) a n"),
                                       res[d][:].rearrange("p a h c -> p a (h c)")).then_inc(stored[d], 16)
                steps_of(pool, NCH, step)
                for d in range(2):
                    pool.wait_ge(stored[d], 16 * NCH)


def rwkv_recurrence(nc, chunks, dec, ys):
    H = 8
    CC = CTX // CH
    with ExitStack() as ctx:
        sb, ps = memory(nc, ctx)
        res = [[sb(f"res{s}{d}", [CH, 4, H, CH]) for d in range(2)] for s in range(2)]
        state = [sb(f"state{d}", [HD, H, HD]) for d in range(2)]
        grown = [sb(f"grown{d}", [HD, H, HD]) for d in range(2)]
        y = [[sb(f"y{s}{d}", [HD, H, CH]) for d in range(2)] for s in range(2)]
        wc = [sb(f"wc{d}", [HD, H, NCH]) for d in range(2)]
        g_ps = [ps(f"g_ps{d}", [HD, H, HD]) for d in range(2)]
        y_ps = [ps(f"y_ps{d}", [HD, H, CH]) for d in range(2)]
        with stage(nc, "dec_loaded", "loaded0", "loaded1", "cleared", "grown_p", "y_p", "grown_c", "state_ready", "y_c",
                   "stored0", "stored1", "passed") as (
                block, dec_loaded, loaded0, loaded1, cleared, grown_p, y_p, grown_c, state_ready, y_c, stored0, stored1,
                passed):
            loaded, stored = (loaded0, loaded1), (stored0, stored1)

            def order(i, d, latent):
                return i if d == 0 else (NCH + CC - 1 if latent else CC - 1) - i

            def both_phases(eng, body):
                for i in range(CC + 2):
                    body(i, i % 2, i >= CC, i < 2)
                with eng.Fori(CC // 2 + 1, NCH // 2) as t:
                    for s in range(2):
                        body(2 * t + s, s, True, False)

            @block.sync
            def _(sp):
                for d in range(2):
                    sp.dma_start(wc[d][:], dec[d].rearrange("(h k) n -> k h n", k=HD)).then_inc(dec_loaded, 16)

                def load(i, s, latent, first):
                    if not first:
                        sp.wait_ge(y_c, 2 * i - 2)
                        sp.wait_ge(state_ready, 2 * i - 2)
                    for d in range(2):
                        sp.dma_start(res[s][d][:].rearrange("p a h c -> p a (h c)"),
                                     chunks[d, bass.ds(order(i, d, latent), 1)].rearrange("o p a n -> (o p) a n")
                                     ).then_inc(loaded[s], 16)
                both_phases(sp, load)

            @block.tensor
            def _(pe):
                def step(i, s, latent, first):
                    pe.wait_ge(loaded[s], (i - s) * 16 + 32)
                    for d in range(2):
                        if first and s == 0:
                            pe.wait_ge(cleared, 2)
                        else:
                            pe.wait_ge(state_ready, 2 * i + (d - 1))
                            pe.wait_ge(y_c, 2 * i + (d - 1))
                        pe.sem_inc(passed, 1)
                        for h in range(H):
                            mm = nc.tensor.matmul(g_ps[d][:, h], res[s][d][:, 0, h], state[d][:, h], start=True, stop=True)
                        mm.then_inc(grown_p, 1)
                        for h in range(H):
                            mm = nc.tensor.matmul(y_ps[d][:, h], state[d][:, h], res[s][d][:, 1, h], start=True, stop=True)
                        mm.then_inc(y_p, 1)
                both_phases(pe, step)

            @block.vector
            def _(dve):
                for d in range(2):
                    nc.vector.memset(state[d][:], 0.0).then_inc(cleared, 1)
                dve.wait_ge(dec_loaded, 32)

                def step(i, s, latent, first):
                    for d in range(2):
                        dve.wait_ge(grown_p, 2 * i + (d + 1))
                        nc.vector.tensor_tensor(grown[d][:], g_ps[d][:], res[s][d][:, 2], ALU.add).then_inc(grown_c, 1)
                        dve.wait_ge(grown_c, 2 * i + (d + 1))
                        dve.wait_ge(y_p, 2 * i + (d + 1))
                        dve.sem_inc(passed, 1)
                        w = wc[d][:, :, bass.ds(order(i, d, latent), 1)].to_broadcast([HD, H, HD])
                        nc.vector.tensor_tensor(state[d][:], grown[d][:], w, ALU.mult).then_inc(state_ready, 1)
                    for d in range(2):
                        if latent and not (type(i) is int and i < CC + 2):
                            dve.wait_ge(stored[s], (i - s) * 16 - 32 * (CC // 2))
                        nc.vector.tensor_tensor(y[s][d][:], y_ps[d][:], res[s][d][:, 3], ALU.add).then_inc(y_c, 1)
                both_phases(dve, step)

            @block.gpsimd
            def _(pool):
                with pool.Fori(CC // 2, NCH // 2) as t:
                    for s in range(2):
                        i = 2 * t + s
                        pool.wait_ge(y_c, 2 * i + 2)
                        for d in range(2):
                            pool.dma_start(ys[d].rearrange("(h v) t -> v h t", v=HD)[:, :, bass.ds((order(i, d, True) - CC) * CH, CH)],
                                           y[s][d][:]).then_inc(stored[s], 16)
                for s in range(2):
                    pool.wait_ge(stored[s], 32 * (NCH - CC) // 2)


def rwkv_readout(nc, ys, block_ones, ln_w, ln_b, bonus, gate, mix, row0):
    TILES = RW // P
    with ExitStack() as ctx:
        sb, ps = memory(nc, ctx)
        y = [[sb(f"y{s}{n}", [P, LAT]) for n in range(4)] for s in range(2)]
        total, centred, square, std, out = ([sb(f"{n}{s}", [P, LAT]) for s in range(2)]
                                            for n in ("total", "centred", "square", "std", "out"))
        eps = sb("eps", [P, 1])
        mean_ps = [ps(f"mean{s}", [P, LAT]) for s in range(2)]
        var_ps = [ps(f"var{s}", [P, LAT]) for s in range(2)]
        with stage(nc, "eps_set", "loaded0", "loaded1", "total_ready", "mean_ready", "square_ready", "centred_ready", "var_ready", "std_ready",
                   "read_step", "ready", "stored0", "stored1") as (
                block, eps_set, loaded0, loaded1, total_ready, mean_ready, square_ready, centred_ready, var_ready, std_ready,
                read_step, ready, stored0, stored1):
            loaded, stored = (loaded0, loaded1), (stored0, stored1)

            @block.sync
            def _(sp):
                def load(i, s, first):
                    if not first:
                        sp.wait_ge(ready, i - 1)
                    for n, src in enumerate((ys[0], ys[1], bonus, gate)):
                        sp.dma_start(y[s][n][:], src[bass.ds(i * P, P), :]).then_inc(loaded[s], 16)
                steps_of(sp, TILES, load)

            @block.tensor
            def _(pe):
                def step(i, s, first):
                    pe.wait_ge(total_ready, i + 1)
                    nc.tensor.matmul(mean_ps[s][:], block_ones[:], total[s][:], start=True, stop=True).then_inc(mean_ready, 1)
                    pe.wait_ge(square_ready, i + 1)
                    nc.tensor.matmul(var_ps[s][:], block_ones[:], square[s][:], start=True, stop=True).then_inc(var_ready, 1)
                steps_of(pe, TILES, step)

            @block.scalar
            def _(act):
                act.wait_ge(eps_set, 1)
                def step(i, s, first):
                    act.wait_ge(centred_ready, i + 1)
                    nc.scalar.activation(square[s][:], centred[s][:], ACT.Square).then_inc(square_ready, 1)
                    act.wait_ge(var_ready, i + 1)
                    nc.scalar.activation(std[s][:], var_ps[s][:], ACT.Sqrt, bias=eps[:, 0:1], scale=1.0 / HD).then_inc(std_ready, 1)
                steps_of(act, TILES, step)

            @block.vector
            def _(dve):
                done = Chain(dve, read_step, 4)
                nc.vector.memset(eps[:], 64e-5).then_inc(eps_set, 1)

                def step(i, s, first):
                    done.start(i)
                    dve.wait_ge(loaded[s], 64 if first else (i - s) * 32 + 64)
                    nc.vector.tensor_tensor(total[s][:], y[s][0][:], y[s][1][:], ALU.add).then_inc(total_ready, 1)
                    dve.wait_ge(total_ready, i + 1)
                    dve.wait_ge(mean_ready, i + 1)
                    nc.vector.scalar_tensor_tensor(out=centred[s][:], in0=mean_ps[s][:], scalar=-1.0 / HD, in1=total[s][:],
                                                   op0=ALU.mult, op1=ALU.add).then_inc(centred_ready, 1)
                    dve.wait_ge(std_ready, i + 1)
                    done(nc.vector.reciprocal(std[s][:], std[s][:]))
                    done(nc.vector.tensor_tensor(centred[s][:], centred[s][:], std[s][:], ALU.mult))
                    done(nc.vector.tensor_scalar(centred[s][:], centred[s][:], ln_w[:, bass.ds(i, 1)], ln_b[:, bass.ds(i, 1)],
                                                 ALU.mult, ALU.add))
                    done(nc.vector.tensor_tensor(centred[s][:], centred[s][:], y[s][2][:], ALU.add))
                    if not first:
                        dve.wait_ge(stored[s], (i - s) * 8)
                    nc.vector.tensor_tensor(out[s][:], centred[s][:], y[s][3][:], ALU.mult).then_inc(ready, 1)
                steps_of(dve, TILES, step)

            @block.gpsimd
            def _(pool):
                def store(i, s, first):
                    pool.wait_ge(ready, i + 1)
                    pool.dma_start(mix[bass.ds(i * P + row0, P), CTX:TOK], out[s][:]).then_inc(stored[s], 16)
                steps_of(pool, TILES, store)
                for s in range(2):
                    pool.wait_ge(stored[s], 16 * TILES // 2)

def linear_narrow(nc, hT, w, col0, n, dram, row0, spans=SPANS):
    with ExitStack() as ctx:
        sb, ps = memory(nc, ctx)
        wb, out = sb("w", [P, KD, n]), sb("out", [n, TOK])
        acc = [ps(f"acc{b}", [n, 512]) for b in range(2)]
        lo = min(t0 for t0, _ in spans)
        with stage(nc, "w_ready", "products", "copied", "stored") as (block, w_ready, products, copied, stored):
            @block.sync
            def _(sp):
                sp.dma_start(wb[:], w.rearrange("(k p) n -> p k n", p=P)[:, :, col0:col0 + n]).then_inc(w_ready, 16)
                sp.wait_ge(copied, 1)
                sp.dma_start(dram[row0:row0 + n, lo:TOK], out[:, lo:TOK]).then_inc(stored, 16)
                sp.wait_ge(stored, 16)

            @block.tensor
            def _(pe):
                pe.wait_ge(w_ready, 16)
                for b, (t0, tn) in enumerate(spans):
                    for k in range(KD):
                        mm = nc.tensor.matmul(acc[b][:, 0:tn], wb[:, k, :], hT[:, k, t0:t0 + tn],
                                              start=(k == 0), stop=(k == KD - 1))
                mm.then_inc(products, 1)

            @block.vector
            def _(dve):
                dve.wait_ge(products, 1)
                for b, (t0, tn) in enumerate(spans):
                    op = nc.vector.tensor_copy(out[:, t0:t0 + tn], acc[b][:, 0:tn])
                op.then_inc(copied, 1)


GH, GK, GV = 4, 64, 128
GKW, GVW = GH * GK, GH * GV
AB_V, AB_LR, AB_Q, AB_R, AB_U, AB_G = 256, 768, 800, 1056, 1568, 2080


def gla_features(nc, proj, gate_w, gate_b, reset, arrays, dec):
    jobs = [(m, d) for m in range(2) for d in range(2)]
    with ExitStack() as ctx:
        sb, ps = memory(nc, ctx)
        lr = [sb(f"lr{d}", [16, TOK]) for d in range(2)]
        gw = sb("gw", [16, 2, GKW])
        k, q = ([sb(f"{n}{m}", [P, TOK]) for m in range(2)] for n in ("k", "q"))
        ones = sb("one", [P, 1])
        mag, low, la, c, e, c1, e1, up, down, rest = (sb(n, [P, TOK]) for n in (
            "mag", "low", "la", "c", "e", "c1", "e1", "up", "down", "rest"))
        outs = [sb(f"o{n}", [P, TOK]) for n in range(3)]
        wc = sb("wc", [P, NCH])
        zp = [ps(f"z{i}", [P, 1024]) for i in range(2)]
        with stage(nc, "loaded", "one_set", "z_ready", "low_ready", "mag_ready", "ln_ready", "features", "sums_ready", "exps_ready",
                   "ready", "stored") as (
                block, loaded, one_set, z_ready, low_ready, mag_ready, ln_ready, features, sums_ready, exps_ready, ready, stored):
            @block.sync
            def _(sp):
                for d in range(2):
                    sp.dma_start(lr[d][:], proj[AB_LR + 16 * d:AB_LR + 16 * d + 16, :]).then_inc(loaded, 16)
                sp.dma_start(gw[:], gate_w.rearrange("d l n -> l d n")).then_inc(loaded, 16)
                for m in range(2):
                    sp.dma_start(k[m][:], proj[m * P:(m + 1) * P, :]).then_inc(loaded, 16)
                    sp.dma_start(q[m][:], proj[AB_Q + m * P:AB_Q + (m + 1) * P, :]).then_inc(loaded, 16)

            @block.tensor
            def _(pe):
                pe.wait_ge(loaded, 112)
                for i, (m, d) in enumerate(jobs):
                    if i >= 2:
                        pe.wait_ge(mag_ready, i - 1)
                        pe.wait_ge(low_ready, i - 1)
                    for t0, tn in ((0, 512), (512, 256)):
                        mm = nc.tensor.matmul(zp[i % 2][:, t0:t0 + tn], gw[:, d, m * P:(m + 1) * P], lr[d][:, t0:t0 + tn],
                                              start=True, stop=True)
                    mm.then_inc(z_ready, 1)

            @block.scalar
            def _(act):
                act.wait_ge(one_set, 1)
                for i, (m, d) in enumerate(jobs):
                    act.wait_ge(z_ready, i + 1)
                    nc.scalar.activation(mag[:], zp[i % 2][:, 0:TOK], ACT.Abs, bias=gate_b[:, 2 * d + m:2 * d + m + 1]
                                         ).then_inc(mag_ready, 1)
                    act.wait_ge(mag_ready, i + 1)
                    nc.scalar.activation(mag[:], mag[:], ACT.Exp, scale=-1.0).then_inc(ln_ready, 1)
                    act.wait_ge(ln_ready, 2 * i + 1)
                    nc.scalar.activation(mag[:], mag[:], ACT.Ln, bias=ones[:, 0:1]).then_inc(ln_ready, 1)
                    act.wait_ge(sums_ready, i + 1)
                    if i:
                        act.wait_ge(ready, i)
                        act.wait_ge(stored, 64 * i)
                    cd, ed = (c, e) if d == 0 else (c1, e1)
                    nc.scalar.activation(up[:], cd[:], ACT.Exp)
                    nc.scalar.activation(down[:], cd[:], ACT.Exp, scale=-1.0)
                    nc.scalar.activation(rest[:], ed[:], ACT.Exp)
                    last = cd[:].rearrange("p (n c) -> p n c", c=CH)[:, :, (CH - 1) * (1 - d)]
                    nc.scalar.activation(wc[:], last, ACT.Exp).then_inc(exps_ready, 1)

            @block.vector
            def _(dve):
                done = Chain(dve, features, 7)
                nc.vector.memset(ones[:], 1.0).then_inc(one_set, 1)
                cv, ev = (t[:].rearrange("p (n c) -> p n c", c=CH) for t in (c, e))
                dve.wait_ge(loaded, 112)
                for i, (m, d) in enumerate(jobs):
                    if d == 0:
                        done.start(m)
                    col = gate_b[:, 2 * d + m:2 * d + m + 1]
                    dve.wait_ge(mag_ready, i + 1)
                    nc.vector.tensor_scalar(low[:], zp[i % 2][:, 0:TOK], col, 0.0, ALU.add, ALU.min).then_inc(low_ready, 1)
                    dve.wait_ge(low_ready, i + 1)
                    dve.wait_ge(ln_ready, 2 * i + 2)
                    done(nc.vector.tensor_tensor(low[:], low[:], mag[:], ALU.subtract))
                    done(nc.vector.tensor_scalar(la[:], low[:], 1.0 / 16, None, ALU.mult))
                    if i:
                        dve.wait_ge(exps_ready, i)
                    done(nc.vector.tensor_tensor_scan(c[:], reset[:], la[:], 0.0, ALU.mult, ALU.add))
                    total = cv[:, :, CH - 1:CH].to_broadcast([P, NCH, CH])
                    total_minus = nc.vector.tensor_tensor(ev, total, cv, ALU.subtract)
                    if d == 0:
                        total_minus.then_inc(sums_ready, 1)
                    else:
                        done(total_minus)
                    if d == 1:
                        nc.vector.tensor_tensor(e1[:], c[:], la[:], ALU.subtract)
                        nc.vector.tensor_tensor(c1[:], e[:], la[:], ALU.add).then_inc(sums_ready, 1)
                    dve.wait_ge(exps_ready, i + 1)
                    if i:
                        dve.wait_ge(stored, 64 * i)
                    nc.vector.tensor_tensor(outs[0][:], k[m][:], down[:], ALU.mult)
                    nc.vector.scalar_tensor_tensor(out=outs[1][:], in0=q[m][:], scalar=GK ** -0.5, in1=up[:], op0=ALU.mult, op1=ALU.mult)
                    nc.vector.tensor_tensor(outs[2][:], k[m][:], rest[:], ALU.mult).then_inc(ready, 1)

            @block.gpsimd
            def _(pool):
                for i, (m, d) in enumerate(jobs):
                    pool.wait_ge(ready, i + 1)
                    for n in range(3):
                        pool.dma_start(arrays[d, n, m * P:(m + 1) * P, :], outs[n][:]).then_inc(stored, 16)
                    pool.dma_start(dec[d, m * P:(m + 1) * P, :], wc[:]).then_inc(stored, 16)
                pool.wait_ge(stored, 64 * len(jobs))


CC = CTX // CH


def gla_chunks(nc, ident, masks, arrays, proj, dec, ys):
    with ExitStack() as ctx:
        sb, ps = memory(nc, ctx)
        kqr = [[sb(f"kqr{s}{d}", [GK, 3, GH, CH]) for d in range(2)] for s in range(2)]
        vf = [[sb(f"vf{s}{d}", [P, GH, CH]) for d in range(2)] for s in range(2)]
        two = lambda n, shape: [sb(f"{n}{d}", shape) for d in range(2)]
        sc = two("sc", [CH, GH, CH])
        kr = two("kr", [CH, GH, GK])
        vt = two("vt", [CH, GH, GV])
        state, scaled = two("state", [GK, GH, GV]), two("scaled", [GK, GH, GV])
        o = [[sb(f"o{s}{d}", [GV, GH, CH]) for d in range(2)] for s in range(2)]
        wc = two("wc", [GK, GH, NCH])
        b_ps = [ps(f"small{d}", [CH, 2, GH, CH]) for d in range(2)]
        v_ps = [ps(f"v{d}", [CH, GH, GV]) for d in range(2)]
        g_ps = [ps(f"g{d}", [GK, GH, GV]) for d in range(2)]
        o_ps = [ps(f"o{d}", [GV, GH, CH]) for d in range(2)]
        with stage(nc, "dec_loaded", "loaded0", "loaded1", "cleared", "sc_p", "v_p", "sc_c", "kr_c", "vt_c", "grown_p",
                   "o_p", "scaled_c", "state_c", "o_c", "stored0", "stored1", "passed") as (
                block, dec_loaded, loaded0, loaded1, cleared, sc_p, v_p, sc_c, kr_c, vt_c, grown_p, o_p, scaled_c,
                state_c, o_c, stored0, stored1, passed):
            loaded, stored = (loaded0, loaded1), (stored0, stored1)

            def order(i, d, latent):
                return i if d == 0 else (NCH + CC - 1 if latent else CC - 1) - i

            def both_phases(eng, body):
                for i in range(CC):
                    body(i, i % 2, False, i < 2)
                with eng.Fori(CC // 2, NCH // 2) as t:
                    for s in range(2):
                        body(2 * t + s, s, True, False)

            @block.sync
            def _(sp):
                for d in range(2):
                    sp.dma_start(wc[d][:], dec[d].rearrange("(h k) n -> k h n", k=GK)).then_inc(dec_loaded, 16)

                def load(i, s, latent, first):
                    if not first:
                        sp.wait_ge(o_p, 2 * i - 2)
                        sp.wait_ge(v_p, 2 * i - 2)
                    for d in range(2):
                        cols = bass.ds(order(i, d, latent) * CH, CH)
                        for n in range(3):
                            sp.dma_start(kqr[s][d][:, n], arrays[d, n].rearrange("(h k) t -> k h t", k=GK)[:, :, cols]
                                         ).then_inc(loaded[s], 16)
                        sp.dma_start(vf[s][d][:], proj[AB_V:AB_V + GVW, :].rearrange("(h v) t -> v h t", v=GV)[:, :, cols]
                                     ).then_inc(loaded[s], 16)
                both_phases(sp, load)

            @block.tensor
            def _(pe):
                def step(i, s, latent, first):
                    fresh = first and s == 0
                    for d in range(2):
                        if not fresh:
                            pe.wait_ge(kr_c, 2 * i + (d - 1))
                            pe.wait_ge(sc_c, 2 * i + (d - 1))
                            pe.wait_ge(vt_c, 2 * i + (d - 1))
                        pe.wait_ge(loaded[s], (i - s) * 64 + 128)
                        pe.sem_inc(passed, 1)
                        for h in range(GH):
                            nc.tensor.matmul(b_ps[d][:, 0, h], kqr[s][d][:, 0, h], kqr[s][d][:, 1, h], start=True, stop=True)
                        for h in range(GH):
                            mm = nc.tensor.transpose(b_ps[d][:, 1, h], kqr[s][d][:, 2, h], ident[0:GK, 0:GK])
                        mm.then_inc(sc_p, 1)
                        for h in range(GH):
                            mm = nc.tensor.transpose(v_ps[d][:, h], vf[s][d][:, h], ident[:])
                        mm.then_inc(v_p, 1)
                    for d in range(2):
                        pe.wait_ge(kr_c, 2 * i + (d + 1))
                        pe.wait_ge(vt_c, 2 * i + (d + 1))
                        pe.wait_ge(sc_c, 2 * i + (d + 1))
                        if fresh:
                            pe.wait_ge(cleared, 2)
                        else:
                            pe.wait_ge(o_c, 2 * i + (d - 1))
                            pe.wait_ge(state_c, 2 * i + (d - 1))
                        pe.sem_inc(passed, 1)
                        for h in range(GH):
                            nc.tensor.matmul(o_ps[d][:, h], state[d][:, h], kqr[s][d][:, 1, h], start=True, stop=False)
                            mm = nc.tensor.matmul(o_ps[d][:, h], vt[d][:, h], sc[d][:, h], start=False, stop=True)
                        mm.then_inc(o_p, 1)
                        for h in range(GH):
                            mm = nc.tensor.matmul(g_ps[d][:, h], kr[d][:, h], vt[d][:, h], start=True, stop=True)
                        mm.then_inc(grown_p, 1)
                both_phases(pe, step)

            @block.scalar
            def _(act):
                def step(i, s, latent, first):
                    fresh = first and s == 0
                    for d in range(2):
                        act.wait_ge(sc_c, 2 * i + (d + 1))
                        if not fresh:
                            act.wait_ge(grown_p, 2 * i + (d - 1))
                        nc.scalar.copy(kr[d][:], b_ps[d][:, 1]).then_inc(kr_c, 1)
                        act.wait_ge(v_p, 2 * i + (d + 1))
                        nc.scalar.copy(vt[d][:], v_ps[d][:]).then_inc(vt_c, 1)
                    for d in range(2):
                        act.wait_ge(o_p, 2 * i + (d + 1))
                        if not first:
                            act.wait_ge(stored[s], (i - s) * 16)
                        nc.scalar.copy(o[s][d][:], o_ps[d][:]).then_inc(o_c, 1)
                both_phases(act, step)

            @block.vector
            def _(dve):
                for d in range(2):
                    nc.vector.memset(state[d][:], 0.0).then_inc(cleared, 1)
                dve.wait_ge(dec_loaded, 32)

                def step(i, s, latent, first):
                    fresh = first and s == 0
                    for d in range(2):
                        dve.wait_ge(sc_p, 2 * i + (d + 1))
                        if not fresh:
                            dve.wait_ge(o_p, 2 * i + (d - 1))
                        m = masks[:, d, 1, :].rearrange("p (o c) -> p o c", o=1).to_broadcast([CH, GH, CH])
                        nc.vector.tensor_tensor(sc[d][:], b_ps[d][:, 0], m, ALU.mult).then_inc(sc_c, 1)
                    for d in range(2):
                        if fresh:
                            dve.wait_ge(cleared, 2)
                        else:
                            dve.wait_ge(state_c, 2 * i + (d - 1))
                        dve.sem_inc(passed, 1)
                        w = wc[d][:, :, bass.ds(order(i, d, latent), 1)].to_broadcast([GK, GH, GV])
                        nc.vector.tensor_tensor(scaled[d][:], state[d][:], w, ALU.mult).then_inc(scaled_c, 1)
                    for d in range(2):
                        dve.wait_ge(scaled_c, 2 * i + (d + 1))
                        dve.wait_ge(o_p, 2 * i + (d + 1))
                        dve.wait_ge(grown_p, 2 * i + (d + 1))
                        nc.vector.tensor_tensor(state[d][:], scaled[d][:], g_ps[d][:], ALU.add).then_inc(state_c, 1)
                both_phases(dve, step)

            @block.gpsimd
            def _(pool):
                def store(i, s, latent, first):
                    pool.wait_ge(o_c, 2 * i + 2)
                    for d in range(2):
                        pool.dma_start(ys[d].rearrange("(h v) t -> v h t", v=GV)[:, :, bass.ds(order(i, d, latent) * CH, CH)],
                                       o[s][d][:]).then_inc(stored[s], 16)
                both_phases(pool, store)
                for s in range(2):
                    pool.wait_ge(stored[s], 16 * NCH)


def gla_readout(nc, ys, ones, gain, proj, mix):
    with ExitStack() as ctx:
        sb, ps = memory(nc, ctx)
        y0, y1, r, square, std, out = ([sb(f"{n}{s}", [P, TOK]) for s in range(2)] for n in ("y0", "y1", "r", "sq", "std", "out"))
        eps = sb("eps", [P, 1])
        total = [ps(f"total{s}", [P, 1024]) for s in range(2)]
        with stage(nc, "eps_set", "loaded0", "loaded1", "sum_ready", "squared", "summed", "std_ready", "silu_ready",
                   "read_step", "ready", "stored0", "stored1") as (
                block, eps_set, loaded0, loaded1, sum_ready, squared, summed, std_ready, silu_ready, read_step, ready,
                stored0, stored1):
            loaded, stored = (loaded0, loaded1), (stored0, stored1)

            @block.sync
            def _(sp):
                def load(i, s, first):
                    if not first:
                        sp.wait_ge(ready, i - 1)
                    for dst, src in ((y0[s], ys[0][bass.ds(i * P, P), :]), (y1[s], ys[1][bass.ds(i * P, P), :]),
                                     (r[s], proj[bass.ds(i * P + AB_R, P), :])):
                        sp.dma_start(dst[:], src).then_inc(loaded[s], 16)
                steps_of(sp, GH, load)

            @block.tensor
            def _(pe):
                def step(i, s, first):
                    pe.wait_ge(squared, i + 1)
                    for t0, tn in ((0, 512), (512, 256)):
                        mm = nc.tensor.matmul(total[s][:, t0:t0 + tn], ones[:], square[s][:, t0:t0 + tn], start=True, stop=True)
                    mm.then_inc(summed, 1)
                steps_of(pe, GH, step)

            @block.scalar
            def _(act):
                act.wait_ge(eps_set, 1)

                def step(i, s, first):
                    act.wait_ge(sum_ready, i + 1)
                    nc.scalar.activation(square[s][:], y0[s][:], ACT.Square).then_inc(squared, 1)
                    nc.scalar.activation(r[s][:], r[s][:], ACT.Silu).then_inc(silu_ready, 1)
                    act.wait_ge(summed, i + 1)
                    nc.scalar.activation(std[s][:], total[s][:, 0:TOK], ACT.Sqrt, bias=eps[:, 0:1], scale=1.0 / GV).then_inc(std_ready, 1)
                steps_of(act, GH, step)

            @block.vector
            def _(dve):
                done = Chain(dve, read_step, 2)
                nc.vector.memset(eps[:], EPS).then_inc(eps_set, 1)

                def step(i, s, first):
                    done.start(i)
                    dve.wait_ge(loaded[s], 48 if first else (i - s) * 24 + 48)
                    nc.vector.tensor_tensor(y0[s][:], y0[s][:], y1[s][:], ALU.add).then_inc(sum_ready, 1)
                    dve.wait_ge(std_ready, i + 1)
                    done(nc.vector.reciprocal(std[s][:], std[s][:]))
                    done(nc.vector.tensor_tensor(y0[s][:], y0[s][:], std[s][:], ALU.mult))
                    dve.wait_ge(silu_ready, i + 1)
                    if not first:
                        dve.wait_ge(stored[s], (i - s) * 8)
                    nc.vector.scalar_tensor_tensor(out=out[s][:], in0=y0[s][:], scalar=gain[:, bass.ds(i, 1)], in1=r[s][:],
                                                   op0=ALU.mult, op1=ALU.mult).then_inc(ready, 1)
                steps_of(dve, GH, step)

            @block.gpsimd
            def _(pool):
                def store(i, s, first):
                    pool.wait_ge(ready, i + 1)
                    pool.dma_start(mix[bass.ds(i * P, P), :], out[s][:]).then_inc(stored[s], 16)
                steps_of(pool, GH, store)
                for s in range(2):
                    pool.wait_ge(stored[s], 16 * GH // 2)


def gmlp(nc, ident, ones, proj, spatial_w, spatial_b, gain, mix):
    G = 4
    NT = TOK // P
    parts = ((0, 512), (512, 256))
    with ExitStack() as ctx:
        sb, ps = memory(nc, ctx)
        u, v = sb("u", [P, G, TOK]), sb("v", [P, G, TOK])
        square = sb("square", [P, G, TOK])
        mean, std, vt = sb("mean", [P, TOK]), sb("std", [P, TOK]), sb("vt", [P, NT, P])
        w, wt, bias = sb("w", [P, G, P]), sb("wt", [P, G, P]), sb("bias", [P, G, P])
        eps = sb("eps", [P, 1])
        sums = ps("sums", [P, 1024])
        turned = ps("turned", [P, 1024])
        mixed = ps("mixed", [P, 1024])
        with stage(nc, "loaded", "eps_set", "gelu_ready", "summed", "mean_ready", "centred", "squared", "squares_summed", "std_ready",
                   "norm_step", "normed", "w_turned", "w_ready", "v_turned", "v_ready", "mixed_ready", "biased", "ready", "stored") as (
                block, loaded, eps_set, gelu_ready, summed, mean_ready, centred, squared, squares_summed, std_ready, norm_step,
                normed, w_turned, w_ready, v_turned, v_ready, mixed_ready, biased, ready, stored):
            @block.sync
            def _(sp):
                for dst, row in ((v, AB_G), (u, AB_U)):
                    sp.dma_start(dst[:], proj[row:row + G * P, :].rearrange("(g p) t -> p g t", p=P)).then_inc(loaded, 16)
                sp.dma_start(w[:], spatial_w.rearrange("g t s -> t g s")).then_inc(loaded, 16)
                sp.dma_start(bias[:], spatial_b.rearrange("(o g) t -> o g t", o=1).to_broadcast([P, G, P])).then_inc(loaded, 16)

            @block.scalar
            def _(act):
                act.wait_ge(loaded, 64)
                nc.scalar.activation(v[:], v[:], ACT.Gelu_apprx_tanh).then_inc(gelu_ready, 1)
                nc.scalar.activation(u[:], u[:], ACT.Gelu_apprx_tanh).then_inc(gelu_ready, 1)
                for g in range(G):
                    act.wait_ge(centred, g + 1)
                    nc.scalar.activation(square[:, g, :], v[:, g, :], ACT.Square).then_inc(squared, 1)
                act.wait_ge(eps_set, 1)
                act.wait_ge(squares_summed, 1)
                nc.scalar.activation(std[:], sums[:, 0:TOK], ACT.Sqrt, bias=eps[:, 0:1], scale=1.0 / (G * P)).then_inc(std_ready, 1)
                act.wait_ge(w_turned, 1)
                nc.scalar.copy(wt[:], mixed[:, 0:G * P]).then_inc(w_ready, 1)
                for g in range(G):
                    act.wait_ge(v_turned, g + 1)
                    if g:
                        act.wait_ge(mixed_ready, g)
                    nc.scalar.copy(vt[:], turned[:, 0:TOK]).then_inc(v_ready, 1)

            @block.tensor
            def _(pe):
                pe.wait_ge(loaded, 64)
                for g in range(G):
                    tr = nc.tensor.transpose(mixed[:, g * P:(g + 1) * P], w[:, g, :], ident[:])
                tr.then_inc(w_turned, 1)
                pe.wait_ge(gelu_ready, 1)
                for t0, tn in parts:
                    for g in range(G):
                        mm = nc.tensor.matmul(sums[:, t0:t0 + tn], ones[:], v[:, g, t0:t0 + tn], start=(g == 0), stop=(g == G - 1))
                mm.then_inc(summed, 1)
                pe.wait_ge(squared, G)
                for t0, tn in parts:
                    for g in range(G):
                        mm = nc.tensor.matmul(sums[:, t0:t0 + tn], ones[:], square[:, g, t0:t0 + tn], start=(g == 0), stop=(g == G - 1))
                mm.then_inc(squares_summed, 1)
                pe.wait_ge(w_ready, 1)
                for g in range(G):
                    pe.wait_ge(normed, g + 1)
                    if g:
                        pe.wait_ge(v_ready, g)
                    for t in range(NT):
                        tr = nc.tensor.transpose(turned[:, t * P:(t + 1) * P], v[:, g, t * P:(t + 1) * P], ident[:])
                    tr.then_inc(v_turned, 1)
                    pe.wait_ge(v_ready, g + 1)
                    if g:
                        pe.wait_ge(biased, g)
                    for t in range(NT):
                        mm = nc.tensor.matmul(mixed[:, t * P:(t + 1) * P], vt[:, t, :], wt[:, g, :], start=True, stop=True)
                    mm.then_inc(mixed_ready, 1)

            @block.vector
            def _(dve):
                done = Chain(dve, norm_step, 1)
                done.start(0)
                nc.vector.memset(eps[:], EPS).then_inc(eps_set, 1)
                dve.wait_ge(summed, 1)
                nc.vector.tensor_scalar(mean[:], sums[:, 0:TOK], 1.0 / (G * P), None, ALU.mult).then_inc(mean_ready, 1)
                dve.wait_ge(mean_ready, 1)
                for g in range(G):
                    nc.vector.tensor_tensor(v[:, g, :], v[:, g, :], mean[:], ALU.subtract).then_inc(centred, 1)
                dve.wait_ge(std_ready, 1)
                done(nc.vector.reciprocal(std[:], std[:]))
                dve.wait_ge(centred, G)
                for g in range(G):
                    nc.vector.scalar_tensor_tensor(out=v[:, g, :], in0=v[:, g, :], scalar=gain[:, g:g + 1], in1=std[:],
                                                   op0=ALU.mult, op1=ALU.mult).then_inc(normed, 1)
                dve.wait_ge(gelu_ready, 2)
                dve.wait_ge(loaded, 64)
                for g in range(G):
                    dve.wait_ge(mixed_ready, g + 1)
                    dve.wait_ge(squared, G)
                    b = bias[:, g:g + 1, :].to_broadcast([P, NT, P])
                    nc.vector.tensor_tensor(square[:, g, :].rearrange("p (n t) -> p n t", t=P),
                                            mixed[:, 0:TOK].rearrange("p (n t) -> p n t", t=P), b, ALU.add).then_inc(biased, 1)
                    dve.wait_ge(biased, g + 1)
                    nc.vector.tensor_tensor(u[:, g, :], u[:, g, :], square[:, g, :], ALU.mult).then_inc(ready, 1)

            @block.gpsimd
            def _(pool):
                pool.wait_ge(ready, G)
                pool.dma_start(mix[GVW:GVW + G * P, :].rearrange("(g p) t -> p g t", p=P), u[:]).then_inc(stored, 16)
                pool.wait_ge(stored, 16)

SI, SG, SH, SN = 2048, 4, 8, 128
GW = SI // SG
SC = 128
NSC = TOK // SC
SCC = CTX // SC
SSD_B, SSD_C, SSD_DT, SSD_Z = 2048, 2560, 3072, 3136


def conv_silu(nc, proj, tiles, taps, bias, xbc):
    W = TOK + 8
    L0 = CTX + 6
    with ExitStack() as ctx:
        sb, _ = memory(nc, ctx)
        z = [sb(f"z{s}", [P, W]) for s in range(2)]
        acc = [sb(f"acc{s}", [P, W - 4]) for s in range(2)]
        out = [sb(f"out{s}", [P, W - 4]) for s in range(2)]
        with stage(nc, "zeroed", "loaded0", "loaded1", "tap_done", "taps_done", "ready", "stored0", "stored1") as (
                block, zeroed, loaded0, loaded1, tap_done, taps_done, ready, stored0, stored1):
            loaded, stored = (loaded0, loaded1), (stored0, stored1)

            @block.sync
            def _(sp):
                sp.wait_ge(zeroed, 2)

                def load(i, s, first):
                    if not first:
                        sp.wait_ge(taps_done, i - 1)
                    rows = proj[bass.ds(i * P, P), :]
                    sp.dma_start(z[s][:, 2:2 + CTX], rows[:, 0:CTX]).then_inc(loaded[s], 16)
                    sp.dma_start(z[s][:, L0:L0 + LAT], rows[:, CTX:TOK]).then_inc(loaded[s], 16)
                steps_of(sp, tiles, load)

            @block.vector
            def _(dve):
                done = Chain(dve, tap_done, 4)

                def step(i, s, first):
                    done.start(i)
                    dve.wait_ge(loaded[s], 32 if first else (i - s) * 16 + 32)
                    if not first:
                        dve.wait_ge(ready, i - 1)
                    done(nc.vector.tensor_scalar(acc[s][:], z[s][:, 0:W - 4], taps[:, bass.ds(i, 1)], bias[:, bass.ds(i, 1)],
                                                 ALU.mult, ALU.add))
                    for j in range(1, 5):
                        op = nc.vector.scalar_tensor_tensor(out=acc[s][:], in0=z[s][:, j:W - 4 + j],
                                                            scalar=taps[:, bass.ds(i + j * tiles, 1)], in1=acc[s][:],
                                                            op0=ALU.mult, op1=ALU.add)
                        if j < 4:
                            done(op)
                    op.then_inc(taps_done, 1)
                steps_of(dve, tiles, step)

            @block.scalar
            def _(act):
                def step(i, s, first):
                    act.wait_ge(taps_done, i + 1)
                    if not first:
                        act.wait_ge(stored[s], (i - s) * 16)
                    nc.scalar.activation(out[s][:], acc[s][:], ACT.Silu).then_inc(ready, 1)
                steps_of(act, tiles, step)

            @block.gpsimd
            def _(pool):
                for s in range(2):
                    nc.gpsimd.memset(z[s][:], 0.0).then_inc(zeroed, 1)

                def store(i, s, first):
                    pool.wait_ge(ready, i + 1)
                    rows = xbc[bass.ds(i * P, P), :]
                    pool.dma_start(rows[:, 0:CTX], out[s][:, 0:CTX]).then_inc(stored[s], 16)
                    pool.dma_start(rows[:, CTX:TOK], out[s][:, CTX + 4:CTX + 4 + LAT]).then_inc(stored[s], 16)
                steps_of(pool, tiles, store)
                for s in range(2):
                    pool.wait_ge(stored[s], 32 * ((tiles + 1 - s) // 2))


def ssd_steps(nc, ident, proj, dt_bias, a_log, reset, by_token, acum):
    R = 2 * SG * SH
    nac, eac, dtt, drt = by_token
    with ExitStack() as ctx:
        sb, ps = memory(nc, ctx)
        raw, mag, dt, da, c, e, rest = (sb(n, [R, TOK]) for n in ("raw", "mag", "dt", "da", "c", "e", "rest"))
        bias, a, one = sb("bias", [R, 1]), sb("a", [R, 1]), sb("one", [R, 1])
        turned = [ps(f"turned{n}", [P, NSC, R]) for n in range(3)]
        with stage(nc, "loaded", "act_step", "act_turned", "dve_step", "sums_ready", "rest_ready", "all_ready", "turned_ready",
                   "stored") as (
                block, loaded, act_step, act_turned, dve_step, sums_ready, rest_ready, all_ready, turned_ready, stored):
            @block.sync
            def _(sp):
                sp.dma_start(raw[:], proj[SSD_DT:SSD_DT + R, :]).then_inc(loaded, 16)
                sp.dma_start(bias[:], dt_bias.rearrange("d (h o) -> (d h) o", o=1)).then_inc(loaded, 16)
                sp.dma_start(a[:], a_log.rearrange("d (h o) -> (d h) o", o=1)).then_inc(loaded, 16)
                sp.wait_ge(all_ready, 1)
                sp.dma_start(acum, c[:]).then_inc(stored, 16)
                sp.wait_ge(stored, 16)

            @block.scalar
            def _(act):
                done = Chain(act, act_step, 4)
                done.start(0)
                act.wait_ge(loaded, 48)
                act.wait_ge(dve_step, 2)
                done(nc.scalar.activation(mag[:], raw[:], ACT.Abs, bias=bias[:, 0:1]))
                done(nc.scalar.activation(mag[:], mag[:], ACT.Exp, scale=-1.0))
                done(nc.scalar.activation(mag[:], mag[:], ACT.Ln, bias=one[:, 0:1]))
                done(nc.scalar.activation(a[:], a[:], ACT.Exp))
                act.wait_ge(sums_ready, 1)
                nc.scalar.activation(rest[:], e[:], ACT.Exp).then_inc(rest_ready, 1)
                act.wait_ge(turned_ready, 3)
                nc.scalar.mul(nac[:], turned[0][:], -1.0)
                nc.scalar.activation(eac[:], turned[0][:], ACT.Exp)
                nc.scalar.copy(dtt[:], turned[1][:])
                nc.scalar.copy(drt[:], turned[2][:])

            @block.vector
            def _(dve):
                done = Chain(dve, dve_step, 9)
                done.start(0)
                dve.wait_ge(loaded, 48)
                done(nc.vector.memset(one[:], 1.0))
                done(nc.vector.tensor_scalar(dt[:], raw[:], bias[:, 0:1], 0.0, ALU.add, ALU.max))
                dve.wait_ge(act_step, 4)
                done(nc.vector.tensor_tensor(dt[:], dt[:], mag[:], ALU.add))
                done(nc.vector.tensor_scalar(da[:], dt[:], a[:, 0:1], -1.0, ALU.mult, ALU.mult))
                done(nc.vector.tensor_tensor_scan(c[:], reset[0:R, :], da[:], 0.0, ALU.mult, ALU.add))
                cv, ev = (t[:].rearrange("p (n c) -> p n c", c=SC) for t in (c, e))
                done(nc.vector.tensor_tensor(ev, cv[:, :, SC - 1:SC].to_broadcast([R, NSC, SC]), cv, ALU.subtract))
                b = slice(R // 2, R)
                done(nc.vector.tensor_tensor(rest[b, :], c[b, :], da[b, :], ALU.subtract))
                done(nc.vector.tensor_tensor(c[b, :], e[b, :], da[b, :], ALU.add))
                nc.vector.tensor_copy(e[b, :], rest[b, :]).then_inc(sums_ready, 1)
                dve.wait_ge(rest_ready, 1)
                done(nc.vector.tensor_tensor(rest[:], rest[:], dt[:], ALU.mult))
                nc.vector.tensor_copy(one[:], bias[:]).then_inc(all_ready, 1)

            @block.tensor
            def _(pe):
                pe.wait_ge(all_ready, 1)
                for n, src in enumerate((c, dt, rest)):
                    for k in range(NSC):
                        tr = nc.tensor.transpose(turned[n][:, k, :], src[:, k * SC:(k + 1) * SC], ident[0:R, 0:R])
                    tr.then_inc(turned_ready, 1)


def ssd_groups(nc, ident, mask, by_token, acum, xbc, skip, ys):
    nac, eac, dtt, drt = by_token
    work = [(d, j, j if d == 0 else (SCC - 1 - j if j < SCC else NSC + SCC - 1 - j)) for j in range(NSC) for d in range(2)]
    NW = len(work)
    LATW = [w for w in work if w[1] >= SCC]
    FILLS = NSC + 3
    with ExitStack() as ctx:
        sb, ps = memory(nc, ctx)
        xf, bf, cf = sb("xf", [P, 4, TOK]), sb("bf", [P, TOK]), sb("cf", [P, TOK])
        xt, bt, cb = sb("xt", [P, NSC, GW]), sb("bt", [P, NSC, SN]), sb("cb", [P, NSC - SCC, SC])
        rows = [sb(f"rows{s}", [P, SH, SC]) for s in range(2)]
        two = lambda n, shape: [sb(f"{n}{d}", shape) for d in range(2)]
        shifted, decay, last = two("shifted", [P, SH, SC]), two("decay", [P, SH, SC]), two("last", [P, SH])
        xr, xd, dx = two("xr", [P, SH, HD]), two("xd", [P, SH, HD]), sb("dx", [P, SH, HD])
        state, faded = two("state", [P, SH, HD]), two("faded", [P, SH, HD])
        off, y = two("off", [P, SH, HD]), two("y", [P, SH, HD])
        bank = [ps(f"bank{i}", [P, 512]) for i in range(2)]
        off_ps, diag_ps, grow_ps = ([ps(f"{n}{d}", [P, SH, HD]) for d in range(2)] for n in ("off_ps", "diag_ps", "grow_ps"))
        names = ["loaded", "rows0", "rows1", "filled", "emptied", "shifted_c", "exp_c", "last_c", "scores_c", "xr_c", "xd_c", "dx_c",
                 "off_p", "diag_p", "grow_p", "zeroed", "passed", "faded_c", "state_c", "off_c", "y0_c", "y_c", "stored0", "stored1"]
        with stage(nc, *names) as (block, *sems):
            S = dict(zip(names, sems))
            rows_loaded, stored = (S["rows0"], S["rows1"]), (S["stored0"], S["stored1"])

            def groups(eng, body):
                body(0, True)
                with eng.Fori(1, SG) as g:
                    body(g, False)

            def heads_of(t, c, g, d):
                return t[:, c, bass.ds(g * SH + d * (SG * SH), SH)]

            def spread(t, n):
                return t.rearrange("p (h o) -> p h o", o=1).to_broadcast([P, SH, n])

            @block.sync
            def _(sp):
                def load(g, first):
                    if not first:
                        sp.wait_ge(S["filled"], g * FILLS)
                        sp.sem_inc(S["passed"], 1)
                        sp.wait_ge(S["off_p"], g * len(LATW))
                    sp.sem_inc(S["passed"], 1)
                    sp.dma_start(xf[:], xbc[bass.ds(g * GW, GW), :].rearrange("(k p) t -> p k t", p=P)).then_inc(S["loaded"], 16)
                    sp.dma_start(bf[:], xbc[bass.ds(g * SN + SSD_B, SN), :]).then_inc(S["loaded"], 16)
                    sp.dma_start(cf[:], xbc[bass.ds(g * SN + SSD_C, SN), :]).then_inc(S["loaded"], 16)
                    for w, (d, j, c) in enumerate(work):
                        s = w % 2
                        if w >= 2:
                            sp.wait_ge(S["last_c"], g * (NW - 2) + (w - 1))
                            sp.sem_inc(S["passed"], 1)
                        if w - 1 > 2 * SCC:
                            sp.wait_ge(S["shifted_c"], g * len(LATW) + (w - 1 - 2 * SCC))
                        elif w < 2 and not first:
                            sp.wait_ge(S["shifted_c"], g * len(LATW) + (w - 1))
                        sp.sem_inc(S["passed"], 1)
                        sp.dma_start(rows[s][:], acum[bass.ds(g * SH + d * (SG * SH), SH), c * SC:(c + 1) * SC]
                                     .rearrange("(o h) t -> o h t", o=1).to_broadcast([P, SH, SC])).then_inc(rows_loaded[s], 16)
                groups(sp, load)

            @block.tensor
            def _(pe):
                def group(g, first):
                    pe.wait_ge(S["loaded"], g * 48 + 48)
                    for f in range(FILLS):
                        if f >= 2 or not first:
                            pe.wait_ge(S["emptied"], g * FILLS + (f - 1 if f >= 2 else 0))
                        b = bank[f % 2]
                        if f < NSC:
                            for k in range(4):
                                mm = nc.tensor.transpose(b[:, k * P:(k + 1) * P], xf[:, k, f * SC:(f + 1) * SC], ident[:])
                        elif f < NSC + 2:
                            for k in range(4 if f == NSC else 2):
                                c = k + 4 * (f - NSC)
                                mm = nc.tensor.transpose(b[:, k * P:(k + 1) * P], bf[:, c * SC:(c + 1) * SC], ident[:])
                        else:
                            for c in range(SCC, NSC):
                                mm = nc.tensor.matmul(b[:, (c - SCC) * SC:(c - SCC + 1) * SC], bf[:, c * SC:(c + 1) * SC],
                                                      cf[:, c * SC:(c + 1) * SC], start=True, stop=True)
                        mm.then_inc(S["filled"], 1)
                    pe.wait_ge(S["emptied"], g * FILLS + FILLS)
                    m = 0
                    for w, (d, j, c) in enumerate(work):
                        if j >= SCC:
                            mm_n = g * len(LATW) + m
                            if not (first and m < 2):
                                pe.wait_ge(S["y0_c"], mm_n - 1)
                            pe.wait_ge(S["state_c"], g * (NW - 2) + (w - 1))
                            nc.tensor.matmul(off_ps[d][:].rearrange("p h v -> p (h v)"), cf[:, c * SC:(c + 1) * SC],
                                             state[d][:].rearrange("p h v -> p (h v)"), start=True, stop=True).then_inc(S["off_p"], 1)
                            pe.wait_ge(S["scores_c"], mm_n + 1)
                            pe.wait_ge(S["xd_c"], mm_n + 1)
                            for h in range(SH):
                                mm = nc.tensor.matmul(diag_ps[d][:, h], decay[d][:, h], xd[d][:, h], start=True, stop=True)
                            mm.then_inc(S["diag_p"], 1)
                            m += 1
                        if j < NSC - 1:
                            k = g * (NW - 2) + w
                            pe.wait_ge(S["xr_c"], k + 1)
                            if not (first and w < 2):
                                pe.wait_ge(S["state_c"], k - 1)
                            nc.tensor.matmul(grow_ps[d][:].rearrange("p h v -> p (h v)"), bt[:, c, :],
                                             xr[d][:].rearrange("p h v -> p (h v)"), start=True, stop=True).then_inc(S["grow_p"], 1)
                groups(pe, group)

            @block.scalar
            def _(act):
                def group(g, first):
                    for f in range(FILLS):
                        act.wait_ge(S["filled"], g * FILLS + (f + 1))
                        if not first and f == 0:
                            act.wait_ge(S["grow_p"], g * (NW - 2))
                            act.wait_ge(S["scores_c"], g * len(LATW))
                            act.wait_ge(S["xr_c"], g * (NW - 2))
                            act.wait_ge(S["xd_c"], g * len(LATW))
                            act.wait_ge(S["dx_c"], g * (NSC - SCC))
                        b = bank[f % 2]
                        if f < NSC:
                            op = nc.scalar.copy(xt[:, f, :], b[:])
                        elif f < NSC + 2:
                            k, c = (4, 0) if f == NSC else (2, 4)
                            op = nc.scalar.copy(bt[:, c:c + k, :], b[:, 0:k * P])
                        else:
                            op = nc.scalar.copy(cb[:], b[:])
                        op.then_inc(S["emptied"], 1)
                    m = 0
                    for w, (d, j, c) in enumerate(work):
                        s = w % 2
                        act.wait_ge(rows_loaded[s], g * (8 * NW) + 16 * (w // 2 + 1))
                        if j < NSC - 1:
                            if not (first and w < 2):
                                act.wait_ge(S["faded_c"], g * (NW - 2) + (w - 1))
                            edge = (SC - 1) * (1 - d)
                            nc.scalar.activation(last[d][:], rows[s][:, :, edge], ACT.Exp).then_inc(S["last_c"], 1)
                        if j >= SCC:
                            mm_n = g * len(LATW) + m
                            act.wait_ge(S["shifted_c"], mm_n + 1)
                            if not (first and m < 2):
                                act.wait_ge(S["diag_p"], mm_n - 1)
                            act.sem_inc(S["passed"], 1)
                            for h in range(SH):
                                op = nc.scalar.activation(decay[d][:, h], shifted[d][:, h], ACT.Exp,
                                                          bias=nac[:, c, bass.ds(g * SH + (d * (SG * SH) + h), 1)])
                            op.then_inc(S["exp_c"], 1)
                            m += 1
                groups(act, group)

            @block.gpsimd
            def _(pool):
                def group(g, first):
                    pool.wait_ge(S["emptied"], g * FILLS + FILLS)
                    m = 0
                    for w, (d, j, c) in enumerate(work):
                        xc = xt[:, c, :].rearrange("p (h v) -> p h v", v=HD)
                        if j < NSC - 1:
                            k = g * (NW - 2) + w
                            if not (first and w < 2):
                                pool.wait_ge(S["grow_p"], k - 1)
                            pool.sem_inc(S["passed"], 1)
                            nc.gpsimd.tensor_tensor(xr[d][:], xc, spread(heads_of(drt, c, g, d), HD), ALU.mult).then_inc(S["xr_c"], 1)
                        if j >= SCC:
                            mm_n = g * len(LATW) + m
                            if not (first and m < 2):
                                pool.wait_ge(S["diag_p"], mm_n - 1)
                            pool.sem_inc(S["passed"], 1)
                            nc.gpsimd.tensor_tensor(xd[d][:], xc, spread(heads_of(dtt, c, g, d), HD), ALU.mult).then_inc(S["xd_c"], 1)
                            if d == 0:
                                if not (first and m < 1):
                                    pool.wait_ge(S["y_c"], g * (NSC - SCC) + m // 2)
                                pool.sem_inc(S["passed"], 1)
                                nc.gpsimd.tensor_tensor(dx[:], xc, spread(skip[:, bass.ds(g * SH, SH)], HD), ALU.mult
                                                        ).then_inc(S["dx_c"], 1)
                            store(g, m - 1)
                            m += 1
                    store(g, len(LATW) - 1)

                def store(g, m):
                    if m < 0:
                        return
                    d, j, c = LATW[m]
                    if d == 0:
                        pool.wait_ge(S["y_c"], g * (NSC - SCC) + (m // 2 + 1))
                    else:
                        pool.wait_ge(S["y0_c"], g * len(LATW) + (m + 1))
                    pool.dma_start(ys[d][(c - SCC) * SC:(c - SCC + 1) * SC, bass.ds(g * GW, GW)],
                                   y[d][:].rearrange("p h v -> p (h v)")).then_inc(stored[d], 16)
                groups(pool, group)
                for d in range(2):
                    pool.wait_ge(stored[d], 16 * SG * (NSC - SCC))

            @block.vector
            def _(dve):
                V = nc.vector

                def shift(g, first, m):
                    d, j, c = LATW[m]
                    w = work.index(LATW[m])
                    s = w % 2
                    dve.wait_ge(rows_loaded[s], g * (8 * NW) + 16 * (w // 2 + 1))
                    if not (first and m < 2):
                        dve.wait_ge(S["exp_c"], g * len(LATW) + (m - 1))
                    V.tensor_tensor(shifted[d][:], rows[s][:], mask[:, d, :].rearrange("p (o t) -> p o t", o=1)
                                    .to_broadcast([P, SH, SC]), ALU.add).then_inc(S["shifted_c"], 1)

                def group(g, first):
                    if not first:
                        dve.wait_ge(S["off_p"], g * len(LATW))
                        dve.wait_ge(S["faded_c"], g * (NW - 2))
                    for d in range(2):
                        V.memset(state[d][:], 0.0).then_inc(S["zeroed"], 1)
                    dve.wait_ge(S["zeroed"], g * 2 + 2)
                    m = 0
                    for w, (d, j, c) in enumerate(work):
                        if j < NSC - 1 and j < SCC:
                            fade(g, w, d, j, None)
                        if j < SCC:
                            if w + 1 == 2 * SCC:
                                shift(g, first, 0)
                            continue
                        mm_n = g * len(LATW) + m
                        if m + 1 < len(LATW):
                            shift(g, first, m + 1)
                        dve.wait_ge(S["exp_c"], mm_n + 1)
                        dve.wait_ge(S["emptied"], g * FILLS + FILLS)
                        V.tensor_tensor(decay[d][:], decay[d][:], cb[:, c - SCC, :].rearrange("p (o t) -> p o t", o=1)
                                        .to_broadcast([P, SH, SC]), ALU.mult).then_inc(S["scores_c"], 1)
                        if j < NSC - 1:
                            fade(g, w, d, j, mm_n)
                        dve.wait_ge(S["off_p"], mm_n + 1)
                        dve.sem_inc(S["passed"], 1)
                        V.tensor_tensor(off[d][:], off_ps[d][:], spread(heads_of(eac, c, g, d), HD), ALU.mult).then_inc(S["off_c"], 1)
                        dve.wait_ge(S["off_c"], mm_n + 1)
                        dve.wait_ge(S["diag_p"], mm_n + 1)
                        if not (first and m < 2):
                            dve.wait_ge(stored[d], (g * len(LATW) + (m - d)) * 8)
                        V.tensor_tensor(y[d][:], off[d][:], diag_ps[d][:], ALU.add).then_inc(S["y0_c"], 1)
                        if d == 0:
                            dve.wait_ge(S["y0_c"], mm_n + 1)
                            dve.wait_ge(S["dx_c"], g * (NSC - SCC) + (m // 2 + 1))
                            V.tensor_tensor(y[d][:], y[d][:], dx[:], ALU.add).then_inc(S["y_c"], 1)
                        m += 1

                def fade(g, w, d, j, mm_n):
                    k = g * (NW - 2) + w
                    dve.wait_ge(S["last_c"], k + 1)
                    if w >= 2:
                        dve.wait_ge(S["state_c"], k - 1)
                    V.tensor_tensor(faded[d][:], state[d][:], spread(last[d][:], HD), ALU.mult).then_inc(S["faded_c"], 1)
                    dve.wait_ge(S["faded_c"], k + 1)
                    dve.wait_ge(S["grow_p"], k + 1)
                    if mm_n is not None:
                        dve.wait_ge(S["off_p"], mm_n + 1)
                    V.tensor_tensor(state[d][:], faded[d][:], grow_ps[d][:], ALU.add).then_inc(S["state_c"], 1)
                groups(dve, group)



def ssd_readout(nc, ident, ones, ys, proj, gain, out):
    T = GW // P
    with ExitStack() as ctx:
        sb, ps = memory(nc, ctx)
        y0, y1, z, gated, square = ([sb(f"{n}{s}", [P, 4, 512]) for s in range(2)] for n in ("y0", "y1", "z", "gated", "sq"))
        std = [sb(f"std{s}", [P, LAT]) for s in range(2)]
        eps = sb("eps", [P, 1])
        turned = [ps(f"turned{t}", [P, LAT]) for t in range(T)]
        total = [ps(f"total{s}", [P, LAT]) for s in range(2)]
        with stage(nc, "eps_set", "loaded0", "loaded1", "sum_ready", "turned_ready", "silu_ready", "gated_ready", "squared",
                   "summed", "std_ready", "rstd_ready", "ready") as (
                block, eps_set, loaded0, loaded1, sum_ready, turned_ready, silu_ready, gated_ready, squared, summed,
                std_ready, rstd_ready, ready):
            loaded = (loaded0, loaded1)

            @block.sync
            def _(sp):
                def load(g, s, first):
                    if not first:
                        sp.wait_ge(gated_ready, T * g - T)
                    for dst, d in ((y0[s], 0), (y1[s], 1)):
                        sp.dma_start(dst[:], ys[d].rearrange("(n p) f -> p n f", p=P)[:, :, bass.ds(g * GW, GW)]).then_inc(loaded[s], 16)
                    sp.dma_start(z[s][:], proj[bass.ds(g * GW + SSD_Z, GW), CTX:TOK].rearrange("(k p) t -> p k t", p=P)).then_inc(loaded[s], 16)
                steps_of(sp, SG, load)

            @block.tensor
            def _(pe):
                def step(g, s, first):
                    pe.wait_ge(sum_ready, g + 1)
                    for k in range(T):
                        if not (first and s == 0):
                            pe.wait_ge(gated_ready, T * g + (k - T + 1))
                        for n in range(4):
                            tr = nc.tensor.transpose(turned[k][:, n * P:(n + 1) * P], y0[s][:, n, k * P:(k + 1) * P], ident[:])
                        tr.then_inc(turned_ready, 1)
                    if not first:
                        pe.wait_ge(std_ready, g - 1)
                    pe.wait_ge(squared, g + 1)
                    for k in range(T):
                        mm = nc.tensor.matmul(total[s][:], ones[:], square[s][:, k, :], start=(k == 0), stop=(k == T - 1))
                    mm.then_inc(summed, 1)
                steps_of(pe, SG, step)

            @block.scalar
            def _(act):
                act.wait_ge(eps_set, 1)

                def step(g, s, first):
                    act.wait_ge(loaded[s], 48 if first else (g - s) * 24 + 48)
                    nc.scalar.activation(z[s][:], z[s][:], ACT.Silu).then_inc(silu_ready, 1)
                    act.wait_ge(gated_ready, T * g + T)
                    if not first:
                        act.wait_ge(summed, g - 1)
                    nc.scalar.activation(square[s][:], gated[s][:], ACT.Square).then_inc(squared, 1)
                    act.wait_ge(summed, g + 1)
                    if not first:
                        act.wait_ge(ready, g - 1)
                    nc.scalar.activation(std[s][:], total[s][:], ACT.Sqrt, bias=eps[:, 0:1], scale=1.0 / GW).then_inc(std_ready, 1)
                steps_of(act, SG, step)

            @block.vector
            def _(dve):
                nc.vector.memset(eps[:], EPS).then_inc(eps_set, 1)

                def step(g, s, first):
                    dve.wait_ge(loaded[s], 48 if first else (g - s) * 24 + 48)
                    nc.vector.tensor_tensor(y0[s][:], y0[s][:], y1[s][:], ALU.add).then_inc(sum_ready, 1)
                    dve.wait_ge(silu_ready, g + 1)
                    if not first:
                        dve.wait_ge(ready, g - 1)
                    for k in range(T):
                        dve.wait_ge(turned_ready, T * g + (k + 1))
                        nc.vector.tensor_tensor(gated[s][:, k, :], turned[k][:], z[s][:, k, :], ALU.mult).then_inc(gated_ready, 1)
                    dve.wait_ge(std_ready, g + 1)
                    nc.vector.reciprocal(std[s][:], std[s][:]).then_inc(rstd_ready, 1)
                    dve.wait_ge(rstd_ready, g + 1)
                    for k in range(T):
                        into = out[:, bass.ds(T * g + k, 1), CTX:TOK].rearrange("p o (r c) -> p (o c) r", c=64)
                        op = nc.vector.scalar_tensor_tensor(
                            out=into, in0=gated[s][:, k, :].rearrange("p (c r) -> p c r", r=8), scalar=gain[:, bass.ds(T * g + k, 1)],
                            in1=std[s][:].rearrange("p (c r) -> p c r", r=8), op0=ALU.mult, op1=ALU.mult)
                    op.then_inc(ready, 1)
                steps_of(dve, SG, step)


LAYERS = 2
GATE_MIX, GATE_FFN = 2, 5
SHIFT_MIX, SCALE_MIX, SHIFT_FFN, SCALE_FFN = 0, 1, 3, 4


def gates_of(modT, which):
    return modT[:, KD * which:KD * (which + 1), :]


def load_tables(nc, jobs):
    with stage(nc, "loaded") as (block, loaded):
        @block.sync
        def _(sp):
            for dst, src in jobs:
                sp.dma_start(dst[:], src).then_inc(loaded, 16)
            sp.wait_ge(loaded, 16 * len(jobs))


def on_lanes(vec, n):
    return vec.rearrange("(o n) -> o n", o=1).to_broadcast([P, n])


def build(nc, a, out):
    def dram(name, shape):
        return nc.dram_tensor(name, shape, F32, kind="Internal").ap()

    proj = dram("proj", (5184, TOK))
    mix = dram("mix", (D, TOK))
    rot = dram("rot", (1536, TOK))
    mixed = dram("mixed", (1792, TOK))
    rwkv_arrays = dram("rwkv_arrays", (2, 4, RW, TOK))
    rwkv_dec = dram("rwkv_dec", (2, RW, NCH))
    bonus, gate = dram("bonus", (RW, LAT)), dram("gate", (RW, LAT))
    rwkv_ch = dram("rwkv_ch", (2, NCH, CH, 4, RW))
    rwkv_ys = dram("rwkv_ys", (2, RW, LAT))
    gla_arrays = dram("gla_arrays", (2, 3, GKW, TOK))
    gla_dec = dram("gla_dec", (2, GKW, NCH))
    gla_ys = dram("gla_ys", (2, GVW, TOK))
    xbc, acum = dram("xbc", (3072, TOK)), dram("acum", (2 * SG * SH, TOK))
    ssd_ys = dram("ssd_ys", (2, LAT, SI))

    with ExitStack() as ctx:
        sb, _ = memory(nc, ctx)
        xT = sb("xT", [P, KD, TOK])
        ident, ones, block_ones = sb("ident", [P, P]), sb("ones", [P, P]), sb("block_ones", [P, P])
        load_tables(nc, [(ident, a["identity"]), (ones, a["all_ones"]), (block_ones, a["block_ones"])])

        def block_of(x_parts, c, c_ctx, w_mod, b_mod, gains, mixers, w_ffn_in, w_ffn_out, final):
            load_tokens(nc, xT, ident, x_parts)
            with ExitStack() as inner:
                sb, _ = memory(nc, inner)
                cond_cols, cond = sb("cond_cols", [P, 2 * KD]), sb("cond", [P, KD, 2])
                last_gain = sb("last_gain", [P, KD])
                gain = [sb(f"gain{i}", [P, KD]) for i in range(2 * LAYERS)]
                b_cols = [sb(f"b_cols{i}", [P, 6 * KD]) for i in range(LAYERS)]
                modT = [sb(f"modT{i}", [P, 6 * KD, 2]) for i in range(LAYERS)]
                columns(nc, ident, [(cond_cols[:, 0:KD], c), (cond_cols[:, KD:2 * KD], c_ctx), (last_gain, final)]
                        + list(zip(gain, gains)) + [(b_cols[i], b_mod[i]) for i in range(LAYERS)])
                with stage(nc, "silu_done") as (block, silu_done):
                    @block.scalar
                    def _(act):
                        for b in range(2):
                            nc.scalar.activation(cond[:, :, b], cond_cols[:, KD * b:KD * (b + 1)], ACT.Silu)
                for i in range(LAYERS):
                    modulation(nc, ident, cond, w_mod[i], b_cols[i], modT[i])
                for i in range(LAYERS):
                    spans = SPANS if i < LAYERS - 1 else SPANS[:1]
                    mixers[i](modT[i], gain[2 * i])
                    with ExitStack() as ffn:
                        hT = memory(nc, ffn)[0]("hT", [P, KD, TOK])
                        rms_modulate(nc, xT, hT, ones, gain[2 * i + 1], modT[i], SHIFT_FFN, SCALE_FFN, spans)
                        swiglu(nc, xT, hT, w_ffn_in[i], w_ffn_out[i], gates_of(modT[i], GATE_FFN), spans)
                rms_modulate(nc, xT, xT, ones, last_gain, spans=SPANS[:1])

        def project(modT, gain, jobs, by_column=False):
            with ExitStack() as inner:
                hT = memory(nc, inner)[0]("hT", [P, KD, TOK])
                rms_modulate(nc, xT, hT, ones, gain, modT, SHIFT_MIX, SCALE_MIX, by_column=by_column)
                for w, col0, n, spans in jobs:
                    if n < 256:
                        linear_narrow(nc, hT, w, col0, n, proj, col0, spans)
                    else:
                        linear(nc, hT, w, col0, n, ("store", proj, col0), spans)

        def add_out(modT, w, spans):
            with ExitStack() as inner:
                hT = memory(nc, inner)[0]("hT", [P, KD, TOK])
                load_columns(nc, hT, mix, min(t0 for t0, _ in spans))
                linear(nc, hT, w, 0, D, ("residual", xT, gates_of(modT, GATE_MIX)), spans)

        def attention_layer(modT, gain):
            project(modT, gain, [(a["w_in_even"][0], 0, 1536, SPANS)])
            with ExitStack() as inner:
                sb, _ = memory(nc, inner)
                cos, sin, gains = sb("cos", [P, TOK]), sb("sin", [P, TOK]), sb("gains", [P, 10])
                window, sinks = sb("window", [P, 4, TOK]), sb("sinks", [P, 8])
                load_tables(nc, [(cos, a["rope_cos"]), (sin, a["rope_sin"]), (window, a["window_mask"]),
                                 (sinks, on_lanes(a["sink_b"][0], 8))])
                columns(nc, ident, [(gains, a["qk_gains"])])
                with stage(nc, "negated") as (block, negated):
                    @block.vector
                    def _(dve):
                        nc.vector.tensor_scalar(sinks[:], sinks[:], -1.0, None, ALU.mult)
                even_mixer(nc, ident, proj, rot, mix, (block_ones, cos, sin), gains[:].rearrange("p (n t) -> p t n", n=2),
                           window, sinks)
            add_out(modT, a["w_out_even"][0], SPANS)

        def rwkv_layer(modT, gain):
            w = a["w_in_odd"][0]
            project(modT, gain, [(w, 0, 512, SPANS[:1]), (w, 512, 2816, SPANS)])
            with ExitStack() as inner:
                sb, _ = memory(nc, inner)
                mask, exchange = sb("mask", [P, 4, TOK]), sb("exchange", [P, P])
                load_tables(nc, [(mask, a["neighbour_mask"]), (exchange, a["exchange"])])
                attention(nc, ident, 8, proj, 0, 512, 1, proj, 1024, mix, 0, QUERIES_MASKED, HD ** -0.5, mask=mask,
                          rpb=(a["rpb_padded"], exchange), q_from=CTX)
            with ExitStack() as inner:
                sb, _ = memory(nc, inner)
                mu, kk, ka, rk, w0, a0, ln_w, ln_b = (sb(n, [P, k]) for n, k in (
                    ("mu", 14), ("kk", 4), ("ka", 4), ("rk", 4), ("w0", 8), ("a0", 8), ("ln_w", 4), ("ln_b", 4)))
                reset, masks = sb("reset", [P, TOK]), sb("masks", [CH, 2, 9, CH])
                load_tables(nc, [(reset, a["scan_reset"]), (masks, a["chunk_masks"])])
                columns(nc, ident, [(mu, a["shift_mu"][0]), (kk, a["k_k"][0]), (ka, a["k_a"][0]),
                                    (rk, a["r_k"][0].rearrange("h n -> (h n)")), (w0, a["decay_w0"][0].rearrange("d n -> (d n)")),
                                    (a0, a["iclr_a0"][0].rearrange("d n -> (d n)")), (ln_w, a["ln_x_w"][0]), (ln_b, a["ln_x_b"][0])])
                shift_mix(nc, proj, 1536, 14, mu, mixed)
                rwkv_features(nc, mixed, a["decay_w2"][0], a["iclr_a2"][0], a["gate_g2"][0], (kk, ka, rk, w0, a0), block_ones,
                              reset, rwkv_arrays, rwkv_dec, bonus, gate)
                rwkv_chunks(nc, ident, masks, rwkv_arrays, mixed, rwkv_ch)
                rwkv_recurrence(nc, rwkv_ch, rwkv_dec, rwkv_ys)
                rwkv_readout(nc, rwkv_ys, block_ones, ln_w, ln_b, bonus, gate, mix, RW)
            add_out(modT, a["w_out_odd"][0], SPANS[:1])

        def gla_layer(modT, gain):
            w = a["ab_w_in_2"][0]
            project(modT, gain, [(w, 0, 768, SPANS), (w, AB_LR, 32, SPANS), (w, AB_Q, 1792, SPANS)])
            with ExitStack() as inner:
                sb, _ = memory(nc, inner)
                gate_b, gla_gain, v_gain = sb("gate_b", [P, 4]), sb("gla_gain", [P, 4]), sb("v_gain", [P, 4])
                reset, masks = sb("reset", [P, TOK]), sb("masks", [CH, 2, 9, CH])
                load_tables(nc, [(reset, a["scan_reset"]), (masks, a["chunk_masks"])])
                columns(nc, ident, [(gate_b, a["ab_gate_b_2"][0].rearrange("d n -> (d n)")), (gla_gain, a["ab_gla_norm_g_2"][0]),
                                    (v_gain, a["ab_vnorm_g_2"][0])])
                gla_features(nc, proj, a["ab_gate_w_2"][0], gate_b, reset, gla_arrays, gla_dec)
                gla_chunks(nc, ident, masks, gla_arrays, proj, gla_dec, gla_ys)
                gla_readout(nc, gla_ys, ones, gla_gain, proj, mix)
                gmlp(nc, ident, ones, proj, a["ab_spatial_w_2"][0], a["ab_spatial_b_2"][0], v_gain, mix)
            add_out(modT, a["ab_w_out_2"][0], SPANS)

        def ssd_layer(modT, gain):
            w = a["ssd_w_in_2"][0]
            project(modT, gain, [(w, 0, 3072, SPANS), (w, SSD_DT, 64, SPANS), (w, SSD_Z, SI, SPANS[:1])], by_column=True)
            with ExitStack() as inner:
                sb, _ = memory(nc, inner)
                ssd_gain = sb("ssd_gain", [P, 16])
                with ExitStack() as scan:
                    sb, _ = memory(nc, scan)
                    taps, bias, skip = sb("taps", [P, 5 * 24]), sb("bias", [P, 24]), sb("skip", [P, SG * SH])
                    reset, mask = sb("reset", [P, TOK]), sb("mask", [P, 2, SC])
                    by_token = [sb(f"by_token{n}", [P, NSC, 2 * SG * SH]) for n in range(4)]
                    load_tables(nc, [(reset, a["scan_reset_ssd"]), (mask, a["ssd_mask"]),
                                     (skip, on_lanes(a["ssd_d_2"][0], SG * SH))])
                    columns(nc, ident, [(taps[:, 24 * j:24 * (j + 1)], a["ssd_conv_w_2"][0, j]) for j in range(5)]
                            + [(bias, a["ssd_conv_b_2"][0]), (ssd_gain, a["ssd_norm_g_2"][0])])
                    conv_silu(nc, proj, 24, taps, bias, xbc)
                    ssd_steps(nc, ident, proj, a["ssd_dt_bias_2"][0], a["ssd_a_log_2"][0], reset, by_token, acum)
                    ssd_groups(nc, ident, mask, by_token, acum, xbc, skip, ssd_ys)
                wide = memory(nc, inner)[0]("wide", [P, SI // P, TOK])
                ssd_readout(nc, ident, ones, ssd_ys, proj, ssd_gain, wide)
                linear(nc, wide, a["ssd_w_out_2"][0], 0, D, ("residual", xT, gates_of(modT, GATE_MIX)), SPANS[:1])

        block_of([(a["ctx"][0], 0), (a["x"][0], CTX)], a["c"][0], a["c_ctx"], a["w_mod"], a["b_mod"],
                 [a["norm_mix"][0], a["norm_ffn"][0], a["norm_mix"][1], a["norm_ffn"][1]],
                 (attention_layer, rwkv_layer), a["w_ffn_in"], a["w_ffn_out"], a["norm_out"])
        block_of([(a["ctx_2"][0], 0)], a["c_2"][0], a["c_ctx_2"], a["mod_w_2"], a["mod_b_2"],
                 [a["norm_g_2"][0, 0], a["norm_g_2"][0, 1], a["norm_g_2"][1, 0], a["norm_g_2"][1, 1]],
                 (gla_layer, ssd_layer), a["ffn_w_in_2"], a["ffn_w_out_2"], a["final_norm_g_2"])
        store_tokens(nc, xT, ident, out)



def rope_tables():
    t = np.arange(LAT)
    inv = 10000.0 ** (-np.arange(16) / 16)
    ang = np.concatenate([(t // 64)[:, None] * inv, (t % 64)[:, None] * inv], -1).T
    cos, sin = np.ones((P, TOK), np.float32), np.zeros((P, TOK), np.float32)
    for h in range(4):
        cos[32 * h:32 * h + 32, CTX:] = np.cos(ang)
        sin[32 * h:32 * h + 32, CTX:] = np.sin(ang) * (1 if h % 2 else -1)
    return cos, sin


def window_mask():
    q, k = np.arange(LAT)[:, None], np.arange(LAT)[None]
    m = np.zeros((LAT, TOK), np.float32)
    m[:, CTX:] = np.where(np.abs(q - k) <= 128, 0, NEG)
    return np.ascontiguousarray(m.reshape(4, P, TOK).transpose(1, 0, 2))


def neighbour_mask():
    q, k = np.arange(LAT)[:, None] % 64, np.arange(LAT)[None] % 64
    start = np.clip(q - 8, 0, 48)
    m = np.zeros((LAT, TOK), np.float32)
    m[:, CTX:] = np.where((k >= start) & (k < start + 16), 0, NEG)
    return np.ascontiguousarray(m.reshape(4, P, TOK).transpose(1, 0, 2))


def chunk_masks():
    j, t = np.arange(64)[:, None], np.arange(64)[None]
    out = np.zeros((64, 2, 9, 64), np.float32)
    for d in range(2):
        before, pos = (j < t, t) if d == 0 else (j > t, 63 - t)
        out[:, d, 0], out[:, d, 1], out[:, d, 2] = before, before | (j == t), -1.0 * (before | (j == t))
        for n in range(6):
            s = 1 << n
            out[:, d, 3 + n] = -1.0 * (before & (j // (2 * s) == t // (2 * s)) & (j // s != t // s))
    return out


def scan_reset():
    m = np.ones((P, TOK), np.float32)
    m[:, ::64] = 0
    return m


def scan_reset_ssd():
    m = np.ones((P, TOK), np.float32)
    m[:, ::128] = 0
    return m


def ssd_mask():
    s, l = np.arange(128)[:, None], np.arange(128)[None]
    out = np.zeros((128, 2, 128), np.float32)
    out[:, 0], out[:, 1] = np.where(s <= l, 0, NEG), np.where(s >= l, 0, NEG)
    return out


def tables():
    cos, sin = rope_tables()
    exchange = np.zeros((P, P), np.float32)
    for p in range(P):
        exchange[p, p // 64 * 64 + 63 - p % 64] = HD ** 0.5
    return {"identity": np.eye(P, dtype=np.float32), "all_ones": np.ones((P, P), np.float32),
            "block_ones": np.kron(np.eye(2), np.ones((HD, HD))).astype(np.float32),
            "rope_cos": cos, "rope_sin": sin, "window_mask": window_mask(), "neighbour_mask": neighbour_mask(),
            "exchange": exchange, "scan_reset": scan_reset(), "scan_reset_ssd": scan_reset_ssd(),
            "chunk_masks": chunk_masks(), "ssd_mask": ssd_mask()}


def kernel(**inputs):
    import concourse.bacc as bacc
    from concourse.bass_utils import run_bass_kernel_spmd

    arrays = {n: np.ascontiguousarray(v) for n, v in inputs.items()}
    rpb = arrays.pop("rpb_c")
    padded = np.zeros((8, 15, 127), rpb.dtype)
    padded[:, :, 48:79] = rpb[0]
    arrays["rpb_padded"] = padded
    q, k = arrays.pop("q_norm_a")[0], arrays.pop("k_norm_a")[0]
    swap = lambda g: np.concatenate([g[32:], g[:32]])
    arrays["qk_gains"] = np.concatenate([g for turn in (lambda g: g, swap) for g in [turn(q)] * 8 + [turn(k)] * 2])
    arrays.update(tables())

    nc = bacc.Bacc("TRN2", target_bir_lowering=False, num_devices=1)
    aps = {n: nc.dram_tensor(f"in_{n}", v.shape, mybir.dt.from_np(v.dtype), kind="ExternalInput").ap()
           for n, v in arrays.items()}
    out = nc.dram_tensor("out_0", (LAT, D), F32, kind="ExternalOutput").ap()
    build(nc, aps, out)
    got = run_bass_kernel_spmd(nc, [{f"in_{n}": v for n, v in arrays.items()}], core_ids=[0])
    return got.results[0]["out_0"].reshape(1, LAT, D)
```

```python
from contextlib import ExitStack, contextmanager

import numpy as np

import concourse.bass as bass
from concourse import mybir

F32 = mybir.dt.float32
F32R = mybir.dt.float32r
ALU = mybir.AluOpType
ACT = mybir.ActivationFunctionType
AX = mybir.AxisListType.X

P = 128
D = 1024
KD = D // P
CTX = 256
LAT = 512
TOK = CTX + LAT
FF = 2816
FT = FF // P
HD = 64
EPS = 1e-6
NEG = -1e30
SPANS = ((CTX, LAT), (0, CTX))


@contextmanager
def stage(nc, *names):
    sems = [nc.alloc_semaphore(f"{n}_{nc.next_id()}") for n in names]
    with nc.Block() as block:
        yield (block, *sems)
    nc.clear_and_free_semaphores(sems)
    nc.all_engine_barrier()


def memory(nc, ctx):
    def sb(name, shape, dt=F32):
        return ctx.enter_context(nc.sbuf_tensor(f"{name}_{nc.next_id()}", shape, dt))

    def ps(name, shape):
        return ctx.enter_context(nc.psum_tensor(f"{name}_{nc.next_id()}", shape, F32))
    return sb, ps


class Halves:

    def __init__(self, sb, name, shape):
        self.shape = shape
        self.hi, self.lo = sb(f"{name}_hi", shape, F32R), sb(f"{name}_lo", shape, F32R)


def three_pass(nc, out, w, x, start, stop):
    nc.tensor.matmul(out, w[0], x[0], start=start, stop=False)
    nc.tensor.matmul(out, w[0], x[1], start=False, stop=False)
    return nc.tensor.matmul(out, w[1], x[0], start=False, stop=stop)


def steps_of(eng, n, body):
    for i in range(min(n, 2)):
        body(i, i, True)
    if n // 2 > 1:
        with eng.Fori(1, n // 2) as t:
            for slot in range(2):
                body(2 * t + slot, slot, False)
    if n % 2 and n > 2:
        body(n - 1, 0, False)


def steps_ahead(eng, n, pre, body):
    def step(i, s, first):
        if not (type(i) is int and i == n - 1):
            pre(i + 1, 1 - s, type(i) is int and i == 0)
        body(i, s, first)
    pre(0, 0, True)
    for i in range(min(n, 2)):
        step(i, i, True)
    m = (n - 1) // 2
    if m > 1:
        with eng.Fori(1, m) as t:
            for slot in range(2):
                step(2 * t + slot, slot, False)
    for i in range(max(2, 2 * m), n):
        step(i, i % 2, False)


def linear(nc, x, w, col0, ncols, emit, spans=SPANS, x0=0):
    KT = x.shape[1]
    kind = emit[0]
    steps = ncols // (P if kind == "swiglu" else 2 * P)
    wr = w.rearrange("(k p) n -> p k n", p=P)
    lo = min(t0 for t0, _ in spans)
    with ExitStack() as ctx:
        sb, ps = memory(nc, ctx)
        staged = sb("staged", [P, KT, 256])
        ws = [Halves(sb, f"w{s}", [P, KT, 256]) for s in range(2)]
        out = [sb(f"out{s}", [P, TOK]) for s in range(2)] if kind != "residual" else None
        acc = [[ps(f"acc{s}{j}", [P, 512]) for j in range(2)] for s in range(4)]
        with stage(nc, "w_landed0", "w_landed1", "w_hi", "w_ready", "tile_ready", "tile_used", "silu_ready", "hidden_step",
                   "stored0", "stored1") as (
                block, w_landed0, w_landed1, w_hi, w_ready, tile_ready, tile_used, silu_ready, hidden_step, stored0,
                stored1):
            w_landed, stored = (w_landed0, w_landed1), (stored0, stored1)
            step_cols = P if kind == "swiglu" else 2 * P
            tile_cols = emit[2] if kind == "swiglu" else P

            @block.sync
            def _(sp):
                def load(i, s, first):
                    for j in range(2):
                        if not (first and s == 0):
                            sp.wait_ge(w_ready, 2 * i + (j - 1))
                        sp.dma_start(staged[:, :, j * P:(j + 1) * P],
                                     wr[:, :, bass.ds(i * step_cols + (col0 + j * tile_cols), P)]).then_inc(w_landed[j], 16)
                steps_of(sp, steps, load)

            @block.tensor
            def _(pe):
                def products(i, s, first):
                    for j in range(2):
                        pe.wait_ge(w_ready, 2 * i + (j + 1))
                        if not first:
                            pe.wait_ge(tile_used, 2 * i + (j - 3))
                        for b, (t0, tn) in enumerate(spans):
                            for k in range(KT):
                                cols, toks = slice(j * P, (j + 1) * P), slice(t0 - x0, t0 - x0 + tn)
                                mm = three_pass(nc, acc[2 * s + j][b][:, 0:tn],
                                                (ws[s].hi[:, k, cols], ws[s].lo[:, k, cols]),
                                                (x.hi[:, k, toks], x.lo[:, k, toks]), k == 0, k == KT - 1)
                        mm.then_inc(tile_ready, 1)
                steps_of(pe, steps, products)

            @block.vector
            def _(dve):
                def split_lo(i, s, first):
                    for j in range(2):
                        cols = slice(j * P, (j + 1) * P)
                        dve.wait_ge(w_hi, 2 * i + (j + 1))
                        nc.vector.tensor_tensor(ws[s].lo[:, :, cols], staged[:, :, cols], ws[s].hi[:, :, cols].bitcast(F32),
                                                ALU.subtract).then_inc(w_ready, 1)

                def finish(i, s, first):
                    if kind == "swiglu":
                        dve.wait_ge(tile_ready, 2 * i + 2)
                        dve.wait_ge(silu_ready, i + 1)
                        for b, (t0, tn) in enumerate(spans):
                            op = nc.vector.tensor_tensor(out[s][:, t0:t0 + tn], acc[2 * s + 1][b][:, 0:tn],
                                                         out[s][:, t0:t0 + tn], ALU.mult)
                        op.then_inc(tile_used, 2)
                        dve.wait_ge(tile_used, 2 * i + 2)
                        hi = emit[1].hi[:, bass.ds(i, 1), lo:TOK]
                        nc.vector.tensor_copy(hi, out[s][:, lo:TOK]).then_inc(hidden_step, 1)
                        dve.wait_ge(hidden_step, 2 * i + 1)
                        nc.vector.tensor_tensor(emit[1].lo[:, bass.ds(i, 1), lo:TOK], out[s][:, lo:TOK], hi.bitcast(F32),
                                                ALU.subtract).then_inc(hidden_step, 1)
                        return
                    for j in range(2):
                        dve.wait_ge(tile_ready, 2 * i + (j + 1))
                        if kind == "store" and not (first and s == 0):
                            dve.wait_ge(stored[j], 16 * i)
                        for b, (t0, tn) in enumerate(spans):
                            a = acc[2 * s + j][b][:, 0:tn]
                            if kind == "store":
                                op = nc.vector.tensor_copy(out[j][:, t0:t0 + tn], a)
                            else:
                                xt = emit[1][:, bass.ds(2 * i + j, 1), t0:t0 + tn]
                                op = nc.vector.scalar_tensor_tensor(
                                    out=xt, in0=a, scalar=emit[2][:, bass.ds(2 * i + j, 1), b], in1=xt,
                                    op0=ALU.mult, op1=ALU.add)
                        op.then_inc(tile_used, 1)
                steps_ahead(dve, steps, split_lo, finish)

            @block.scalar
            def _(act):
                def split_hi(i, s, first):
                    if not first:
                        act.wait_ge(tile_ready, 2 * i - 2)
                    for j in range(2):
                        cols = slice(j * P, (j + 1) * P)
                        act.wait_ge(w_landed[j], i * 16 + 16)
                        nc.scalar.copy(ws[s].hi[:, :, cols], staged[:, :, cols]).then_inc(w_hi, 1)

                def finish(i, s, first):
                    if kind == "store":
                        for j in range(2):
                            act.wait_ge(tile_used, 2 * i + (j + 1))
                            act.dma_start(emit[1][bass.ds(i * 256 + (emit[2] + j * P), P), lo:TOK],
                                          out[j][:, lo:TOK]).then_inc(stored[j], 16)
                    if kind == "swiglu":
                        act.wait_ge(tile_ready, 2 * i + 1)
                        if not first:
                            act.wait_ge(hidden_step, 2 * i - 2)
                        for b, (t0, tn) in enumerate(spans):
                            op = nc.scalar.activation(out[s][:, t0:t0 + tn], acc[2 * s][b][:, 0:tn], ACT.Silu)
                        op.then_inc(silu_ready, 1)
                steps_ahead(act, steps, split_hi, finish)
                if kind == "store":
                    for j in range(2):
                        act.wait_ge(stored[j], 16 * steps)


def swiglu(nc, xT, x, w_in, w_out, gates, spans):
    FH = FT // 2
    with ExitStack() as ctx:
        sb, _ = memory(nc, ctx)
        hidden = Halves(sb, "hidden", [P, FH, TOK])
        for half in range(2):
            f0 = half * FH * P
            linear(nc, x, w_in, f0, FH * P, ("swiglu", hidden, FF), spans)
            linear(nc, hidden, w_out[f0:f0 + FH * P, :], 0, D, ("residual", xT, gates), spans)

def load_tokens(nc, xT, ident, parts):
    jobs = [(src, t, c0 + t) for src, c0 in parts for t in range(0, src.shape[0], P)]
    with ExitStack() as ctx:
        sb, ps = memory(nc, ctx)
        rows = [sb(f"rows{i}", [P, D]) for i in range(len(jobs))]
        turned = [ps(f"turned{i}", [P, 4, P]) for i in range(4)]
        with stage(nc, "rows_ready", "turned_ready", "turned_used") as (
                block, rows_ready, turned_ready, turned_used):
            @block.sync
            def _(sp):
                for i, (src, t, _) in enumerate(jobs):
                    sp.dma_start(rows[i][:], src[t:t + P, :]).then_inc(rows_ready, 16)

            @block.tensor
            def _(pe):
                pe.wait_ge(rows_ready, 16 * len(jobs))
                for i in range(len(jobs)):
                    for g in range(2):
                        n = 2 * i + g
                        if n >= 4:
                            pe.wait_ge(turned_used, n - 3)
                        for k in range(4):
                            tr = nc.tensor.transpose(turned[n % 4][:, k, :], rows[i][:, (4 * g + k) * P:(4 * g + k + 1) * P],
                                                     ident[:])
                        tr.then_inc(turned_ready, 1)

            @block.vector
            def _(dve):
                for i, (_, _, c) in enumerate(jobs):
                    for g in range(2):
                        n = 2 * i + g
                        dve.wait_ge(turned_ready, n + 1)
                        nc.vector.tensor_copy(xT[:, 4 * g:4 * g + 4, c:c + P], turned[n % 4][:]).then_inc(turned_used, 1)


def columns(nc, ident, jobs):
    jobs = [(dst, vec, w) for dst, vec, *rest in jobs for w in [rest[0] if rest else P]]
    with ExitStack() as ctx:
        sb, ps = memory(nc, ctx)
        rows = [sb(f"rows{i}", [64, P]) for i in range(len(jobs))]
        turned = [ps(f"turned{i}", [P, 64]) for i in range(2)]
        with stage(nc, "rows_ready", "turned_ready", "turned_used") as (
                block, rows_ready, turned_ready, turned_used):
            @block.sync
            def _(sp):
                for i, (dst, vec, w) in enumerate(jobs):
                    sp.dma_start(rows[i][0:dst.shape[1], 0:w], vec.rearrange("(n p) -> n p", p=w)).then_inc(rows_ready, 16)

            @block.tensor
            def _(pe):
                pe.wait_ge(rows_ready, 16 * len(jobs))
                for i, (dst, _, w) in enumerate(jobs):
                    n = dst.shape[1]
                    if i >= 2:
                        pe.wait_ge(turned_used, i - 1)
                    nc.tensor.transpose(turned[i % 2][0:w, 0:n], rows[i][0:n, 0:w], ident[0:n, 0:n]).then_inc(turned_ready, 1)

            @block.vector
            def _(dve):
                for i, (dst, _, w) in enumerate(jobs):
                    n = dst.shape[1]
                    dve.wait_ge(turned_ready, i + 1)
                    nc.vector.tensor_copy(dst[0:w, :], turned[i % 2][0:w, 0:n]).then_inc(turned_used, 1)


def modulation_rows(nc, w, cond, rows):
    NC = 512
    steps = 6 * D // NC
    wr = w.rearrange("(k p) n -> p k n", p=P)
    with ExitStack() as ctx:
        sb, ps = memory(nc, ctx)
        wbuf = [sb(f"w{s}", [P, KD, NC]) for s in range(3)]
        row = [sb(f"row{s}", [2, NC]) for s in range(3)]
        acc = [ps(f"acc{s}", [2, NC]) for s in range(3)]
        with stage(nc, *(f"w_ready{s}" for s in range(3)), *(f"stored{s}" for s in range(3)), "row_ready", "row_copied") as (
                block, w0, w1, w2, st0, st1, st2, row_ready, row_copied):
            w_ready, stored = (w0, w1, w2), (st0, st1, st2)

            def turns(eng, body):
                for s in range(3):
                    body(0, s, True)
                with eng.Fori(1, steps // 3) as t:
                    for s in range(3):
                        body(t, s, False)

            @block.sync
            def _(sp):
                def load(t, s, first):
                    if not first:
                        sp.wait_ge(row_ready, 3 * t + (s - 2))
                    sp.dma_start(wbuf[s][:], wr[:, :, bass.ds((3 * t + s) * NC, NC)]).then_inc(w_ready[s], 16)
                turns(sp, load)

            @block.tensor
            def _(pe):
                def products(t, s, first):
                    pe.wait_ge(w_ready[s], 16 * t + 16)
                    if not first:
                        pe.wait_ge(row_copied, 3 * t + (s - 2))
                    for k in range(KD):
                        mm = nc.tensor.matmul(acc[s][:], cond[:, k, :], wbuf[s][:, k, :], start=(k == 0), stop=(k == KD - 1))
                    mm.then_inc(row_ready, 1)
                turns(pe, products)

            @block.vector
            def _(dve):
                def copy(t, s, first):
                    dve.wait_ge(row_ready, 3 * t + (s + 1))
                    if not first:
                        dve.wait_ge(stored[s], 16 * t)
                    nc.vector.tensor_copy(row[s][:], acc[s][:]).then_inc(row_copied, 1)
                turns(dve, copy)

            @block.gpsimd
            def _(pool):
                def store(t, s, first):
                    pool.wait_ge(row_copied, 3 * t + (s + 1))
                    pool.dma_start(rows[:, bass.ds((3 * t + s) * NC, NC)], row[s][:]).then_inc(stored[s], 16)
                turns(pool, store)
                for s in range(3):
                    pool.wait_ge(stored[s], 16 * steps // 3)


def modulation_columns(nc, ident, rows, b_cols, modT):
    with ExitStack() as ctx:
        sb, _ = memory(nc, ctx)
        cols = [sb(f"cols{b}", [P, 6 * KD]) for b in range(2)]
        columns(nc, ident, [(cols[b], rows[b]) for b in range(2)])
        with stage(nc, "added") as (block, added):
            @block.vector
            def _(dve):
                for b in range(2):
                    nc.vector.tensor_tensor(modT[:, :, b], cols[b][:], b_cols[:], ALU.add)


def rms_modulate(nc, xT, dst, ones, gain, modT=None, shift=0, scale=0, spans=SPANS, by_column=False):
    with ExitStack() as ctx:
        sb, ps = memory(nc, ctx)
        square = sb("square", [P, KD, TOK])
        rstd = sb("rstd", [P, TOK])
        std = sb("std", [P, TOK])
        eps = sb("eps", [P, 1])
        factor = sb("factor", [P, KD, 2])
        held = dst if modT is None else square
        total = [ps(f"total{b}", [P, 512]) for b in range(2)]
        with stage(nc, "squared_even", "squared_odd", "eps_set", "summed", "std_ready", "rstd_ready", "one_plus", "factor_ready",
                   "scaled", "hi_ready") as (block, squared_even, squared_odd, eps_set, summed, std_ready, rstd_ready,
                                             one_plus, factor_ready, scaled, hi_ready):
            def views(half, k, t0, tn):
                into, source = half[:, k, t0:t0 + tn], held[:, k, t0:t0 + tn]
                if by_column and t0 == CTX:
                    return into.rearrange("p (c r) -> p r c", c=64), source.rearrange("p (r c) -> p r c", c=64)
                return into, source

            @block.gpsimd
            def _(pool):
                nc.gpsimd.memset(eps[:], EPS).then_inc(eps_set, 1)

            @block.scalar
            def _(act):
                for b, (t0, tn) in enumerate(spans):
                    for k in range(0, KD, 2):
                        nc.scalar.activation(square[:, k, t0:t0 + tn], xT[:, k, t0:t0 + tn], ACT.Square
                                             ).then_inc(squared_even, 1)
                act.wait_ge(eps_set, 1)
                for b, (t0, tn) in enumerate(spans):
                    act.wait_ge(summed, b + 1)
                    nc.scalar.activation(std[:, t0:t0 + tn], total[b][:, 0:tn], ACT.Sqrt, bias=eps[:, 0:1],
                                         scale=1.0 / D).then_inc(std_ready, 1)
                if modT is not None:
                    n = 0
                    for b, (t0, tn) in enumerate(spans):
                        for k in range(KD):
                            n += 1
                            act.wait_ge(scaled, n)
                            into, source = views(dst.hi, k, t0, tn)
                            nc.scalar.activation(into, source, ACT.Identity, bias=modT[:, KD * shift + k, b:b + 1]
                                                 ).then_inc(hi_ready, 1)

            @block.tensor
            def _(pe):
                for b, (t0, tn) in enumerate(spans):
                    for k in range(KD):
                        pe.wait_ge(squared_odd if k % 2 else squared_even, (b * KD + k) // 2 + 1)
                        mm = nc.tensor.matmul(total[b][:, 0:tn], ones[:], square[:, k, t0:t0 + tn],
                                              start=(k == 0), stop=(k == KD - 1))
                    mm.then_inc(summed, 1)

            @block.vector
            def _(dve):
                def low_half(b, k, t0, tn):
                    dve.wait_ge(hi_ready, b * KD + k + 1)
                    (into, source), (hi, _) = views(dst.lo, k, t0, tn), views(dst.hi, k, t0, tn)
                    nc.vector.scalar_tensor_tensor(out=into, in0=source, scalar=modT[:, KD * shift + k, b:b + 1],
                                                   in1=hi.bitcast(F32), op0=ALU.add, op1=ALU.subtract)

                for t0, tn in spans:
                    for k in range(1, KD, 2):
                        nc.vector.tensor_tensor(square[:, k, t0:t0 + tn], xT[:, k, t0:t0 + tn], xT[:, k, t0:t0 + tn], ALU.mult
                                                ).then_inc(squared_odd, 1)
                if modT is not None:
                    nc.vector.tensor_scalar(factor[:], modT[:, KD * scale:KD * (scale + 1), :], 1.0, None, ALU.add
                                            ).then_inc(one_plus, 1)
                    dve.wait_ge(one_plus, 1)
                    for b in range(2):
                        f = nc.vector.tensor_tensor(factor[:, :, b], factor[:, :, b], gain[:], ALU.mult)
                else:
                    for b in range(2):
                        f = nc.vector.tensor_copy(factor[:, :, b], gain[:])
                f.then_inc(factor_ready, 1)
                dve.wait_ge(factor_ready, 1)
                for b, (t0, tn) in enumerate(spans):
                    dve.wait_ge(std_ready, b + 1)
                    nc.vector.reciprocal(rstd[:, t0:t0 + tn], std[:, t0:t0 + tn]).then_inc(rstd_ready, 1)
                    dve.wait_ge(rstd_ready, b + 1)
                    for k in range(KD):
                        nc.vector.scalar_tensor_tensor(
                            out=held[:, k, t0:t0 + tn], in0=xT[:, k, t0:t0 + tn], scalar=factor[:, k, b:b + 1],
                            in1=rstd[:, t0:t0 + tn], op0=ALU.mult, op1=ALU.mult).then_inc(scaled, 1)
                        if modT is not None and k:
                            low_half(b, k - 1, t0, tn)
                    if modT is not None:
                        low_half(b, KD - 1, t0, tn)


def load_columns(nc, h, dram, lo=0):
    KT = h.shape[1]
    with ExitStack() as ctx:
        sb, _ = memory(nc, ctx)
        staged = sb("staged", [P, KT, TOK])
        with stage(nc, "hi_ready", *(f"loaded{k}" for k in range(0, KT, 2))) as (block, hi_ready, *loaded):
            @block.sync
            def _(sp):
                for k in range(0, KT, 2):
                    sp.dma_start(staged[:, k:k + 2, lo:TOK],
                                 dram[k * P:(k + 2) * P, lo:TOK].rearrange("(k p) t -> p k t", p=P)).then_inc(loaded[k // 2], 16)

            @block.scalar
            def _(act):
                for k in range(0, KT, 2):
                    act.wait_ge(loaded[k // 2], 16)
                    nc.scalar.copy(h.hi[:, k:k + 2, lo:TOK], staged[:, k:k + 2, lo:TOK]).then_inc(hi_ready, 1)

            @block.vector
            def _(dve):
                for k in range(0, KT, 2):
                    dve.wait_ge(hi_ready, k // 2 + 1)
                    nc.vector.tensor_tensor(h.lo[:, k:k + 2, lo:TOK], staged[:, k:k + 2, lo:TOK],
                                            h.hi[:, k:k + 2, lo:TOK].bitcast(F32), ALU.subtract)


def store_tokens(nc, xT, ident, out):
    with ExitStack() as ctx:
        sb, ps = memory(nc, ctx)
        rows = [sb(f"rows{i}", [P, D]) for i in range(LAT // P)]
        turned = [ps(f"turned{i}", [P, 4, P]) for i in range(4)]
        with stage(nc, "turned_ready", "turned_used", "stored") as (block, turned_ready, turned_used, stored):
            @block.tensor
            def _(pe):
                for n in range(2 * LAT // P):
                    if n >= 4:
                        pe.wait_ge(turned_used, n - 3)
                    c = CTX + n // 2 * P
                    for k in range(4):
                        tr = nc.tensor.transpose(turned[n % 4][:, k, :], xT[:, n % 2 * 4 + k, c:c + P], ident[:])
                    tr.then_inc(turned_ready, 1)

            @block.vector
            def _(dve):
                for n in range(2 * LAT // P):
                    dve.wait_ge(turned_ready, n + 1)
                    nc.vector.tensor_copy(rows[n // 2][:, n % 2 * 512:n % 2 * 512 + 512], turned[n % 4][:]
                                          ).then_inc(turned_used, 1)

            @block.sync
            def _(sp):
                for i in range(LAT // P):
                    sp.wait_ge(turned_used, 2 * i + 2)
                    sp.dma_start(out[i * P:(i + 1) * P, :], rows[i][:]).then_inc(stored, 16)
                sp.wait_ge(stored, 16 * LAT // P)

def rope(nc, src, dst, row0, tiles, consts, gains=None):
    block_ones, cos, sin = consts
    with ExitStack() as ctx:
        sb, ps = memory(nc, ctx)
        plain = [sb(f"plain{s}", [P, TOK]) for s in range(2)]
        swapped = [sb(f"swapped{s}", [P, TOK]) for s in range(2)]
        square = [sb(f"square{s}", [P, TOK]) for s in range(2)]
        std = [sb(f"std{s}", [P, TOK]) for s in range(2)]
        rstd = [sb(f"rstd{s}", [P, TOK]) for s in range(2)]
        turned = [sb(f"turned{s}", [P, TOK]) for s in range(2)]
        other = [sb(f"other{s}", [P, TOK]) for s in range(2)]
        eps = sb("eps", [P, 1])
        total = [ps(f"total{s}", [P, 1024]) for s in range(2)]
        with stage(nc, "loaded0", "loaded1", "eps_set", "squared", "summed", "std_ready", "rstd_ready", "parts",
                   "joined", "ready", "stored0", "stored1") as (
                block, loaded0, loaded1, eps_set, squared, summed, std_ready, rstd_ready, parts, joined, ready,
                stored0, stored1):
            loaded, stored = (loaded0, loaded1), (stored0, stored1)

            @block.sync
            def _(sp):
                def load(i, s, first):
                    if not first:
                        sp.wait_ge(ready, i - 1)
                    sp.dma_start(plain[s][:], src[bass.ds(i * P + row0, P), :]).then_inc(loaded[s], 16)
                    for h in range(4):
                        sp.dma_start(swapped[s][32 * h:32 * h + 32, :],
                                     src[bass.ds(i * P + (row0 + 32 * (h ^ 1)), 32), :]).then_inc(loaded[s], 16)
                steps_of(sp, tiles, load)

            @block.gpsimd
            def _(pool):
                nc.gpsimd.memset(eps[:], EPS).then_inc(eps_set, 1)

            @block.scalar
            def _(act):
                def norm(i, s, first):
                    act.wait_ge(loaded[s], 80 if first else (i - s) * 40 + 80)
                    if not first:
                        act.wait_ge(summed, i - 1)
                    nc.scalar.activation(square[s][:], plain[s][:], ACT.Square).then_inc(squared, 1)
                    act.wait_ge(summed, i + 1)
                    nc.scalar.activation(std[s][:], total[s][:, 0:TOK], ACT.Sqrt, bias=eps[:, 0:1], scale=1.0 / HD
                                         ).then_inc(std_ready, 1)
                if gains is not None:
                    act.wait_ge(eps_set, 1)
                    steps_of(act, tiles, norm)

            @block.tensor
            def _(pe):
                def norm(i, s, first):
                    pe.wait_ge(squared, i + 1)
                    if not first:
                        pe.wait_ge(std_ready, i - 1)
                    for t0, tn in ((0, 512), (512, 256)):
                        mm = nc.tensor.matmul(total[s][:, t0:t0 + tn], block_ones[:], square[s][:, t0:t0 + tn],
                                              start=True, stop=True)
                    mm.then_inc(summed, 1)
                if gains is not None:
                    steps_of(pe, tiles, norm)

            @block.vector
            def _(dve):
                def rotate(i, s, first):
                    dve.wait_ge(loaded[s], 80 if first else (i - s) * 40 + 80)
                    if not first:
                        dve.wait_ge(stored[s], (i - s) * 8)
                    for n, (t, table, into) in enumerate(((plain[s], cos, turned[s]), (swapped[s], sin, other[s]))):
                        if gains is not None:
                            op = nc.vector.scalar_tensor_tensor(out=into[:], in0=t[:], scalar=gains[:, bass.ds(i, 1), n],
                                                                in1=table[:], op0=ALU.mult, op1=ALU.mult)
                        else:
                            op = nc.vector.tensor_tensor(into[:], t[:], table[:], ALU.mult)
                        op.then_inc(parts, 1)
                    dve.wait_ge(parts, 2 * i + 2)
                    op = nc.vector.tensor_tensor(turned[s][:], turned[s][:], other[s][:], ALU.add)
                    if gains is not None:
                        op.then_inc(joined, 1)
                        dve.wait_ge(std_ready, i + 1)
                        nc.vector.reciprocal(rstd[s][:], std[s][:]).then_inc(rstd_ready, 1)
                        dve.wait_ge(joined, i + 1)
                        dve.wait_ge(rstd_ready, i + 1)
                        op = nc.vector.tensor_tensor(turned[s][:], turned[s][:], rstd[s][:], ALU.mult)
                    op.then_inc(ready, 1)
                steps_of(dve, tiles, rotate)

            @block.gpsimd
            def _(pool):
                def store(i, s, first):
                    pool.wait_ge(ready, i + 1)
                    pool.dma_start(dst[bass.ds(i * P + row0, P), :], turned[s][:]).then_inc(stored[s], 16)
                steps_of(pool, tiles, store)
                for s in range(2):
                    pool.wait_ge(stored[s], 16 * ((tiles + 1 - s) // 2))


MOD_STEPS = (1, 3)


def heads_of(eng, heads, body):
    for h in range(2):
        body(h, h, False)
    with eng.Fori(1, heads // 2 - 1) as t:
        for s in range(2):
            body(2 * t + s, s, False)
    for s in range(2):
        body(heads - 2 + s, s, s == 1)


def attention(nc, ident, heads, qk, q_row, k_row, per_kv, v, v_row, mix, mix_row, queries, scale,
              mask=None, sinks=None, rpb=None, q_from=0, beside=None):
    QT = len(queries)
    q_min = min(c for c, _, _ in queries)
    MN = 6 * D // (2 * heads)
    with ExitStack() as ctx:
        sb, ps = memory(nc, ctx)
        qT = [sb(f"qT{s}", [HD, TOK]) for s in range(2)]
        kT = [sb(f"kT{s}", [HD, TOK]) for s in range(2)]
        vT = [sb(f"vT{s}", [HD, TOK]) for s in range(2)]
        vrow = [sb(f"vrow{s}", [P, 6, HD]) for s in range(2)]
        scores = [sb(f"scores{s}", [P, TOK]) for s in range(2)]
        probs = [sb(f"probs{s}", [P, TOK]) for s in range(2)]
        probsT = [sb(f"probsT{s}", [P, 6, P]) for s in range(2)]
        rows = [sb(f"rows{s}", [P, HD]) for s in range(2)]
        outT = [sb(f"outT{s}", [HD, TOK]) for s in range(2)]
        stats = [[sb(f"{n}{s}", [P, 1]) for s in range(2)] for n in ("top", "ntop", "esink", "sum", "den", "rden")]
        top, ntop, esink, total, den, rden = stats
        hankel = [sb(f"hankel{s}", [P, 14, HD]) for s in range(2)] if rpb else None
        raw = [ps(f"raw{s}", [P, 1024]) for s in range(2)]
        probsT_ps = ps("probsT_ps", [P, 1024])
        turn_ps = ps("turn_ps", [P, 512])
        v_ps, outT_ps = turn_ps[:, 0:6 * HD].rearrange("p (k d) -> p k d", d=HD), turn_ps[0:HD, 6 * HD:6 * HD + P]
        sum_ps = ps("sum_ps", [P, 512])
        out_ps = sum_ps[:, 0:HD]
        mod_ps = sum_ps[0:2, HD:HD + MN]
        if beside:
            w_mod, cond, mod_rows = beside
            w_mod = w_mod.rearrange("(k p) n -> p k n", p=P)
            wbuf = [sb(f"wmod{j}", [P, KD, MN]) for j in range(2)]
            mod_row = [sb(f"mod_row{j}", [2, MN]) for j in range(2)]
        with stage(nc, "loaded0", "loaded1", "w_loaded0", "w_loaded1", "mod_copied", "mod_stored0", "mod_stored1", "v_turned", "v_ready", "raw_ready", "masked",
                   "top_ready", "ntop_ready", "exp_ready", "den_ready", "rden_ready", "probsT_ready", "probsT_copied",
                   "out_ready", "passed", "row_ready", "outT_ready", "out_copied", "stored0", "stored1") as (
                block, loaded0, loaded1, w_loaded0, w_loaded1, mod_copied, mod_stored0, mod_stored1, v_turned, v_ready, raw_ready, masked,
                top_ready, ntop_ready, exp_ready, den_ready, rden_ready, probsT_ready, probsT_copied,
                out_ready, passed, row_ready, outT_ready, out_copied, stored0, stored1):
            loaded, w_loaded, stored = (loaded0, loaded1), (w_loaded0, w_loaded1), (stored0, stored1)
            mod_stored = (mod_stored0, mod_stored1)
            full = 16 * (5 if rpb else 3)
            n_masked = sum(m is not None for _, _, m in queries)

            def slot_full(h, s, amount):
                return (h - s) * (amount // 2) + amount

            def after(eng, sem, count):
                if type(count) is not int or count > 0:
                    eng.wait_ge(sem, count)

            def tile_at(h, s, last, i):
                if (last and i >= QT) or (type(h) is int and h == 0 and i < 0):
                    return None
                return h + i // QT, s if 0 <= i < QT else 1 - s, i % QT

            @block.sync
            def _(sp):
                def load(h, s, last):
                    after(sp, raw_ready, (h - 1) * QT)
                    kv = h if per_kv == 1 else h // per_kv
                    sp.dma_start(qT[s][:, q_from:TOK], qk[bass.ds(h * HD + q_row, HD), q_from:TOK]).then_inc(loaded[s], 16)
                    sp.dma_start(kT[s][:], qk[bass.ds(kv * HD + k_row, HD), :]).then_inc(loaded[s], 16)
                    sp.dma_start(vT[s][:], v[bass.ds(kv * HD + v_row, HD), :]).then_inc(loaded[s], 16)
                    if rpb:
                        for r in range(2):
                            sp.dma_start(hankel[s][64 * r:64 * r + 64, :, :],
                                         bass.AP(rpb[0].tensor, h * (15 * 127) + (1 - r) * 127,
                                                 [[1, 64], [127, 14], [1, 64]])).then_inc(loaded[s], 16)
                    for j in range(2 if beside else 0):
                        after(sp, mod_copied, 2 * h + (j - 1))
                        sp.dma_start(wbuf[j][:], w_mod[:, :, bass.ds(h * (2 * MN) + j * MN, MN)]).then_inc(w_loaded[j], 16)
                heads_of(sp, heads, load)

            @block.tensor
            def _(pe):
                def score(h, s, q):
                    c, nk, m = queries[q]
                    n, b = h * QT + q, raw[q % 2]
                    if q == 0:
                        pe.wait_ge(loaded[s], slot_full(h, s, full))
                    after(pe, exp_ready, n - 1)
                    for t0, tn in ((0, min(nk, 512)), (512, nk - 512)):
                        if tn > 0:
                            mm = nc.tensor.matmul(b[:, t0:t0 + tn], qT[s][:, c:c + P], kT[s][:, t0:t0 + tn],
                                                  start=True, stop=not rpb)
                    if rpb:
                        w = hankel[s][:, 6 - 2 * q:14 - 2 * q, :].rearrange("p a b -> p (a b)")
                        nc.tensor.matmul(b[:, 256:512], rpb[1][:], w[:, 0:256], start=False, stop=True)
                        mm = nc.tensor.matmul(b[:, 512:768], rpb[1][:], w[:, 256:512], start=False, stop=True)
                    mm.then_inc(raw_ready, 1)

                def turn(h, q):
                    _, nk, _ = queries[q]
                    n, p = h * QT + q, q % 2
                    pe.wait_ge(exp_ready, n + 1)
                    after(pe, probsT_copied, n)
                    for k in range(nk // P):
                        tr = nc.tensor.transpose(probsT_ps[:, k * P:(k + 1) * P], probs[p][:, k * P:(k + 1) * P], ident[:])
                    tr.then_inc(probsT_ready, 1)

                def modulate(h, j):
                    pe.wait_ge(w_loaded[j], h * 16 + 16)
                    for k in range(KD):
                        nc.tensor.matmul(mod_ps, cond[:, k, :], wbuf[j][:, k, :], start=(k == 0), stop=(k == KD - 1))

                def values(h, s, q):
                    _, nk, _ = queries[q]
                    pe.wait_ge(probsT_copied, h * QT + (q + 1))
                    for k in range(nk // P):
                        mm = nc.tensor.matmul(out_ps, probsT[q % 2][:, k, :], vrow[s][:, k, :],
                                              start=(k == 0), stop=(k == nk // P - 1))
                    mm.then_inc(out_ready, 1)

                def turn_out(h, s, q):
                    n = h * QT + q
                    pe.wait_ge(row_ready, n + 1)
                    after(pe, out_copied, n)
                    pe.sem_inc(passed, 1)
                    nc.tensor.transpose(outT_ps, rows[q % 2][:], ident[:]).then_inc(outT_ready, 1)

                def head(h, s, last):
                    if type(h) is int and h == 0:
                        score(h, s, 0)
                    after(pe, out_copied, h * QT - 2)
                    after(pe, v_ready, h)
                    pe.sem_inc(passed, 1)
                    for k in range(6):
                        tr = nc.tensor.transpose(v_ps[:, k, :], vT[s][:, k * P:(k + 1) * P], ident[0:HD, 0:HD])
                    tr.then_inc(v_turned, 1)
                    for q in range(QT):
                        ahead, behind, turned = (tile_at(h, s, last, q + i) for i in (1, -1, -2))
                        if ahead:
                            score(*ahead)
                        turn(h, q)
                        after(pe, row_ready, h * QT + (q - 1))
                        if beside and q in MOD_STEPS:
                            modulate(h, MOD_STEPS.index(q))
                        if q == 0:
                            pe.wait_ge(v_ready, h + 1)
                        if behind:
                            values(*behind)
                        if turned:
                            turn_out(*turned)
                    if last:
                        pe.wait_ge(row_ready, heads * QT - 1)
                        values(h, s, QT - 1)
                        turn_out(h, s, QT - 2)
                        turn_out(h, s, QT - 1)
                heads_of(pe, heads, head)

            @block.vector
            def _(dve):
                def softmax_top(h, s, q):
                    c, nk, m = queries[q]
                    n, p = h * QT + q, q % 2
                    dve.wait_ge(raw_ready, n + 1)
                    after(dve, exp_ready, n - 1)
                    src = raw[p]
                    if m is not None:
                        nc.vector.tensor_tensor(scores[p][:, 0:nk], raw[p][:, 0:nk], mask[:, m, 0:nk], ALU.add
                                                ).then_inc(masked, 1)
                        dve.wait_ge(masked, h * n_masked + sum(x[2] is not None for x in queries[:q + 1]))
                        src = scores[p]
                    nc.vector.tensor_reduce(top[p][:], src[:, 0:nk], AX, ALU.max).then_inc(top_ready, 1)
                    dve.wait_ge(top_ready, n + 1)
                    if sinks is not None:
                        nc.vector.tensor_scalar(ntop[p][:], top[p][:], -scale, sinks[:, bass.ds(h, 1)], ALU.mult, ALU.min
                                                ).then_inc(ntop_ready, 1)
                    else:
                        nc.vector.tensor_scalar(ntop[p][:], top[p][:], -scale, None, ALU.mult).then_inc(ntop_ready, 1)

                def reciprocal(h, s, q):
                    n, p = h * QT + q, q % 2
                    dve.wait_ge(exp_ready, n + 1)
                    src = total[p]
                    if sinks is not None:
                        nc.vector.tensor_tensor(den[p][:], total[p][:], esink[p][:], ALU.add).then_inc(den_ready, 1)
                        dve.wait_ge(den_ready, n + 1)
                        src = den[p]
                    nc.vector.reciprocal(rden[p][:], src[:]).then_inc(rden_ready, 1)

                def normalise(h, s, q):
                    n, p = h * QT + q, q % 2
                    dve.wait_ge(out_ready, n + 1)
                    dve.wait_ge(rden_ready, n + 1)
                    after(dve, outT_ready, n - 1)
                    nc.vector.tensor_scalar(rows[p][:], out_ps, rden[p][:, 0:1], None, ALU.mult).then_inc(row_ready, 1)

                def output(h, s, q):
                    c, _, _ = queries[q]
                    n = h * QT + q
                    dve.wait_ge(outT_ready, n + 1)
                    if q == 0 and not (type(h) is int and h < 2):
                        dve.wait_ge(stored[s], (h - s) * 8)
                    nc.vector.tensor_copy(outT[s][:, c:c + P], outT_ps).then_inc(out_copied, 1)

                def head(h, s, last):
                    if type(h) is int and h == 0:
                        softmax_top(h, s, 0)
                    dve.wait_ge(v_turned, h + 1)
                    nc.vector.tensor_copy(vrow[s][:], v_ps).then_inc(v_ready, 1)
                    for q in range(QT):
                        ahead, behind, turned = (tile_at(h, s, last, q + i) for i in (1, -1, -2))
                        if ahead:
                            softmax_top(*ahead)
                        if beside and q in MOD_STEPS:
                            modulated(h, q, MOD_STEPS.index(q))
                        if behind:
                            normalise(*behind)
                        reciprocal(h, s, q)
                        if turned:
                            output(*turned)
                    if last:
                        normalise(h, s, QT - 1)
                        output(h, s, QT - 2)
                        output(h, s, QT - 1)

                def modulated(h, q, j):
                    dve.wait_ge(out_ready, h * QT + q)
                    after(dve, mod_stored[j], h * 16)
                    nc.vector.tensor_copy(mod_row[j][:], mod_ps).then_inc(mod_copied, 1)
                heads_of(dve, heads, head)

            @block.scalar
            def _(act):
                def exponent(h, s, q):
                    _, nk, m = queries[q]
                    n, p = h * QT + q, q % 2
                    act.wait_ge(ntop_ready, n + 1)
                    after(act, probsT_ready, n - 1)
                    after(act, rden_ready, n - 1)
                    src = raw[p] if m is None else scores[p]
                    op = nc.scalar.activation(probs[p][:, 0:nk], src[:, 0:nk], ACT.Exp, bias=ntop[p][:, 0:1],
                                              scale=scale, accum_out=total[p][:, 0:1])
                    if sinks is not None:
                        op = nc.scalar.activation(esink[p][:], sinks[:, bass.ds(h, 1)], ACT.Exp,
                                                  bias=ntop[p][:, 0:1], scale=-1.0)
                    op.then_inc(exp_ready, 1)

                def head(h, s, last):
                    if type(h) is int and h == 0:
                        exponent(h, s, 0)
                    for q in range(QT):
                        ahead = tile_at(h, s, last, q + 1)
                        _, nk, _ = queries[q]
                        n, p = h * QT + q, q % 2
                        act.wait_ge(probsT_ready, n + 1)
                        after(act, out_ready, n - 1)
                        nc.scalar.copy(probsT[p][:, 0:nk // P, :], probsT_ps[:, 0:nk]).then_inc(probsT_copied, 1)
                        if ahead:
                            exponent(*ahead)
                heads_of(act, heads, head)

            @block.gpsimd
            def _(pool):
                def store(h, s, last):
                    for j in range(2 if beside else 0):
                        pool.wait_ge(mod_copied, 2 * h + (j + 1))
                        pool.dma_start(mod_rows[:, bass.ds(h * (2 * MN) + j * MN, MN)], mod_row[j][:]).then_inc(mod_stored[j], 16)
                    pool.wait_ge(out_copied, (h + 1) * QT)
                    pool.dma_start(mix[bass.ds(h * HD + mix_row, HD), q_min:TOK], outT[s][:, q_min:TOK]
                                   ).then_inc(stored[s], 16)
                heads_of(pool, heads, store)
                for s in range(2):
                    pool.wait_ge(stored[s], 8 * heads)
                    if beside:
                        pool.wait_ge(mod_stored[s], 16 * heads)


QUERIES_LAT = [(CTX + P * i, TOK, None) for i in range(LAT // P)]
QUERIES_CTX = [(P * i, CTX, None) for i in range(CTX // P)]
QUERIES_MASKED = [(CTX + P * i, TOK, i) for i in range(LAT // P)]


def even_mixer(nc, ident, proj, rot, mix, consts, gains, window, sinks, beside=(None, None)):
    rope(nc, proj, rot, 0, 5, consts, gains)
    rope(nc, proj, rot, 768, 5, consts)
    attention(nc, ident, 8, rot, 0, 512, 4, proj, 640, mix, 0, QUERIES_CTX + QUERIES_LAT, HD ** -0.5,
              beside=beside[0])
    attention(nc, ident, 8, rot, 768, 1280, 4, proj, 1408, mix, 512, QUERIES_CTX + QUERIES_MASKED, HD ** -0.5,
              mask=window, sinks=sinks, beside=beside[1])

class Chain:

    def __init__(self, eng, sem, per):
        self.eng, self.sem, self.per, self.k, self.i = eng, sem, per, 0, 0

    def start(self, i):
        assert self.k in (0, self.per), (self.k, self.per)
        self.i, self.k = i, 0

    def __call__(self, ins):
        self.k += 1
        ins.then_inc(self.sem, 1)
        self.eng.wait_ge(self.sem, self.i * self.per + self.k)


RW = 512
CH = 64
NCH = TOK // CH


def shift_mix(nc, proj, row0, tiles, mu, mixed):
    W = TOK + 4
    with ExitStack() as ctx:
        sb, _ = memory(nc, ctx)
        z = [sb(f"z{s}", [P, W]) for s in range(2)]
        around = [sb(f"around{s}", [P, W - 2]) for s in range(2)]
        out = [sb(f"out{s}", [P, W - 2]) for s in range(2)]
        with stage(nc, "zeroed", "loaded0", "loaded1", "added", "centred", "ready", "stored0", "stored1") as (
                block, zeroed, loaded0, loaded1, added, centred, ready, stored0, stored1):
            loaded, stored = (loaded0, loaded1), (stored0, stored1)

            @block.sync
            def _(sp):
                sp.wait_ge(zeroed, 2)
                def load(i, s, first):
                    if not first:
                        sp.wait_ge(ready, i - 1)
                    rows = proj[bass.ds(i * P + row0, P), :]
                    sp.dma_start(z[s][:, 1:1 + CTX], rows[:, 0:CTX]).then_inc(loaded[s], 16)
                    sp.dma_start(z[s][:, CTX + 3:CTX + 3 + LAT], rows[:, CTX:TOK]).then_inc(loaded[s], 16)
                steps_of(sp, tiles, load)

            @block.gpsimd
            def _(pool):
                for s in range(2):
                    nc.gpsimd.memset(z[s][:], 0.0).then_inc(zeroed, 1)

                def store(i, s, first):
                    pool.wait_ge(ready, i + 1)
                    rows = mixed[bass.ds(i * P, P), :]
                    pool.dma_start(rows[:, 0:CTX], out[s][:, 0:CTX]).then_inc(stored[s], 16)
                    pool.dma_start(rows[:, CTX:TOK], out[s][:, CTX + 2:CTX + 2 + LAT]).then_inc(stored[s], 16)
                steps_of(pool, tiles, store)
                for s in range(2):
                    pool.wait_ge(stored[s], 32 * ((tiles + 1 - s) // 2))

            @block.vector
            def _(dve):
                def step(i, s, first):
                    dve.wait_ge(loaded[s], 32 if first else (i - s) * 16 + 32)
                    nc.vector.tensor_tensor(around[s][:], z[s][:, 0:W - 2], z[s][:, 2:W], ALU.add).then_inc(added, 1)
                    dve.wait_ge(added, i + 1)
                    nc.vector.scalar_tensor_tensor(out=around[s][:], in0=around[s][:], scalar=0.5, in1=z[s][:, 1:W - 1],
                                                   op0=ALU.mult, op1=ALU.subtract).then_inc(centred, 1)
                    dve.wait_ge(centred, i + 1)
                    if not first:
                        dve.wait_ge(stored[s], (i - s) * 16)
                    nc.vector.scalar_tensor_tensor(out=out[s][:], in0=around[s][:], scalar=mu[:, bass.ds(i, 1)],
                                                   in1=z[s][:, 1:W - 1], op0=ALU.mult, op1=ALU.add).then_inc(ready, 1)
                steps_of(dve, tiles, step)


def rwkv_features(nc, mixed, w2, a2, g2, cols, block_ones, reset, arrays, dec, bonus, gate):
    (kk_c, ka_c, rk_c, w0_c, a0_c) = cols
    with ExitStack() as ctx:
        sb, ps = memory(nc, ctx)
        tw, ad, sg = sb("tanh_w", [HD, TOK]), sb("ad", [HD, TOK]), sb("sig_g", [P, TOK])
        r, k, v = ([sb(f"{n}{s}", [P, TOK]) for s in range(2)] for n in "rkv")
        ws, asl = ([sb(f"{n}{s}", [HD, 2, P]) for s in range(2)] for n in ("w2", "a2"))
        gs = [sb(f"g2{s}", [P, P]) for s in range(2)]
        kk, sq, nrm, rr = sb("kk", [P, TOK]), sb("sq", [P, TOK]), sb("nrm", [P, TOK]), sb("rr", [P, TOK])
        ksum, bon, gat = sb("ksum", [P, TOK]), sb("bon", [P, TOK]), sb("gat", [P, TOK])
        lw = [sb(f"lw{d}", [P, TOK]) for d in range(2)]
        a = [sb(f"a{d}", [P, TOK]) for d in range(2)]
        c, e, kd = sb("c", [P, TOK]), sb("e", [P, TOK]), sb("kd", [P, TOK])
        up, down, excl = (sb(n, [P, TOK]) for n in ("exp_c", "exp_minus_c", "exp_e"))
        outs = [sb(f"o{n}", [P, TOK]) for n in range(4)]
        wc = sb("wc", [P, NCH])
        bias_now = sb("bias_now", [P, 4])
        X, Y, Z = (ps(n, [P, 1024]) for n in ("X", "Y", "Z"))
        parts = ((0, 512), (512, 256))
        with stage(nc, "lora_loaded", "lora_ready", "loaded0", "loaded1", "zw_ready", "za_ready", "sig_ready", "kk_squared",
                   "kk_summed", "kk_root", "feature_step", "sums_ready", "exps_ready", "four_ready", "stored",
                   "tail_ready", "bonus_in", "bonus_summed", "gate_ready", "tail_stored") as (
                block, lora_loaded, lora_ready, loaded0, loaded1, zw_ready, za_ready, sig_ready, kk_squared, kk_summed,
                kk_root, feature_step, sums_ready, exps_ready, four_ready, stored, tail_ready, bonus_in,
                bonus_summed, gate_ready, tail_stored):
            TILES = RW // P
            loaded = (loaded0, loaded1)

            def tiles(eng, body):
                steps_of(eng, TILES, lambda m, s, fresh: body(m, s, fresh and s == 0))

            def arrived(eng, m, s):
                eng.wait_ge(loaded[s], (m - s) * 48 + 96)

            def last_of_chunk(t, d):
                return t[:].rearrange("p (n c) -> p n c", c=CH)[:, :, (CH - 1) * (1 - d)]

            @block.sync
            def _(sp):
                sp.dma_start(tw[:], mixed[3 * RW:3 * RW + 64, :]).then_inc(lora_loaded, 16)
                sp.dma_start(ad[:], mixed[3 * RW + 64:3 * RW + 128, :]).then_inc(lora_loaded, 16)
                sp.dma_start(sg[:], mixed[3 * RW + 128:3 * RW + 256, :]).then_inc(lora_loaded, 16)

                def load(m, s, first):
                    if not (type(m) is int and m < 2):
                        sp.wait_ge(tail_ready, m - 1)
                        sp.wait_ge(gate_ready, m - 1)
                    for n, t in enumerate((r[s], k[s], v[s])):
                        sp.dma_start(t[:], mixed[bass.ds(m * P + n * RW, P), :]).then_inc(loaded[s], 16)
                    sp.dma_start(ws[s][:], w2.rearrange("d l n -> l d n")[:, :, bass.ds(m * P, P)]).then_inc(loaded[s], 16)
                    sp.dma_start(asl[s][:], a2.rearrange("d l n -> l d n")[:, :, bass.ds(m * P, P)]).then_inc(loaded[s], 16)
                    sp.dma_start(gs[s][:], g2[:, bass.ds(m * P, P)]).then_inc(loaded[s], 16)
                tiles(sp, load)

            @block.scalar
            def _(act):
                act.wait_ge(lora_loaded, 48)
                nc.scalar.activation(tw[:], tw[:], ACT.Tanh).then_inc(lora_ready, 1)
                nc.scalar.activation(sg[:], sg[:], ACT.Sigmoid).then_inc(lora_ready, 1)

                def step(m, s, first):
                    act.wait_ge(sums_ready, 3 * m + 1)
                    nc.scalar.activation(sq[:], kk[:], ACT.Square).then_inc(kk_squared, 1)
                    act.wait_ge(kk_summed, m + 1)
                    nc.scalar.activation(nrm[:], Z[:, 0:TOK], ACT.Sqrt).then_inc(kk_root, 1)
                    for d in range(2):
                        act.wait_ge(zw_ready, 2 * m + d + 1)
                        nc.scalar.activation(lw[d][:], X[:, 0:TOK], ACT.Sigmoid, bias=bias_now[:, 2 * d:2 * d + 1])
                        act.wait_ge(za_ready, 2 * m + d + 1)
                        nc.scalar.activation(a[d][:], Y[:, 0:TOK], ACT.Sigmoid, bias=bias_now[:, 2 * d + 1:2 * d + 2]
                                             ).then_inc(sig_ready, 1)
                    for d in range(2):
                        act.wait_ge(sums_ready, 3 * m + (2 + d))
                        nc.scalar.activation(up[:], c[:], ACT.Exp)
                        nc.scalar.activation(down[:], c[:], ACT.Exp, scale=-1.0)
                        nc.scalar.activation(excl[:], e[:], ACT.Exp)
                        if not (first and d == 0):
                            act.wait_ge(stored, 80 * (2 * m + d))
                        nc.scalar.activation(wc[:], last_of_chunk(c, d), ACT.Exp).then_inc(exps_ready, 1)
                tiles(act, step)

            @block.tensor
            def _(pe):
                pe.wait_ge(lora_ready, 2)

                def step(m, s, first):
                    arrived(pe, m, s)
                    for d in range(2):
                        if not (first and d == 0):
                            pe.wait_ge(sig_ready, 2 * m + d)
                        if d == 0 and not first:
                            pe.wait_ge(tail_ready, m)
                        for t0, tn in parts:
                            mm = nc.tensor.matmul(X[:, t0:t0 + tn], ws[s][:, d, :], tw[:, t0:t0 + tn], start=True, stop=True)
                        mm.then_inc(zw_ready, 1)
                        for t0, tn in parts:
                            mm = nc.tensor.matmul(Y[:, t0:t0 + tn], asl[s][:, d, :], ad[:, t0:t0 + tn], start=True, stop=True)
                        mm.then_inc(za_ready, 1)
                        if d == 0:
                            pe.wait_ge(kk_squared, m + 1)
                            for t0, tn in parts:
                                mm = nc.tensor.matmul(Z[:, t0:t0 + tn], block_ones[:], sq[:, t0:t0 + tn], start=True, stop=True)
                            mm.then_inc(kk_summed, 1)
                    pe.wait_ge(sig_ready, 2 * m + 2)
                    for t0, tn in parts:
                        mm = nc.tensor.matmul(Y[:, t0:t0 + tn], gs[s][:], sg[:, t0:t0 + tn], start=True, stop=True)
                    mm.then_inc(gate_ready, 1)
                    pe.wait_ge(bonus_in, m + 1)
                    for t0, tn in parts:
                        mm = nc.tensor.matmul(X[:, t0:t0 + tn], block_ones[:], rr[:, t0:t0 + tn], start=True, stop=True)
                    mm.then_inc(bonus_summed, 1)
                tiles(pe, step)

            @block.vector
            def _(dve):
                done = Chain(dve, feature_step, 23)

                def step(m, s, first):
                    done.start(m)
                    arrived(dve, m, s)
                    if not first:
                        dve.wait_ge(tail_ready, m)
                    for d in range(2):
                        nc.vector.tensor_copy(bias_now[:, 2 * d:2 * d + 1], w0_c[:, bass.ds(m + TILES * d, 1)])
                        nc.vector.tensor_copy(bias_now[:, 2 * d + 1:2 * d + 2], a0_c[:, bass.ds(m + TILES * d, 1)])
                    nc.vector.tensor_scalar(kk[:], k[s][:], kk_c[:, bass.ds(m, 1)], None, ALU.mult).then_inc(sums_ready, 1)
                    dve.wait_ge(kk_root, m + 1)
                    done(nc.vector.tensor_scalar(nrm[:], nrm[:], 1e-12, None, ALU.max))
                    done(nc.vector.reciprocal(nrm[:], nrm[:]))
                    done(nc.vector.tensor_tensor(kk[:], kk[:], nrm[:], ALU.mult))
                    for d in range(2):
                        dve.wait_ge(sig_ready, 2 * m + d + 1)
                        done(nc.vector.tensor_scalar(lw[d][:], lw[d][:], -float(np.exp(-0.5)), None, ALU.mult))
                        if d == 1:
                            dve.wait_ge(exps_ready, 2 * m + 1)
                        elif not first:
                            dve.wait_ge(exps_ready, 2 * m)
                        done(nc.vector.tensor_tensor_scan(c[:], reset[:], lw[d][:], 0.0, ALU.mult, ALU.add))
                        if d == 0:
                            nc.vector.tensor_tensor(e[:], c[:], lw[d][:], ALU.subtract).then_inc(sums_ready, 1)
                        else:
                            cv, ev = (t[:].rearrange("p (n c) -> p n c", c=CH) for t in (c, e))
                            done(nc.vector.tensor_tensor(ev, cv[:, :, CH - 1:CH].to_broadcast([P, NCH, CH]), cv, ALU.subtract))
                            nc.vector.tensor_tensor(c[:], e[:], lw[d][:], ALU.add).then_inc(sums_ready, 1)
                        done(nc.vector.tensor_scalar(kd[:], a[d][:], -1.0, ka_c[:, bass.ds(m, 1)], ALU.add, ALU.mult))
                        done(nc.vector.scalar_tensor_tensor(out=kd[:], in0=kd[:], scalar=1.0, in1=k[s][:], op0=ALU.add, op1=ALU.mult))
                        if d == 0:
                            nc.vector.tensor_copy(ksum[:], kd[:])
                        else:
                            done(nc.vector.tensor_tensor(ksum[:], ksum[:], kd[:], ALU.add))
                        done(nc.vector.tensor_tensor(a[d][:], a[d][:], kk[:], ALU.mult))
                        dve.wait_ge(exps_ready, 2 * m + d + 1)
                        if not (first and d == 0):
                            dve.wait_ge(stored, 80 * (2 * m + d))
                        done(nc.vector.tensor_tensor(outs[0][:], kk[:], excl[:], ALU.mult))
                        done(nc.vector.tensor_tensor(outs[1][:], a[d][:], down[:], ALU.mult))
                        done(nc.vector.tensor_tensor(outs[2][:], kd[:], down[:], ALU.mult))
                        nc.vector.tensor_tensor(outs[3][:], r[s][:], up[:], ALU.mult).then_inc(four_ready, 1)
                        dve.wait_ge(four_ready, 2 * m + d + 1)
                    done(nc.vector.tensor_scalar(rr[:], r[s][:], rk_c[:, bass.ds(m, 1)], None, ALU.mult))
                    nc.vector.tensor_tensor(rr[:], rr[:], ksum[:], ALU.mult).then_inc(bonus_in, 1)
                    if not first:
                        dve.wait_ge(tail_stored, 32 * m)
                    dve.wait_ge(gate_ready, m + 1)
                    done(nc.vector.tensor_copy(gat[:], Y[:, 0:TOK]))
                    dve.wait_ge(bonus_summed, m + 1)
                    nc.vector.tensor_tensor(bon[:], X[:, 0:TOK], v[s][:], ALU.mult).then_inc(tail_ready, 1)
                tiles(dve, step)

            @block.gpsimd
            def _(pool):
                def store(m, s, first):
                    for d in range(2):
                        pool.wait_ge(four_ready, 2 * m + d + 1)
                        pool.wait_ge(exps_ready, 2 * m + d + 1)
                        for n in range(4):
                            pool.dma_start(arrays[d, n, bass.ds(m * P, P), :], outs[n][:]).then_inc(stored, 16)
                        pool.dma_start(dec[d, bass.ds(m * P, P), :], wc[:]).then_inc(stored, 16)
                    pool.wait_ge(tail_ready, m + 1)
                    pool.dma_start(bonus[bass.ds(m * P, P), :], bon[:, CTX:TOK]).then_inc(tail_stored, 16)
                    pool.dma_start(gate[bass.ds(m * P, P), :], gat[:, CTX:TOK]).then_inc(tail_stored, 16)
                tiles(pool, store)
                pool.wait_ge(stored, 160 * TILES)
                pool.wait_ge(tail_stored, 32 * TILES)


def rwkv_chunks(nc, ident, masks, arrays, mixed, chunks):
    H = RW // P
    LEV = 5
    with ExitStack() as ctx:
        sb, ps = memory(nc, ctx)
        ar = [[sb(f"ar{s}{d}", [P, H, 2, CH]) for d in range(2)] for s in range(2)]
        be = [[sb(f"be{s}{d}", [P, H, CH]) for d in range(2)] for s in range(2)]
        ka = [[sb(f"ka{s}{d}", [P, H, CH]) for d in range(2)] for s in range(2)]
        vf = [sb(f"vf{s}", [P, H, CH]) for s in range(2)]
        two = lambda n, shape: [sb(f"{n}{d}", shape) for d in range(2)]
        mp = two("mp", [P, H, 2, CH])
        lt = two("lt", [P, H, CH])
        bq = two("bq", [P, H, 2, CH])
        kt = two("kt", [P, H, HD])
        am = two("am", [P, H, 2, CH])
        vt = two("vt", [P, H, HD])
        lev = [[sb(f"lev{d}{n}", [P, H, CH]) for n in range(LEV + 1)] for d in range(2)]
        z = two("z", [P, H, CH])
        x = two("x", [P, H, CH])
        lx = two("lx", [P, H, CH])
        au = two("au", [P, H, 2, CH])
        res = [sb(f"res{d}", [P, 4, H, CH]) for d in range(2)]
        big = [ps(f"big{d}", [P, H, 2, CH]) for d in range(2)]
        one = [ps(f"one{d}", [P, 2 * H, CH])[:, 0:H] for d in range(2)]
        six = [ps(f"six{d}", [P, 2 * H, CH])[:, 0:H] for d in range(2)]
        names = ["loaded0", "loaded1", "kar", "mp_ready", "bar", "lt_ready", "q_ready", "beta_t", "beta_c", "kappa_t",
                 "kappa_c", "alpha_t", "alpha_c", "v_t", "v_c", "levels", "z1a", "z1", "x1_t", "x1", "lx_p", "lx_c", "x_p", "x_c",
                 "z_p", "z_c", "mv_p", "mv_c", "au_p", "au_c", "gf_p", "g_c", "f_c", "h_p", "h_c", "y_p", "y_c",
                 "stored0", "stored1", "passed"]
        with stage(nc, *names) as (block, *sems):
            S = dict(zip(names, sems))
            loaded = (S["loaded0"], S["loaded1"])
            stored = (S["stored0"], S["stored1"])
            corners = (slice(0, HD), slice(HD, P))
            eye = masks[:, 0, 9, :]

            def wide(t):
                return t.rearrange("p (o c) -> p o c", o=1).to_broadcast([P, H, CH])

            def wait(eng, name, i, d, n=0, per=1):
                eng.wait_ge(S[name], i * (2 * per) + (2 * n + d + 1))

            def wait_last(eng, name, i, d, per=1):
                eng.wait_ge(S[name], i * (2 * per) + (d - 1))

            def dv(name, d):
                return arrays[d, {"alpha": 0, "beta": 1, "kappa": 2, "rho": 3}[name]].rearrange("(h k) t -> k h t", k=P)

            @block.sync
            def _(sp):
                def load(i, s, first):
                    if not first:
                        sp.wait_ge(S["y_c"], 2 * i - 2)
                        sp.wait_ge(S["f_c"], 2 * i - 2)
                    cols = bass.ds(i * CH, CH)
                    for d in range(2):
                        for dst, name in ((ar[s][d][:, :, 0, :], "alpha"), (ar[s][d][:, :, 1, :], "rho"),
                                          (be[s][d][:], "beta"), (ka[s][d][:], "kappa")):
                            sp.dma_start(dst, dv(name, d)[:, :, cols]).then_inc(loaded[s], 16)
                    sp.dma_start(vf[s][:], mixed[2 * RW:3 * RW, :].rearrange("(h k) t -> k h t", k=P)[:, :, cols]
                                 ).then_inc(loaded[s], 16)
                steps_of(sp, NCH, load)

            def arrived(eng, i, s, first):
                eng.wait_ge(loaded[s], 144 if first else (i - s) * 72 + 144)

            @block.tensor
            def _(pe):
                def step(i, s, first):
                    fresh = first and s == 0
                    arrived(pe, i, s, first)

                    def apart():
                        pe.sem_inc(S["passed"], 1)

                    def each(out, lhs, rhs, name, start=True, stop=True):
                        apart()
                        for h in range(H):
                            for c in corners:
                                mm = nc.tensor.matmul(out[c, h], lhs[c, h], rhs[c, h], start=start, stop=stop)
                        if name:
                            mm.then_inc(S[name], 1)

                    def turn(out, src, name):
                        apart()
                        for h in range(H):
                            for c in corners:
                                tr = nc.tensor.matmul(out[c, h], src[c, h], ident[c, c], start=True, stop=True)
                        tr.then_inc(S[name], 1)
                    both = lambda t: t.rearrange("p h a c -> p h (a c)") if hasattr(t, "rearrange") else t[:].rearrange("p h a c -> p h (a c)")
                    for d in range(2):
                        if not fresh:
                            wait_last(pe, "f_c", i, d)
                            wait_last(pe, "g_c", i, d)
                        each(both(big[d][:]), ka[s][d], both(ar[s][d][:]), "kar")
                    for d in range(2):
                        if not fresh:
                            wait_last(pe, "h_c", i, d)
                        turn(one[d], be[s][d], "beta_t")
                    for d in range(2):
                        if not fresh:
                            wait_last(pe, "y_c", i, d)
                        turn(six[d], ka[s][d], "kappa_t")
                    for d in range(2):
                        wait(pe, "mp_ready", i, d)
                        each(both(big[d][:]), be[s][d], both(ar[s][d][:]), "bar")
                    for d in range(2):
                        wait(pe, "beta_c", i, d)
                        turn(one[d], ar[s][d][:, :, 0, :], "alpha_t")
                    for d in range(2):
                        wait(pe, "kappa_c", i, d)
                        turn(six[d], vf[s], "v_t")
                    for d in range(2):
                        wait(pe, "alpha_c", i, d)
                        wait(pe, "z1", i, d)
                        turn(one[d], z[d], "x1_t")
                    for d in range(2):
                        wait(pe, "v_c", i, d)
                        each(six[d], mp[d][:, :, 0, :], vt[d], "mv_p")
                    for n in range(LEV):
                        for d in range(2):
                            if n == 0:
                                wait(pe, "x1", i, d)
                            else:
                                wait(pe, "x_c", i, d, n - 1, LEV)
                                wait(pe, "z_c", i, d, n - 1, LEV)
                            wait(pe, "levels", i, d, 0)
                            each(one[d], lev[d][n + 1], x[d], "lx_p")
                        for d in range(2):
                            if n == 0:
                                wait(pe, "mv_c", i, d)
                            wait(pe, "lx_c", i, d, n, LEV)
                            each(six[d], z[d], lx[d], "x_p")
                            each(one[d], lx[d], z[d], "z_p")
                    for d in range(2):
                        wait(pe, "lt_ready", i, d)
                        wait(pe, "q_ready", i, d)
                        wait(pe, "z_c", i, d, LEV - 1, LEV)
                        each(both(big[d][:]), z[d], both(am[d][:]), "au_p")
                    for d in range(2):
                        wait(pe, "au_c", i, d)
                        apart()
                        for h in range(H):
                            for c in corners:
                                nc.tensor.matmul(one[d][c, h], kt[d][c, h], vt[d][c, h], start=True, stop=False)
                            for c in corners:
                                mm = nc.tensor.matmul(one[d][c, h], bq[d][c, h, 0, :], au[d][c, h, 1, :], start=False, stop=True)
                        mm.then_inc(S["h_p"], 1)
                        each(both(big[d][:]), au[d][:, :, 0, :], both(bq[d][:]), "gf_p")
                        for h in range(H):
                            for c in corners:
                                nc.tensor.matmul(six[d][c, h], vt[d][c, h], mp[d][c, h, 1, :], start=True, stop=False)
                            for c in corners:
                                mm = nc.tensor.matmul(six[d][c, h], au[d][c, h, 1, :], bq[d][c, h, 1, :], start=False, stop=True)
                        mm.then_inc(S["y_p"], 1)
                steps_of(pe, NCH, step)

            @block.vector
            def _(dve):
                def step(i, s, first):
                    fresh = first and s == 0
                    V = nc.vector
                    for d in range(2):
                        wait(dve, "kar", i, d)
                        if not fresh:
                            wait_last(dve, "y_p", i, d)
                        m = masks[:, d, 0:2, :].rearrange("p (o a) c -> p o (a c)", o=1).to_broadcast([P, H, 2 * CH])
                        V.tensor_tensor(mp[d][:].rearrange("p h a c -> p h (a c)"), big[d][:].rearrange("p h a c -> p h (a c)"),
                                        m, ALU.mult).then_inc(S["mp_ready"], 1)
                    for d in range(2):
                        wait(dve, "bar", i, d)
                        if not fresh:
                            wait_last(dve, "y_p", i, d)
                        V.tensor_tensor(bq[d][:, :, 1, :], big[d][:, :, 1, :], wide(masks[:, d, 2, :]), ALU.mult
                                        ).then_inc(S["q_ready"], 1)
                        if not fresh:
                            wait_last(dve, "levels", i, d)
                        V.tensor_copy(lt[d][:], big[d][:, :, 0, :]).then_inc(S["lt_ready"], 1)
                        wait(dve, "lt_ready", i, d)
                        if not fresh:
                            wait_last(dve, "au_p", i, d)
                        V.tensor_tensor(z[d][:], lt[d][:], wide(masks[:, d, 3, :]), ALU.mult).then_inc(S["z1a"], 1)
                        wait(dve, "z1a", i, d)
                        V.tensor_tensor(z[d][:], z[d][:], wide(eye), ALU.add).then_inc(S["z1"], 1)
                    for d in range(2):
                        wait(dve, "x1_t", i, d)
                        V.tensor_copy(x[d][:], one[d][:]).then_inc(S["x1"], 1)
                    for n in range(LEV):
                        for d in range(2):
                            wait(dve, "x_p", i, d, n, LEV)
                            wait(dve, "x1", i, d)
                            if n:
                                wait(dve, "x_c", i, d, n - 1, LEV)
                            V.tensor_tensor(x[d][:], x[d][:], six[d][:], ALU.add).then_inc(S["x_c"], 1)
                            wait(dve, "z_p", i, d, n, LEV)
                            if n:
                                wait(dve, "z_c", i, d, n - 1, LEV)
                            V.tensor_tensor(z[d][:], z[d][:], one[d][:], ALU.add).then_inc(S["z_c"], 1)
                    for d in range(2):
                        wait(dve, "au_p", i, d)
                        if not fresh:
                            wait_last(dve, "y_p", i, d)
                        V.tensor_copy(au[d][:], big[d][:]).then_inc(S["au_c"], 1)
                    for d in range(2):
                        wait(dve, "h_p", i, d)
                        if not fresh:
                            dve.wait_ge(stored[d], i * 16)
                        V.tensor_copy(res[d][:, 2], one[d][:]).then_inc(S["h_c"], 1)
                        wait(dve, "gf_p", i, d)
                        V.tensor_tensor(res[d][:, 0], big[d][:, :, 0, :], wide(eye), ALU.add).then_inc(S["g_c"], 1)
                        V.tensor_tensor(res[d][:, 1], big[d][:, :, 1, :], ar[s][d][:, :, 1, :], ALU.add).then_inc(S["f_c"], 1)
                steps_of(dve, NCH, step)

            @block.scalar
            def _(act):
                def step(i, s, first):
                    fresh = first and s == 0
                    A = nc.scalar
                    for d in range(2):
                        wait(act, "beta_t", i, d)
                        if not fresh:
                            wait_last(act, "y_p", i, d)
                        A.mul(bq[d][:, :, 0, :], one[d][:], -1.0).then_inc(S["beta_c"], 1)
                    for d in range(2):
                        wait(act, "kappa_t", i, d)
                        A.copy(kt[d][:], six[d][:]).then_inc(S["kappa_c"], 1)
                    for d in range(2):
                        wait(act, "alpha_t", i, d)
                        A.copy(am[d][:, :, 0, :], one[d][:]).then_inc(S["alpha_c"], 1)
                    for d in range(2):
                        wait(act, "v_t", i, d)
                        A.copy(vt[d][:], six[d][:]).then_inc(S["v_c"], 1)
                    for d in range(2):
                        wait(act, "mv_p", i, d)
                        A.copy(am[d][:, :, 1, :], six[d][:]).then_inc(S["mv_c"], 1)
                    for n in range(LEV):
                        for d in range(2):
                            wait(act, "lx_p", i, d, n, LEV)
                            A.copy(lx[d][:], one[d][:]).then_inc(S["lx_c"], 1)
                    for d in range(2):
                        wait(act, "y_p", i, d)
                        if not fresh:
                            act.wait_ge(stored[d], i * 16)
                        A.copy(res[d][:, 3], six[d][:]).then_inc(S["y_c"], 1)
                steps_of(act, NCH, step)

            @block.gpsimd
            def _(pool):
                def step(i, s, first):
                    fresh = first and s == 0
                    for d in range(2):
                        wait(pool, "lt_ready", i, d)
                        if not fresh:
                            wait_last(pool, "lx_p", i, d, LEV)
                        for n in range(1, LEV + 1):
                            op = nc.gpsimd.tensor_tensor(lev[d][n][:], lt[d][:], wide(masks[:, d, 3 + n, :]), ALU.mult)
                        op.then_inc(S["levels"], 1)
                    for d in range(2):
                        wait(pool, "y_c", i, d)
                        wait(pool, "f_c", i, d)
                        wait(pool, "h_c", i, d)
                        wait(pool, "g_c", i, d)
                        pool.dma_start(chunks[d, bass.ds(i, 1)].rearrange("o p a n -> (o p) a n"),
                                       res[d][:].rearrange("p a h c -> p a (h c)")).then_inc(stored[d], 16)
                steps_of(pool, NCH, step)
                for d in range(2):
                    pool.wait_ge(stored[d], 16 * NCH)


def rwkv_recurrence(nc, chunks, dec, ys):
    H = RW // P
    corners = (slice(0, HD), slice(HD, P))
    CC = CTX // CH
    with ExitStack() as ctx:
        sb, ps = memory(nc, ctx)
        res = [[sb(f"res{s}{d}", [P, 4, H, CH]) for d in range(2)] for s in range(2)]
        state = [sb(f"state{d}", [P, H, HD]) for d in range(2)]
        grown = [sb(f"grown{d}", [P, H, HD]) for d in range(2)]
        y = [[sb(f"y{s}{d}", [P, H, CH]) for d in range(2)] for s in range(2)]
        wc = [sb(f"wc{d}", [P, H, NCH]) for d in range(2)]
        g_ps = [ps(f"g_ps{d}", [P, 2 * H, HD])[:, 0:H] for d in range(2)]
        y_ps = [ps(f"y_ps{d}", [P, 2 * H, CH])[:, 0:H] for d in range(2)]
        with stage(nc, "dec_loaded", "loaded0", "loaded1", "cleared", "grown_p", "y_p", "grown_c", "state_ready", "y_c",
                   "stored0", "stored1", "passed") as (
                block, dec_loaded, loaded0, loaded1, cleared, grown_p, y_p, grown_c, state_ready, y_c, stored0, stored1,
                passed):
            loaded, stored = (loaded0, loaded1), (stored0, stored1)

            def order(i, d, latent):
                return i if d == 0 else (NCH + CC - 1 if latent else CC - 1) - i

            def both_phases(eng, body):
                for i in range(CC + 2):
                    body(i, i % 2, i >= CC, i < 2)
                with eng.Fori(CC // 2 + 1, NCH // 2) as t:
                    for s in range(2):
                        body(2 * t + s, s, True, False)

            @block.sync
            def _(sp):
                for d in range(2):
                    sp.dma_start(wc[d][:], dec[d].rearrange("(h k) n -> k h n", k=P)).then_inc(dec_loaded, 16)

                def load(i, s, latent, first):
                    if not first:
                        sp.wait_ge(y_c, 2 * i - 2)
                        sp.wait_ge(state_ready, 2 * i - 2)
                    for d in range(2):
                        sp.dma_start(res[s][d][:].rearrange("p a h c -> p a (h c)"),
                                     chunks[d, bass.ds(order(i, d, latent), 1)].rearrange("o p a n -> (o p) a n")
                                     ).then_inc(loaded[s], 16)
                both_phases(sp, load)

            @block.tensor
            def _(pe):
                def step(i, s, latent, first):
                    pe.wait_ge(loaded[s], (i - s) * 16 + 32)
                    for d in range(2):
                        if first and s == 0:
                            pe.wait_ge(cleared, 2)
                        else:
                            pe.wait_ge(state_ready, 2 * i + (d - 1))
                            pe.wait_ge(y_c, 2 * i + (d - 1))
                        pe.sem_inc(passed, 1)
                        for h in range(H):
                            for c in corners:
                                mm = nc.tensor.matmul(g_ps[d][c, h], res[s][d][c, 0, h], state[d][c, h], start=True, stop=True)
                        mm.then_inc(grown_p, 1)
                        for h in range(H):
                            for c in corners:
                                mm = nc.tensor.matmul(y_ps[d][c, h], state[d][c, h], res[s][d][c, 1, h], start=True, stop=True)
                        mm.then_inc(y_p, 1)
                both_phases(pe, step)

            @block.vector
            def _(dve):
                for d in range(2):
                    nc.vector.memset(state[d][:], 0.0).then_inc(cleared, 1)
                dve.wait_ge(dec_loaded, 32)

                def step(i, s, latent, first):
                    for d in range(2):
                        dve.wait_ge(grown_p, 2 * i + (d + 1))
                        nc.vector.tensor_tensor(grown[d][:], g_ps[d][:], res[s][d][:, 2], ALU.add).then_inc(grown_c, 1)
                        dve.wait_ge(grown_c, 2 * i + (d + 1))
                        dve.wait_ge(y_p, 2 * i + (d + 1))
                        dve.sem_inc(passed, 1)
                        w = wc[d][:, :, bass.ds(order(i, d, latent), 1)].to_broadcast([P, H, HD])
                        nc.vector.tensor_tensor(state[d][:], grown[d][:], w, ALU.mult).then_inc(state_ready, 1)
                    for d in range(2):
                        if latent and not (type(i) is int and i < CC + 2):
                            dve.wait_ge(stored[s], (i - s) * 16 - 32 * (CC // 2))
                        nc.vector.tensor_tensor(y[s][d][:], y_ps[d][:], res[s][d][:, 3], ALU.add).then_inc(y_c, 1)
                both_phases(dve, step)

            @block.gpsimd
            def _(pool):
                with pool.Fori(CC // 2, NCH // 2) as t:
                    for s in range(2):
                        i = 2 * t + s
                        pool.wait_ge(y_c, 2 * i + 2)
                        for d in range(2):
                            pool.dma_start(ys[d].rearrange("(h v) t -> v h t", v=P)[:, :, bass.ds((order(i, d, True) - CC) * CH, CH)],
                                           y[s][d][:]).then_inc(stored[s], 16)
                for s in range(2):
                    pool.wait_ge(stored[s], 32 * (NCH - CC) // 2)


def rwkv_readout(nc, ys, block_ones, ln_w, ln_b, bonus, gate, mix, row0):
    TILES = RW // P
    with ExitStack() as ctx:
        sb, ps = memory(nc, ctx)
        y = [[sb(f"y{s}{n}", [P, LAT]) for n in range(4)] for s in range(2)]
        total, centred, square, std, out = ([sb(f"{n}{s}", [P, LAT]) for s in range(2)]
                                            for n in ("total", "centred", "square", "std", "out"))
        eps = sb("eps", [P, 1])
        mean_ps = [ps(f"mean{s}", [P, LAT]) for s in range(2)]
        var_ps = [ps(f"var{s}", [P, LAT]) for s in range(2)]
        with stage(nc, "eps_set", "loaded0", "loaded1", "total_ready", "mean_ready", "square_ready", "centred_ready", "var_ready", "std_ready",
                   "read_step", "ready", "stored0", "stored1") as (
                block, eps_set, loaded0, loaded1, total_ready, mean_ready, square_ready, centred_ready, var_ready, std_ready,
                read_step, ready, stored0, stored1):
            loaded, stored = (loaded0, loaded1), (stored0, stored1)

            @block.sync
            def _(sp):
                def load(i, s, first):
                    if not first:
                        sp.wait_ge(ready, i - 1)
                    for n, src in enumerate((ys[0], ys[1], bonus, gate)):
                        sp.dma_start(y[s][n][:], src[bass.ds(i * P, P), :]).then_inc(loaded[s], 16)
                steps_of(sp, TILES, load)

            @block.tensor
            def _(pe):
                def step(i, s, first):
                    pe.wait_ge(total_ready, i + 1)
                    nc.tensor.matmul(mean_ps[s][:], block_ones[:], total[s][:], start=True, stop=True).then_inc(mean_ready, 1)
                    pe.wait_ge(square_ready, i + 1)
                    nc.tensor.matmul(var_ps[s][:], block_ones[:], square[s][:], start=True, stop=True).then_inc(var_ready, 1)
                steps_of(pe, TILES, step)

            @block.scalar
            def _(act):
                act.wait_ge(eps_set, 1)
                def step(i, s, first):
                    act.wait_ge(centred_ready, i + 1)
                    nc.scalar.activation(square[s][:], centred[s][:], ACT.Square).then_inc(square_ready, 1)
                    act.wait_ge(var_ready, i + 1)
                    nc.scalar.activation(std[s][:], var_ps[s][:], ACT.Sqrt, bias=eps[:, 0:1], scale=1.0 / HD).then_inc(std_ready, 1)
                steps_of(act, TILES, step)

            @block.vector
            def _(dve):
                done = Chain(dve, read_step, 4)
                nc.vector.memset(eps[:], 64e-5).then_inc(eps_set, 1)

                def step(i, s, first):
                    done.start(i)
                    dve.wait_ge(loaded[s], 64 if first else (i - s) * 32 + 64)
                    nc.vector.tensor_tensor(total[s][:], y[s][0][:], y[s][1][:], ALU.add).then_inc(total_ready, 1)
                    dve.wait_ge(total_ready, i + 1)
                    dve.wait_ge(mean_ready, i + 1)
                    nc.vector.scalar_tensor_tensor(out=centred[s][:], in0=mean_ps[s][:], scalar=-1.0 / HD, in1=total[s][:],
                                                   op0=ALU.mult, op1=ALU.add).then_inc(centred_ready, 1)
                    dve.wait_ge(std_ready, i + 1)
                    done(nc.vector.reciprocal(std[s][:], std[s][:]))
                    done(nc.vector.tensor_tensor(centred[s][:], centred[s][:], std[s][:], ALU.mult))
                    done(nc.vector.tensor_scalar(centred[s][:], centred[s][:], ln_w[:, bass.ds(i, 1)], ln_b[:, bass.ds(i, 1)],
                                                 ALU.mult, ALU.add))
                    done(nc.vector.tensor_tensor(centred[s][:], centred[s][:], y[s][2][:], ALU.add))
                    if not first:
                        dve.wait_ge(stored[s], (i - s) * 8)
                    nc.vector.tensor_tensor(out[s][:], centred[s][:], y[s][3][:], ALU.mult).then_inc(ready, 1)
                steps_of(dve, TILES, step)

            @block.gpsimd
            def _(pool):
                def store(i, s, first):
                    pool.wait_ge(ready, i + 1)
                    pool.dma_start(mix[bass.ds(i * P + row0, P), CTX:TOK], out[s][:]).then_inc(stored[s], 16)
                steps_of(pool, TILES, store)
                for s in range(2):
                    pool.wait_ge(stored[s], 16 * TILES // 2)

def linear_narrow(nc, x, w, col0, n, dram, row0, spans=SPANS):
    with ExitStack() as ctx:
        sb, ps = memory(nc, ctx)
        staged, out = sb("staged", [P, KD, n]), sb("out", [n, TOK])
        wh = Halves(sb, "w", [P, KD, n])
        acc = [ps(f"acc{b}", [n, 512]) for b in range(2)]
        lo = min(t0 for t0, _ in spans)
        with stage(nc, "w_landed", "w_hi", "w_ready", "products", "copied", "stored") as (
                block, w_landed, w_hi, w_ready, products, copied, stored):
            @block.sync
            def _(sp):
                sp.dma_start(staged[:], w.rearrange("(k p) n -> p k n", p=P)[:, :, col0:col0 + n]).then_inc(w_landed, 16)
                sp.wait_ge(copied, 1)
                sp.dma_start(dram[row0:row0 + n, lo:TOK], out[:, lo:TOK]).then_inc(stored, 16)
                sp.wait_ge(stored, 16)

            @block.scalar
            def _(act):
                act.wait_ge(w_landed, 16)
                nc.scalar.copy(wh.hi[:], staged[:]).then_inc(w_hi, 1)

            @block.tensor
            def _(pe):
                pe.wait_ge(w_ready, 1)
                for b, (t0, tn) in enumerate(spans):
                    for k in range(KD):
                        mm = three_pass(nc, acc[b][:, 0:tn], (wh.hi[:, k, :], wh.lo[:, k, :]),
                                        (x.hi[:, k, t0:t0 + tn], x.lo[:, k, t0:t0 + tn]), k == 0, k == KD - 1)
                mm.then_inc(products, 1)

            @block.vector
            def _(dve):
                dve.wait_ge(w_hi, 1)
                nc.vector.tensor_tensor(wh.lo[:], staged[:], wh.hi[:].bitcast(F32), ALU.subtract).then_inc(w_ready, 1)
                dve.wait_ge(products, 1)
                for b, (t0, tn) in enumerate(spans):
                    op = nc.vector.tensor_copy(out[:, t0:t0 + tn], acc[b][:, 0:tn])
                op.then_inc(copied, 1)


GH, GK, GV = 4, 64, 128
GKW, GVW = GH * GK, GH * GV
AB_V, AB_LR, AB_Q, AB_R, AB_U, AB_G = 256, 768, 800, 1056, 1568, 2080


def gla_features(nc, proj, gate_w, gate_b, reset, arrays, dec):
    jobs = [(m, d) for m in range(2) for d in range(2)]
    with ExitStack() as ctx:
        sb, ps = memory(nc, ctx)
        lr = [sb(f"lr{d}", [16, TOK]) for d in range(2)]
        gw = sb("gw", [16, 2, GKW])
        k, q = ([sb(f"{n}{m}", [P, TOK]) for m in range(2)] for n in ("k", "q"))
        ones = sb("one", [P, 1])
        mag, low, la, c, e, c1, e1, up, down, rest = (sb(n, [P, TOK]) for n in (
            "mag", "low", "la", "c", "e", "c1", "e1", "up", "down", "rest"))
        outs = [sb(f"o{n}", [P, TOK]) for n in range(3)]
        wc = sb("wc", [P, NCH])
        zp = [ps(f"z{i}", [P, 1024]) for i in range(2)]
        with stage(nc, "loaded", "one_set", "z_ready", "low_ready", "mag_ready", "ln_ready", "features", "sums_ready", "exps_ready",
                   "ready", "stored") as (
                block, loaded, one_set, z_ready, low_ready, mag_ready, ln_ready, features, sums_ready, exps_ready, ready, stored):
            @block.sync
            def _(sp):
                for d in range(2):
                    sp.dma_start(lr[d][:], proj[AB_LR + 16 * d:AB_LR + 16 * d + 16, :]).then_inc(loaded, 16)
                sp.dma_start(gw[:], gate_w.rearrange("d l n -> l d n")).then_inc(loaded, 16)
                for m in range(2):
                    sp.dma_start(k[m][:], proj[m * P:(m + 1) * P, :]).then_inc(loaded, 16)
                    sp.dma_start(q[m][:], proj[AB_Q + m * P:AB_Q + (m + 1) * P, :]).then_inc(loaded, 16)

            @block.tensor
            def _(pe):
                pe.wait_ge(loaded, 112)
                for i, (m, d) in enumerate(jobs):
                    if i >= 2:
                        pe.wait_ge(mag_ready, i - 1)
                        pe.wait_ge(low_ready, i - 1)
                    for t0, tn in ((0, 512), (512, 256)):
                        mm = nc.tensor.matmul(zp[i % 2][:, t0:t0 + tn], gw[:, d, m * P:(m + 1) * P], lr[d][:, t0:t0 + tn],
                                              start=True, stop=True)
                    mm.then_inc(z_ready, 1)

            @block.scalar
            def _(act):
                act.wait_ge(one_set, 1)
                for i, (m, d) in enumerate(jobs):
                    act.wait_ge(z_ready, i + 1)
                    nc.scalar.activation(mag[:], zp[i % 2][:, 0:TOK], ACT.Abs, bias=gate_b[:, 2 * d + m:2 * d + m + 1]
                                         ).then_inc(mag_ready, 1)
                    act.wait_ge(mag_ready, i + 1)
                    nc.scalar.activation(mag[:], mag[:], ACT.Exp, scale=-1.0).then_inc(ln_ready, 1)
                    act.wait_ge(ln_ready, 2 * i + 1)
                    nc.scalar.activation(mag[:], mag[:], ACT.Ln, bias=ones[:, 0:1]).then_inc(ln_ready, 1)
                    act.wait_ge(sums_ready, i + 1)
                    if i:
                        act.wait_ge(ready, i)
                        act.wait_ge(stored, 64 * i)
                    cd, ed = (c, e) if d == 0 else (c1, e1)
                    nc.scalar.activation(up[:], cd[:], ACT.Exp)
                    nc.scalar.activation(down[:], cd[:], ACT.Exp, scale=-1.0)
                    nc.scalar.activation(rest[:], ed[:], ACT.Exp)
                    last = cd[:].rearrange("p (n c) -> p n c", c=CH)[:, :, (CH - 1) * (1 - d)]
                    nc.scalar.activation(wc[:], last, ACT.Exp).then_inc(exps_ready, 1)

            @block.vector
            def _(dve):
                done = Chain(dve, features, 7)
                nc.vector.memset(ones[:], 1.0).then_inc(one_set, 1)
                cv, ev = (t[:].rearrange("p (n c) -> p n c", c=CH) for t in (c, e))
                dve.wait_ge(loaded, 112)
                for i, (m, d) in enumerate(jobs):
                    if d == 0:
                        done.start(m)
                    col = gate_b[:, 2 * d + m:2 * d + m + 1]
                    dve.wait_ge(mag_ready, i + 1)
                    nc.vector.tensor_scalar(low[:], zp[i % 2][:, 0:TOK], col, 0.0, ALU.add, ALU.min).then_inc(low_ready, 1)
                    dve.wait_ge(low_ready, i + 1)
                    dve.wait_ge(ln_ready, 2 * i + 2)
                    done(nc.vector.tensor_tensor(low[:], low[:], mag[:], ALU.subtract))
                    done(nc.vector.tensor_scalar(la[:], low[:], 1.0 / 16, None, ALU.mult))
                    if i:
                        dve.wait_ge(exps_ready, i)
                    done(nc.vector.tensor_tensor_scan(c[:], reset[:], la[:], 0.0, ALU.mult, ALU.add))
                    total = cv[:, :, CH - 1:CH].to_broadcast([P, NCH, CH])
                    total_minus = nc.vector.tensor_tensor(ev, total, cv, ALU.subtract)
                    if d == 0:
                        total_minus.then_inc(sums_ready, 1)
                    else:
                        done(total_minus)
                    if d == 1:
                        nc.vector.tensor_tensor(e1[:], c[:], la[:], ALU.subtract)
                        nc.vector.tensor_tensor(c1[:], e[:], la[:], ALU.add).then_inc(sums_ready, 1)
                    dve.wait_ge(exps_ready, i + 1)
                    if i:
                        dve.wait_ge(stored, 64 * i)
                    nc.vector.tensor_tensor(outs[0][:], k[m][:], down[:], ALU.mult)
                    nc.vector.scalar_tensor_tensor(out=outs[1][:], in0=q[m][:], scalar=GK ** -0.5, in1=up[:], op0=ALU.mult, op1=ALU.mult)
                    nc.vector.tensor_tensor(outs[2][:], k[m][:], rest[:], ALU.mult).then_inc(ready, 1)

            @block.gpsimd
            def _(pool):
                for i, (m, d) in enumerate(jobs):
                    pool.wait_ge(ready, i + 1)
                    for n in range(3):
                        pool.dma_start(arrays[d, n, m * P:(m + 1) * P, :], outs[n][:]).then_inc(stored, 16)
                    pool.dma_start(dec[d, m * P:(m + 1) * P, :], wc[:]).then_inc(stored, 16)
                pool.wait_ge(stored, 64 * len(jobs))


CC = CTX // CH


def gla_chunks(nc, ident, masks, arrays, proj, dec, ys):
    with ExitStack() as ctx:
        sb, ps = memory(nc, ctx)
        kqr = [[sb(f"kqr{s}{d}", [GK, 3, GH, CH]) for d in range(2)] for s in range(2)]
        vf = [[sb(f"vf{s}{d}", [P, GH, CH]) for d in range(2)] for s in range(2)]
        two = lambda n, shape: [sb(f"{n}{d}", shape) for d in range(2)]
        sc = two("sc", [CH, GH, CH])
        kr = two("kr", [CH, GH, GK])
        vt = two("vt", [CH, GH, GV])
        state, scaled = two("state", [GK, GH, GV]), two("scaled", [GK, GH, GV])
        o = [[sb(f"o{s}{d}", [GV, GH, CH]) for d in range(2)] for s in range(2)]
        wc = two("wc", [GK, GH, NCH])
        b_ps = [ps(f"small{d}", [CH, 2, GH, CH]) for d in range(2)]
        v_ps = [ps(f"v{d}", [CH, GH, GV]) for d in range(2)]
        g_ps = [ps(f"g{d}", [GK, GH, GV]) for d in range(2)]
        o_ps = [ps(f"o{d}", [GV, GH, CH]) for d in range(2)]
        with stage(nc, "dec_loaded", "loaded0", "loaded1", "cleared", "sc_p", "v_p", "sc_c", "kr_c", "vt_c", "grown_p",
                   "o_p", "scaled_c", "state_c", "o_c", "stored0", "stored1", "passed") as (
                block, dec_loaded, loaded0, loaded1, cleared, sc_p, v_p, sc_c, kr_c, vt_c, grown_p, o_p, scaled_c,
                state_c, o_c, stored0, stored1, passed):
            loaded, stored = (loaded0, loaded1), (stored0, stored1)

            def order(i, d, latent):
                return i if d == 0 else (NCH + CC - 1 if latent else CC - 1) - i

            def both_phases(eng, body):
                for i in range(CC):
                    body(i, i % 2, False, i < 2)
                with eng.Fori(CC // 2, NCH // 2) as t:
                    for s in range(2):
                        body(2 * t + s, s, True, False)

            @block.sync
            def _(sp):
                for d in range(2):
                    sp.dma_start(wc[d][:], dec[d].rearrange("(h k) n -> k h n", k=GK)).then_inc(dec_loaded, 16)

                def load(i, s, latent, first):
                    if not first:
                        sp.wait_ge(o_p, 2 * i - 2)
                        sp.wait_ge(v_p, 2 * i - 2)
                    for d in range(2):
                        cols = bass.ds(order(i, d, latent) * CH, CH)
                        for n in range(3):
                            sp.dma_start(kqr[s][d][:, n], arrays[d, n].rearrange("(h k) t -> k h t", k=GK)[:, :, cols]
                                         ).then_inc(loaded[s], 16)
                        sp.dma_start(vf[s][d][:], proj[AB_V:AB_V + GVW, :].rearrange("(h v) t -> v h t", v=GV)[:, :, cols]
                                     ).then_inc(loaded[s], 16)
                both_phases(sp, load)

            @block.tensor
            def _(pe):
                def step(i, s, latent, first):
                    fresh = first and s == 0
                    for d in range(2):
                        if not fresh:
                            pe.wait_ge(kr_c, 2 * i + (d - 1))
                            pe.wait_ge(sc_c, 2 * i + (d - 1))
                            pe.wait_ge(vt_c, 2 * i + (d - 1))
                        pe.wait_ge(loaded[s], (i - s) * 64 + 128)
                        pe.sem_inc(passed, 1)
                        for h in range(GH):
                            nc.tensor.matmul(b_ps[d][:, 0, h], kqr[s][d][:, 0, h], kqr[s][d][:, 1, h], start=True, stop=True)
                        for h in range(GH):
                            mm = nc.tensor.transpose(b_ps[d][:, 1, h], kqr[s][d][:, 2, h], ident[0:GK, 0:GK])
                        mm.then_inc(sc_p, 1)
                        for h in range(GH):
                            mm = nc.tensor.transpose(v_ps[d][:, h], vf[s][d][:, h], ident[:])
                        mm.then_inc(v_p, 1)
                    for d in range(2):
                        pe.wait_ge(kr_c, 2 * i + (d + 1))
                        pe.wait_ge(vt_c, 2 * i + (d + 1))
                        pe.wait_ge(sc_c, 2 * i + (d + 1))
                        if fresh:
                            pe.wait_ge(cleared, 2)
                        else:
                            pe.wait_ge(o_c, 2 * i + (d - 1))
                            pe.wait_ge(state_c, 2 * i + (d - 1))
                        pe.sem_inc(passed, 1)
                        for h in range(GH):
                            nc.tensor.matmul(o_ps[d][:, h], state[d][:, h], kqr[s][d][:, 1, h], start=True, stop=False)
                            mm = nc.tensor.matmul(o_ps[d][:, h], vt[d][:, h], sc[d][:, h], start=False, stop=True)
                        mm.then_inc(o_p, 1)
                        for h in range(GH):
                            mm = nc.tensor.matmul(g_ps[d][:, h], kr[d][:, h], vt[d][:, h], start=True, stop=True)
                        mm.then_inc(grown_p, 1)
                both_phases(pe, step)

            @block.scalar
            def _(act):
                def step(i, s, latent, first):
                    fresh = first and s == 0
                    for d in range(2):
                        act.wait_ge(sc_c, 2 * i + (d + 1))
                        if not fresh:
                            act.wait_ge(grown_p, 2 * i + (d - 1))
                        nc.scalar.copy(kr[d][:], b_ps[d][:, 1]).then_inc(kr_c, 1)
                        act.wait_ge(v_p, 2 * i + (d + 1))
                        nc.scalar.copy(vt[d][:], v_ps[d][:]).then_inc(vt_c, 1)
                    for d in range(2):
                        act.wait_ge(o_p, 2 * i + (d + 1))
                        if not first:
                            act.wait_ge(stored[s], (i - s) * 16)
                        nc.scalar.copy(o[s][d][:], o_ps[d][:]).then_inc(o_c, 1)
                both_phases(act, step)

            @block.vector
            def _(dve):
                for d in range(2):
                    nc.vector.memset(state[d][:], 0.0).then_inc(cleared, 1)
                dve.wait_ge(dec_loaded, 32)

                def step(i, s, latent, first):
                    fresh = first and s == 0
                    for d in range(2):
                        dve.wait_ge(sc_p, 2 * i + (d + 1))
                        if not fresh:
                            dve.wait_ge(o_p, 2 * i + (d - 1))
                        m = masks[0:CH, d, 1, :].rearrange("p (o c) -> p o c", o=1).to_broadcast([CH, GH, CH])
                        nc.vector.tensor_tensor(sc[d][:], b_ps[d][:, 0], m, ALU.mult).then_inc(sc_c, 1)
                    for d in range(2):
                        if fresh:
                            dve.wait_ge(cleared, 2)
                        else:
                            dve.wait_ge(state_c, 2 * i + (d - 1))
                        dve.sem_inc(passed, 1)
                        w = wc[d][:, :, bass.ds(order(i, d, latent), 1)].to_broadcast([GK, GH, GV])
                        nc.vector.tensor_tensor(scaled[d][:], state[d][:], w, ALU.mult).then_inc(scaled_c, 1)
                    for d in range(2):
                        dve.wait_ge(scaled_c, 2 * i + (d + 1))
                        dve.wait_ge(o_p, 2 * i + (d + 1))
                        dve.wait_ge(grown_p, 2 * i + (d + 1))
                        nc.vector.tensor_tensor(state[d][:], scaled[d][:], g_ps[d][:], ALU.add).then_inc(state_c, 1)
                both_phases(dve, step)

            @block.gpsimd
            def _(pool):
                def store(i, s, latent, first):
                    pool.wait_ge(o_c, 2 * i + 2)
                    for d in range(2):
                        pool.dma_start(ys[d].rearrange("(h v) t -> v h t", v=GV)[:, :, bass.ds(order(i, d, latent) * CH, CH)],
                                       o[s][d][:]).then_inc(stored[s], 16)
                both_phases(pool, store)
                for s in range(2):
                    pool.wait_ge(stored[s], 16 * NCH)


def gla_readout(nc, ys, ones, gain, proj, mix):
    with ExitStack() as ctx:
        sb, ps = memory(nc, ctx)
        y0, y1, r, square, std, out = ([sb(f"{n}{s}", [P, TOK]) for s in range(2)] for n in ("y0", "y1", "r", "sq", "std", "out"))
        eps = sb("eps", [P, 1])
        total = [ps(f"total{s}", [P, 1024]) for s in range(2)]
        with stage(nc, "eps_set", "loaded0", "loaded1", "sum_ready", "squared", "summed", "std_ready", "silu_ready",
                   "read_step", "ready", "stored0", "stored1") as (
                block, eps_set, loaded0, loaded1, sum_ready, squared, summed, std_ready, silu_ready, read_step, ready,
                stored0, stored1):
            loaded, stored = (loaded0, loaded1), (stored0, stored1)

            @block.sync
            def _(sp):
                def load(i, s, first):
                    if not first:
                        sp.wait_ge(ready, i - 1)
                    for dst, src in ((y0[s], ys[0][bass.ds(i * P, P), :]), (y1[s], ys[1][bass.ds(i * P, P), :]),
                                     (r[s], proj[bass.ds(i * P + AB_R, P), :])):
                        sp.dma_start(dst[:], src).then_inc(loaded[s], 16)
                steps_of(sp, GH, load)

            @block.tensor
            def _(pe):
                def step(i, s, first):
                    pe.wait_ge(squared, i + 1)
                    for t0, tn in ((0, 512), (512, 256)):
                        mm = nc.tensor.matmul(total[s][:, t0:t0 + tn], ones[:], square[s][:, t0:t0 + tn], start=True, stop=True)
                    mm.then_inc(summed, 1)
                steps_of(pe, GH, step)

            @block.scalar
            def _(act):
                act.wait_ge(eps_set, 1)

                def step(i, s, first):
                    act.wait_ge(sum_ready, i + 1)
                    nc.scalar.activation(square[s][:], y0[s][:], ACT.Square).then_inc(squared, 1)
                    nc.scalar.activation(r[s][:], r[s][:], ACT.Silu).then_inc(silu_ready, 1)
                    act.wait_ge(summed, i + 1)
                    nc.scalar.activation(std[s][:], total[s][:, 0:TOK], ACT.Sqrt, bias=eps[:, 0:1], scale=1.0 / GV).then_inc(std_ready, 1)
                steps_of(act, GH, step)

            @block.vector
            def _(dve):
                done = Chain(dve, read_step, 2)
                nc.vector.memset(eps[:], EPS).then_inc(eps_set, 1)

                def step(i, s, first):
                    done.start(i)
                    dve.wait_ge(loaded[s], 48 if first else (i - s) * 24 + 48)
                    nc.vector.tensor_tensor(y0[s][:], y0[s][:], y1[s][:], ALU.add).then_inc(sum_ready, 1)
                    dve.wait_ge(std_ready, i + 1)
                    done(nc.vector.reciprocal(std[s][:], std[s][:]))
                    done(nc.vector.tensor_tensor(y0[s][:], y0[s][:], std[s][:], ALU.mult))
                    dve.wait_ge(silu_ready, i + 1)
                    if not first:
                        dve.wait_ge(stored[s], (i - s) * 8)
                    nc.vector.scalar_tensor_tensor(out=out[s][:], in0=y0[s][:], scalar=gain[:, bass.ds(i, 1)], in1=r[s][:],
                                                   op0=ALU.mult, op1=ALU.mult).then_inc(ready, 1)
                steps_of(dve, GH, step)

            @block.gpsimd
            def _(pool):
                def store(i, s, first):
                    pool.wait_ge(ready, i + 1)
                    pool.dma_start(mix[bass.ds(i * P, P), :], out[s][:]).then_inc(stored[s], 16)
                steps_of(pool, GH, store)
                for s in range(2):
                    pool.wait_ge(stored[s], 16 * GH // 2)


def gmlp(nc, ident, ones, proj, spatial_w, spatial_b, gain, mix):
    G = 4
    NT = TOK // P
    parts = ((0, 512), (512, 256))
    with ExitStack() as ctx:
        sb, ps = memory(nc, ctx)
        u, v = sb("u", [P, G, TOK]), sb("v", [P, G, TOK])
        square = sb("square", [P, G, TOK])
        mean, std, vt = sb("mean", [P, TOK]), sb("std", [P, TOK]), sb("vt", [P, NT, P])
        w, wt, bias = sb("w", [P, G, P]), sb("wt", [P, G, P]), sb("bias", [P, G, P])
        eps = sb("eps", [P, 1])
        sums = ps("sums", [P, 1024])
        turned = ps("turned", [P, 1024])
        mixed = ps("mixed", [P, 1024])
        with stage(nc, "loaded", "eps_set", "gelu_ready", "summed", "mean_ready", "centred", "squared", "squares_summed", "std_ready",
                   "norm_step", "normed", "w_turned", "w_ready", "v_turned", "v_ready", "mixed_ready", "biased", "ready", "stored") as (
                block, loaded, eps_set, gelu_ready, summed, mean_ready, centred, squared, squares_summed, std_ready, norm_step,
                normed, w_turned, w_ready, v_turned, v_ready, mixed_ready, biased, ready, stored):
            @block.sync
            def _(sp):
                for dst, row in ((v, AB_G), (u, AB_U)):
                    sp.dma_start(dst[:], proj[row:row + G * P, :].rearrange("(g p) t -> p g t", p=P)).then_inc(loaded, 16)
                sp.dma_start(w[:], spatial_w.rearrange("g t s -> t g s")).then_inc(loaded, 16)
                sp.dma_start(bias[:], spatial_b.rearrange("(o g) t -> o g t", o=1).to_broadcast([P, G, P])).then_inc(loaded, 16)

            @block.scalar
            def _(act):
                act.wait_ge(loaded, 64)
                nc.scalar.activation(v[:], v[:], ACT.Gelu_apprx_tanh).then_inc(gelu_ready, 1)
                nc.scalar.activation(u[:], u[:], ACT.Gelu_apprx_tanh).then_inc(gelu_ready, 1)
                for g in range(G):
                    act.wait_ge(centred, g + 1)
                    nc.scalar.activation(square[:, g, :], v[:, g, :], ACT.Square).then_inc(squared, 1)
                act.wait_ge(eps_set, 1)
                act.wait_ge(squares_summed, 1)
                nc.scalar.activation(std[:], sums[:, 0:TOK], ACT.Sqrt, bias=eps[:, 0:1], scale=1.0 / (G * P)).then_inc(std_ready, 1)
                act.wait_ge(w_turned, 1)
                nc.scalar.copy(wt[:], mixed[:, 0:G * P]).then_inc(w_ready, 1)
                for g in range(G):
                    act.wait_ge(v_turned, g + 1)
                    if g:
                        act.wait_ge(mixed_ready, g)
                    nc.scalar.copy(vt[:], turned[:, 0:TOK]).then_inc(v_ready, 1)

            @block.tensor
            def _(pe):
                pe.wait_ge(loaded, 64)
                for g in range(G):
                    tr = nc.tensor.transpose(mixed[:, g * P:(g + 1) * P], w[:, g, :], ident[:])
                tr.then_inc(w_turned, 1)
                pe.wait_ge(gelu_ready, 1)
                for t0, tn in parts:
                    for g in range(G):
                        mm = nc.tensor.matmul(sums[:, t0:t0 + tn], ones[:], v[:, g, t0:t0 + tn], start=(g == 0), stop=(g == G - 1))
                mm.then_inc(summed, 1)
                pe.wait_ge(squared, G)
                for t0, tn in parts:
                    for g in range(G):
                        mm = nc.tensor.matmul(sums[:, t0:t0 + tn], ones[:], square[:, g, t0:t0 + tn], start=(g == 0), stop=(g == G - 1))
                mm.then_inc(squares_summed, 1)
                pe.wait_ge(w_ready, 1)
                for g in range(G):
                    pe.wait_ge(normed, g + 1)
                    if g:
                        pe.wait_ge(v_ready, g)
                    for t in range(NT):
                        tr = nc.tensor.transpose(turned[:, t * P:(t + 1) * P], v[:, g, t * P:(t + 1) * P], ident[:])
                    tr.then_inc(v_turned, 1)
                    pe.wait_ge(v_ready, g + 1)
                    if g:
                        pe.wait_ge(biased, g)
                    for t in range(NT):
                        mm = nc.tensor.matmul(mixed[:, t * P:(t + 1) * P], vt[:, t, :], wt[:, g, :], start=True, stop=True)
                    mm.then_inc(mixed_ready, 1)

            @block.vector
            def _(dve):
                done = Chain(dve, norm_step, 1)
                done.start(0)
                nc.vector.memset(eps[:], EPS).then_inc(eps_set, 1)
                dve.wait_ge(summed, 1)
                nc.vector.tensor_scalar(mean[:], sums[:, 0:TOK], 1.0 / (G * P), None, ALU.mult).then_inc(mean_ready, 1)
                dve.wait_ge(mean_ready, 1)
                for g in range(G):
                    nc.vector.tensor_tensor(v[:, g, :], v[:, g, :], mean[:], ALU.subtract).then_inc(centred, 1)
                dve.wait_ge(std_ready, 1)
                done(nc.vector.reciprocal(std[:], std[:]))
                dve.wait_ge(centred, G)
                for g in range(G):
                    nc.vector.scalar_tensor_tensor(out=v[:, g, :], in0=v[:, g, :], scalar=gain[:, g:g + 1], in1=std[:],
                                                   op0=ALU.mult, op1=ALU.mult).then_inc(normed, 1)
                dve.wait_ge(gelu_ready, 2)
                dve.wait_ge(loaded, 64)
                for g in range(G):
                    dve.wait_ge(mixed_ready, g + 1)
                    dve.wait_ge(squared, G)
                    b = bias[:, g:g + 1, :].to_broadcast([P, NT, P])
                    nc.vector.tensor_tensor(square[:, g, :].rearrange("p (n t) -> p n t", t=P),
                                            mixed[:, 0:TOK].rearrange("p (n t) -> p n t", t=P), b, ALU.add).then_inc(biased, 1)
                    dve.wait_ge(biased, g + 1)
                    nc.vector.tensor_tensor(u[:, g, :], u[:, g, :], square[:, g, :], ALU.mult).then_inc(ready, 1)

            @block.gpsimd
            def _(pool):
                pool.wait_ge(ready, G)
                pool.dma_start(mix[GVW:GVW + G * P, :].rearrange("(g p) t -> p g t", p=P), u[:]).then_inc(stored, 16)
                pool.wait_ge(stored, 16)

SI, SG, SH, SN = 2048, 4, 8, 128
GW = SI // SG
SC = 128
NSC = TOK // SC
SCC = CTX // SC
SSD_B, SSD_C, SSD_DT, SSD_Z = 2048, 2560, 3072, 3136


def conv_silu(nc, proj, tiles, taps, bias, xbc):
    W = TOK + 8
    L0 = CTX + 6
    with ExitStack() as ctx:
        sb, _ = memory(nc, ctx)
        z = [sb(f"z{s}", [P, W]) for s in range(2)]
        acc = [sb(f"acc{s}", [P, W - 4]) for s in range(2)]
        out = [sb(f"out{s}", [P, W - 4]) for s in range(2)]
        with stage(nc, "zeroed", "loaded0", "loaded1", "tap_done", "taps_done", "ready", "stored0", "stored1") as (
                block, zeroed, loaded0, loaded1, tap_done, taps_done, ready, stored0, stored1):
            loaded, stored = (loaded0, loaded1), (stored0, stored1)

            @block.sync
            def _(sp):
                sp.wait_ge(zeroed, 2)

                def load(i, s, first):
                    if not first:
                        sp.wait_ge(taps_done, i - 1)
                    rows = proj[bass.ds(i * P, P), :]
                    sp.dma_start(z[s][:, 2:2 + CTX], rows[:, 0:CTX]).then_inc(loaded[s], 16)
                    sp.dma_start(z[s][:, L0:L0 + LAT], rows[:, CTX:TOK]).then_inc(loaded[s], 16)
                steps_of(sp, tiles, load)

            @block.vector
            def _(dve):
                done = Chain(dve, tap_done, 4)

                def step(i, s, first):
                    done.start(i)
                    dve.wait_ge(loaded[s], 32 if first else (i - s) * 16 + 32)
                    if not first:
                        dve.wait_ge(ready, i - 1)
                    done(nc.vector.tensor_scalar(acc[s][:], z[s][:, 0:W - 4], taps[:, bass.ds(i, 1)], bias[:, bass.ds(i, 1)],
                                                 ALU.mult, ALU.add))
                    for j in range(1, 5):
                        op = nc.vector.scalar_tensor_tensor(out=acc[s][:], in0=z[s][:, j:W - 4 + j],
                                                            scalar=taps[:, bass.ds(i + j * tiles, 1)], in1=acc[s][:],
                                                            op0=ALU.mult, op1=ALU.add)
                        if j < 4:
                            done(op)
                    op.then_inc(taps_done, 1)
                steps_of(dve, tiles, step)

            @block.scalar
            def _(act):
                def step(i, s, first):
                    act.wait_ge(taps_done, i + 1)
                    if not first:
                        act.wait_ge(stored[s], (i - s) * 16)
                    nc.scalar.activation(out[s][:], acc[s][:], ACT.Silu).then_inc(ready, 1)
                steps_of(act, tiles, step)

            @block.gpsimd
            def _(pool):
                for s in range(2):
                    nc.gpsimd.memset(z[s][:], 0.0).then_inc(zeroed, 1)

                def store(i, s, first):
                    pool.wait_ge(ready, i + 1)
                    rows = xbc[bass.ds(i * P, P), :]
                    pool.dma_start(rows[:, 0:CTX], out[s][:, 0:CTX]).then_inc(stored[s], 16)
                    pool.dma_start(rows[:, CTX:TOK], out[s][:, CTX + 4:CTX + 4 + LAT]).then_inc(stored[s], 16)
                steps_of(pool, tiles, store)
                for s in range(2):
                    pool.wait_ge(stored[s], 32 * ((tiles + 1 - s) // 2))


def ssd_steps(nc, ident, proj, dt_bias, a_log, reset, by_token, acum):
    R = 2 * SG * SH
    nac, eac, dtt, drt = by_token
    with ExitStack() as ctx:
        sb, ps = memory(nc, ctx)
        raw, mag, dt, da, c, e, rest = (sb(n, [R, TOK]) for n in ("raw", "mag", "dt", "da", "c", "e", "rest"))
        bias, a, one = sb("bias", [R, 1]), sb("a", [R, 1]), sb("one", [R, 1])
        turned = [ps(f"turned{n}", [P, NSC, R]) for n in range(3)]
        with stage(nc, "loaded", "act_step", "act_turned", "dve_step", "sums_ready", "rest_ready", "all_ready", "turned_ready",
                   "stored") as (
                block, loaded, act_step, act_turned, dve_step, sums_ready, rest_ready, all_ready, turned_ready, stored):
            @block.sync
            def _(sp):
                sp.dma_start(raw[:], proj[SSD_DT:SSD_DT + R, :]).then_inc(loaded, 16)
                sp.dma_start(bias[:], dt_bias.rearrange("d (h o) -> (d h) o", o=1)).then_inc(loaded, 16)
                sp.dma_start(a[:], a_log.rearrange("d (h o) -> (d h) o", o=1)).then_inc(loaded, 16)
                sp.wait_ge(all_ready, 1)
                sp.dma_start(acum, c[:]).then_inc(stored, 16)
                sp.wait_ge(stored, 16)

            @block.scalar
            def _(act):
                done = Chain(act, act_step, 4)
                done.start(0)
                act.wait_ge(loaded, 48)
                act.wait_ge(dve_step, 2)
                done(nc.scalar.activation(mag[:], raw[:], ACT.Abs, bias=bias[:, 0:1]))
                done(nc.scalar.activation(mag[:], mag[:], ACT.Exp, scale=-1.0))
                done(nc.scalar.activation(mag[:], mag[:], ACT.Ln, bias=one[:, 0:1]))
                done(nc.scalar.activation(a[:], a[:], ACT.Exp))
                act.wait_ge(sums_ready, 1)
                nc.scalar.activation(rest[:], e[:], ACT.Exp).then_inc(rest_ready, 1)
                act.wait_ge(turned_ready, 3)
                nc.scalar.mul(nac[:], turned[0][:], -1.0)
                nc.scalar.activation(eac[:], turned[0][:], ACT.Exp)
                nc.scalar.copy(dtt[:], turned[1][:])
                nc.scalar.copy(drt[:], turned[2][:])

            @block.vector
            def _(dve):
                done = Chain(dve, dve_step, 9)
                done.start(0)
                dve.wait_ge(loaded, 48)
                done(nc.vector.memset(one[:], 1.0))
                done(nc.vector.tensor_scalar(dt[:], raw[:], bias[:, 0:1], 0.0, ALU.add, ALU.max))
                dve.wait_ge(act_step, 4)
                done(nc.vector.tensor_tensor(dt[:], dt[:], mag[:], ALU.add))
                done(nc.vector.tensor_scalar(da[:], dt[:], a[:, 0:1], -1.0, ALU.mult, ALU.mult))
                done(nc.vector.tensor_tensor_scan(c[:], reset[0:R, :], da[:], 0.0, ALU.mult, ALU.add))
                cv, ev = (t[:].rearrange("p (n c) -> p n c", c=SC) for t in (c, e))
                done(nc.vector.tensor_tensor(ev, cv[:, :, SC - 1:SC].to_broadcast([R, NSC, SC]), cv, ALU.subtract))
                b = slice(R // 2, R)
                done(nc.vector.tensor_tensor(rest[b, :], c[b, :], da[b, :], ALU.subtract))
                done(nc.vector.tensor_tensor(c[b, :], e[b, :], da[b, :], ALU.add))
                nc.vector.tensor_copy(e[b, :], rest[b, :]).then_inc(sums_ready, 1)
                dve.wait_ge(rest_ready, 1)
                done(nc.vector.tensor_tensor(rest[:], rest[:], dt[:], ALU.mult))
                nc.vector.tensor_copy(one[:], bias[:]).then_inc(all_ready, 1)

            @block.tensor
            def _(pe):
                pe.wait_ge(all_ready, 1)
                for n, src in enumerate((c, dt, rest)):
                    for k in range(NSC):
                        tr = nc.tensor.transpose(turned[n][:, k, :], src[:, k * SC:(k + 1) * SC], ident[0:R, 0:R])
                    tr.then_inc(turned_ready, 1)


def ssd_groups(nc, ident, mask, by_token, acum, xbc, skip, ys):
    nac, eac, dtt, drt = by_token
    work = [(d, j, j if d == 0 else (SCC - 1 - j if j < SCC else NSC + SCC - 1 - j)) for j in range(NSC) for d in range(2)]
    NW = len(work)
    LATW = [w for w in work if w[1] >= SCC]
    FILLS = NSC + 3
    with ExitStack() as ctx:
        sb, ps = memory(nc, ctx)
        xf, bf, cf = sb("xf", [P, 4, TOK]), sb("bf", [P, TOK]), sb("cf", [P, TOK])
        xt, bt, cb = sb("xt", [P, NSC, GW]), sb("bt", [P, NSC, SN]), sb("cb", [P, NSC - SCC, SC])
        rows = [sb(f"rows{s}", [P, SH, SC]) for s in range(2)]
        two = lambda n, shape: [sb(f"{n}{d}", shape) for d in range(2)]
        shifted, decay, last = two("shifted", [P, SH, SC]), two("decay", [P, SH, SC]), two("last", [P, SH])
        xr, xd, dx = two("xr", [P, SH, HD]), two("xd", [P, SH, HD]), sb("dx", [P, SH, HD])
        state, faded = two("state", [P, SH, HD]), two("faded", [P, SH, HD])
        off, y = two("off", [P, SH, HD]), two("y", [P, SH, HD])
        bank = [ps(f"bank{i}", [P, 512]) for i in range(2)]
        off_ps, diag_ps, grow_ps = ([ps(f"{n}{d}", [P, SH, HD]) for d in range(2)] for n in ("off_ps", "diag_ps", "grow_ps"))
        names = ["loaded", "rows0", "rows1", "filled", "emptied", "shifted_c", "exp_c", "last_c", "scores_c", "xr_c", "xd_c", "dx_c",
                 "off_p", "diag_p", "grow_p", "zeroed", "passed", "faded_c", "state_c", "off_c", "y0_c", "y_c", "stored0", "stored1"]
        with stage(nc, *names) as (block, *sems):
            S = dict(zip(names, sems))
            rows_loaded, stored = (S["rows0"], S["rows1"]), (S["stored0"], S["stored1"])

            def groups(eng, body):
                body(0, True)
                with eng.Fori(1, SG) as g:
                    body(g, False)

            def heads_of(t, c, g, d):
                return t[:, c, bass.ds(g * SH + d * (SG * SH), SH)]

            def spread(t, n):
                return t.rearrange("p (h o) -> p h o", o=1).to_broadcast([P, SH, n])

            @block.sync
            def _(sp):
                def load(g, first):
                    if not first:
                        sp.wait_ge(S["filled"], g * FILLS)
                        sp.sem_inc(S["passed"], 1)
                        sp.wait_ge(S["off_p"], g * len(LATW))
                    sp.sem_inc(S["passed"], 1)
                    sp.dma_start(xf[:], xbc[bass.ds(g * GW, GW), :].rearrange("(k p) t -> p k t", p=P)).then_inc(S["loaded"], 16)
                    sp.dma_start(bf[:], xbc[bass.ds(g * SN + SSD_B, SN), :]).then_inc(S["loaded"], 16)
                    sp.dma_start(cf[:], xbc[bass.ds(g * SN + SSD_C, SN), :]).then_inc(S["loaded"], 16)
                    for w, (d, j, c) in enumerate(work):
                        s = w % 2
                        if w >= 2:
                            sp.wait_ge(S["last_c"], g * (NW - 2) + (w - 1))
                            sp.sem_inc(S["passed"], 1)
                        if w - 1 > 2 * SCC:
                            sp.wait_ge(S["shifted_c"], g * len(LATW) + (w - 1 - 2 * SCC))
                        elif w < 2 and not first:
                            sp.wait_ge(S["shifted_c"], g * len(LATW) + (w - 1))
                        sp.sem_inc(S["passed"], 1)
                        sp.dma_start(rows[s][:], acum[bass.ds(g * SH + d * (SG * SH), SH), c * SC:(c + 1) * SC]
                                     .rearrange("(o h) t -> o h t", o=1).to_broadcast([P, SH, SC])).then_inc(rows_loaded[s], 16)
                groups(sp, load)

            @block.tensor
            def _(pe):
                def group(g, first):
                    pe.wait_ge(S["loaded"], g * 48 + 48)
                    for f in range(FILLS):
                        if f >= 2 or not first:
                            pe.wait_ge(S["emptied"], g * FILLS + (f - 1 if f >= 2 else 0))
                        b = bank[f % 2]
                        if f < NSC:
                            for k in range(4):
                                mm = nc.tensor.transpose(b[:, k * P:(k + 1) * P], xf[:, k, f * SC:(f + 1) * SC], ident[:])
                        elif f < NSC + 2:
                            for k in range(4 if f == NSC else 2):
                                c = k + 4 * (f - NSC)
                                mm = nc.tensor.transpose(b[:, k * P:(k + 1) * P], bf[:, c * SC:(c + 1) * SC], ident[:])
                        else:
                            for c in range(SCC, NSC):
                                mm = nc.tensor.matmul(b[:, (c - SCC) * SC:(c - SCC + 1) * SC], bf[:, c * SC:(c + 1) * SC],
                                                      cf[:, c * SC:(c + 1) * SC], start=True, stop=True)
                        mm.then_inc(S["filled"], 1)
                    pe.wait_ge(S["emptied"], g * FILLS + FILLS)
                    m = 0
                    for w, (d, j, c) in enumerate(work):
                        if j < NSC - 1:
                            k = g * (NW - 2) + w
                            pe.wait_ge(S["xr_c"], k + 1)
                            if not (first and w < 2):
                                pe.wait_ge(S["state_c"], k - 1)
                            nc.tensor.matmul(grow_ps[d][:].rearrange("p h v -> p (h v)"), bt[:, c, :],
                                             xr[d][:].rearrange("p h v -> p (h v)"), start=True, stop=True).then_inc(S["grow_p"], 1)
                        if j >= SCC:
                            mm_n = g * len(LATW) + m
                            if not (first and m < 2):
                                pe.wait_ge(S["y0_c"], mm_n - 1)
                            pe.wait_ge(S["state_c"], g * (NW - 2) + (w - 1))
                            nc.tensor.matmul(off_ps[d][:].rearrange("p h v -> p (h v)"), cf[:, c * SC:(c + 1) * SC],
                                             state[d][:].rearrange("p h v -> p (h v)"), start=True, stop=True).then_inc(S["off_p"], 1)
                            pe.wait_ge(S["scores_c"], mm_n + 1)
                            pe.wait_ge(S["xd_c"], mm_n + 1)
                            for h in range(SH):
                                mm = nc.tensor.matmul(diag_ps[d][:, h], decay[d][:, h], xd[d][:, h], start=True, stop=True)
                            mm.then_inc(S["diag_p"], 1)
                            m += 1
                groups(pe, group)

            @block.scalar
            def _(act):
                def group(g, first):
                    for f in range(FILLS):
                        act.wait_ge(S["filled"], g * FILLS + (f + 1))
                        if not first and f == 0:
                            act.wait_ge(S["grow_p"], g * (NW - 2))
                            act.wait_ge(S["scores_c"], g * len(LATW))
                            act.wait_ge(S["xr_c"], g * (NW - 2))
                            act.wait_ge(S["xd_c"], g * len(LATW))
                            act.wait_ge(S["dx_c"], g * (NSC - SCC))
                        b = bank[f % 2]
                        if f < NSC:
                            op = nc.scalar.copy(xt[:, f, :], b[:])
                        elif f < NSC + 2:
                            k, c = (4, 0) if f == NSC else (2, 4)
                            op = nc.scalar.copy(bt[:, c:c + k, :], b[:, 0:k * P])
                        else:
                            op = nc.scalar.copy(cb[:], b[:])
                        op.then_inc(S["emptied"], 1)
                    m = 0
                    for w, (d, j, c) in enumerate(work):
                        s = w % 2
                        act.wait_ge(rows_loaded[s], g * (8 * NW) + 16 * (w // 2 + 1))
                        if j < NSC - 1:
                            if not (first and w < 2):
                                act.wait_ge(S["faded_c"], g * (NW - 2) + (w - 1))
                            edge = (SC - 1) * (1 - d)
                            nc.scalar.activation(last[d][:], rows[s][:, :, edge], ACT.Exp).then_inc(S["last_c"], 1)
                        if j >= SCC:
                            mm_n = g * len(LATW) + m
                            act.wait_ge(S["shifted_c"], mm_n + 1)
                            if not (first and m < 2):
                                act.wait_ge(S["diag_p"], mm_n - 1)
                            act.sem_inc(S["passed"], 1)
                            for h in range(SH):
                                op = nc.scalar.activation(decay[d][:, h], shifted[d][:, h], ACT.Exp,
                                                          bias=nac[:, c, bass.ds(g * SH + (d * (SG * SH) + h), 1)])
                            op.then_inc(S["exp_c"], 1)
                            m += 1
                groups(act, group)

            @block.gpsimd
            def _(pool):
                def group(g, first):
                    pool.wait_ge(S["emptied"], g * FILLS + FILLS)
                    m = 0
                    for w, (d, j, c) in enumerate(work):
                        xc = xt[:, c, :].rearrange("p (h v) -> p h v", v=HD)
                        if j < NSC - 1:
                            k = g * (NW - 2) + w
                            if not (first and w < 2):
                                pool.wait_ge(S["grow_p"], k - 1)
                            pool.sem_inc(S["passed"], 1)
                            nc.gpsimd.tensor_tensor(xr[d][:], xc, spread(heads_of(drt, c, g, d), HD), ALU.mult).then_inc(S["xr_c"], 1)
                        if j >= SCC:
                            mm_n = g * len(LATW) + m
                            if not (first and m < 2):
                                pool.wait_ge(S["diag_p"], mm_n - 1)
                            pool.sem_inc(S["passed"], 1)
                            nc.gpsimd.tensor_tensor(xd[d][:], xc, spread(heads_of(dtt, c, g, d), HD), ALU.mult).then_inc(S["xd_c"], 1)
                            if d == 0:
                                if not (first and m < 1):
                                    pool.wait_ge(S["y_c"], g * (NSC - SCC) + m // 2)
                                pool.sem_inc(S["passed"], 1)
                                nc.gpsimd.tensor_tensor(dx[:], xc, spread(skip[:, bass.ds(g * SH, SH)], HD), ALU.mult
                                                        ).then_inc(S["dx_c"], 1)
                            store(g, m - 1)
                            m += 1
                    store(g, len(LATW) - 1)

                def store(g, m):
                    if m < 0:
                        return
                    d, j, c = LATW[m]
                    if d == 0:
                        pool.wait_ge(S["y_c"], g * (NSC - SCC) + (m // 2 + 1))
                    else:
                        pool.wait_ge(S["y0_c"], g * len(LATW) + (m + 1))
                    pool.dma_start(ys[d][(c - SCC) * SC:(c - SCC + 1) * SC, bass.ds(g * GW, GW)],
                                   y[d][:].rearrange("p h v -> p (h v)")).then_inc(stored[d], 16)
                groups(pool, group)
                for d in range(2):
                    pool.wait_ge(stored[d], 16 * SG * (NSC - SCC))

            @block.vector
            def _(dve):
                V = nc.vector

                def shift(g, first, m):
                    d, j, c = LATW[m]
                    w = work.index(LATW[m])
                    s = w % 2
                    dve.wait_ge(rows_loaded[s], g * (8 * NW) + 16 * (w // 2 + 1))
                    if not (first and m < 2):
                        dve.wait_ge(S["exp_c"], g * len(LATW) + (m - 1))
                    V.tensor_tensor(shifted[d][:], rows[s][:], mask[:, d, :].rearrange("p (o t) -> p o t", o=1)
                                    .to_broadcast([P, SH, SC]), ALU.add).then_inc(S["shifted_c"], 1)

                def group(g, first):
                    if not first:
                        dve.wait_ge(S["off_p"], g * len(LATW))
                        dve.wait_ge(S["faded_c"], g * (NW - 2))
                    for d in range(2):
                        V.memset(state[d][:], 0.0).then_inc(S["zeroed"], 1)
                    dve.wait_ge(S["zeroed"], g * 2 + 2)
                    m = 0
                    for w, (d, j, c) in enumerate(work):
                        if j < NSC - 1 and j < SCC:
                            fade(g, w, d, j, None)
                        if j < SCC:
                            if w + 1 == 2 * SCC:
                                shift(g, first, 0)
                            continue
                        mm_n = g * len(LATW) + m
                        dve.wait_ge(S["exp_c"], mm_n + 1)
                        dve.wait_ge(S["emptied"], g * FILLS + FILLS)
                        V.tensor_tensor(decay[d][:], decay[d][:], cb[:, c - SCC, :].rearrange("p (o t) -> p o t", o=1)
                                        .to_broadcast([P, SH, SC]), ALU.mult).then_inc(S["scores_c"], 1)
                        if m + 1 < len(LATW):
                            shift(g, first, m + 1)
                        if j < NSC - 1:
                            fade(g, w, d, j, mm_n)
                        dve.wait_ge(S["off_p"], mm_n + 1)
                        dve.sem_inc(S["passed"], 1)
                        V.tensor_tensor(off[d][:], off_ps[d][:], spread(heads_of(eac, c, g, d), HD), ALU.mult).then_inc(S["off_c"], 1)
                        dve.wait_ge(S["off_c"], mm_n + 1)
                        dve.wait_ge(S["diag_p"], mm_n + 1)
                        if not (first and m < 2):
                            dve.wait_ge(stored[d], (g * len(LATW) + (m - d)) * 8)
                        V.tensor_tensor(y[d][:], off[d][:], diag_ps[d][:], ALU.add).then_inc(S["y0_c"], 1)
                        if d == 0:
                            dve.wait_ge(S["y0_c"], mm_n + 1)
                            dve.wait_ge(S["dx_c"], g * (NSC - SCC) + (m // 2 + 1))
                            V.tensor_tensor(y[d][:], y[d][:], dx[:], ALU.add).then_inc(S["y_c"], 1)
                        m += 1

                def fade(g, w, d, j, mm_n):
                    k = g * (NW - 2) + w
                    dve.wait_ge(S["last_c"], k + 1)
                    if w >= 2:
                        dve.wait_ge(S["state_c"], k - 1)
                    V.tensor_tensor(faded[d][:], state[d][:], spread(last[d][:], HD), ALU.mult).then_inc(S["faded_c"], 1)
                    dve.wait_ge(S["faded_c"], k + 1)
                    dve.wait_ge(S["grow_p"], k + 1)
                    if mm_n is not None:
                        dve.wait_ge(S["off_p"], mm_n + 1)
                    V.tensor_tensor(state[d][:], faded[d][:], grow_ps[d][:], ALU.add).then_inc(S["state_c"], 1)
                groups(dve, group)



def ssd_readout(nc, ident, ones, ys, proj, gain, out):
    T = GW // P
    with ExitStack() as ctx:
        sb, ps = memory(nc, ctx)
        y0, y1, z, gated, square = ([sb(f"{n}{s}", [P, 4, 512]) for s in range(2)] for n in ("y0", "y1", "z", "gated", "sq"))
        std = [sb(f"std{s}", [P, LAT]) for s in range(2)]
        eps = sb("eps", [P, 1])
        scaled_rows = sb("scaled_rows", [P, T, LAT])
        turned = [ps(f"turned{t}", [P, LAT]) for t in range(T)]

        def row_order(tile):
            return tile.rearrange("p (r c) -> p c r", c=64)

        total = [ps(f"total{s}", [P, LAT]) for s in range(2)]
        with stage(nc, "eps_set", "loaded0", "loaded1", "sum_ready", "turned_ready", "silu_ready", "gated_ready", "squared",
                   "summed", "std_ready", "rstd_ready", "scaled", "hi_ready", "ready") as (
                block, eps_set, loaded0, loaded1, sum_ready, turned_ready, silu_ready, gated_ready, squared, summed,
                std_ready, rstd_ready, scaled, hi_ready, ready):
            loaded = (loaded0, loaded1)

            @block.sync
            def _(sp):
                def load(g, s, first):
                    if not first:
                        sp.wait_ge(gated_ready, T * g - T)
                    for dst, d in ((y0[s], 0), (y1[s], 1)):
                        sp.dma_start(dst[:], ys[d].rearrange("(n p) f -> p n f", p=P)[:, :, bass.ds(g * GW, GW)]).then_inc(loaded[s], 16)
                    sp.dma_start(z[s][:], proj[bass.ds(g * GW + SSD_Z, GW), CTX:TOK].rearrange("(k p) t -> p k t", p=P)).then_inc(loaded[s], 16)
                steps_of(sp, SG, load)

            @block.tensor
            def _(pe):
                def step(g, s, first):
                    pe.wait_ge(sum_ready, g + 1)
                    for k in range(T):
                        if not (first and s == 0):
                            pe.wait_ge(gated_ready, T * g + (k - T + 1))
                        for n in range(4):
                            tr = nc.tensor.transpose(turned[k][:, n * P:(n + 1) * P], y0[s][:, n, k * P:(k + 1) * P], ident[:])
                        tr.then_inc(turned_ready, 1)
                    if not first:
                        pe.wait_ge(std_ready, g - 1)
                    pe.wait_ge(squared, g + 1)
                    for k in range(T):
                        mm = nc.tensor.matmul(total[s][:], ones[:], square[s][:, k, :], start=(k == 0), stop=(k == T - 1))
                    mm.then_inc(summed, 1)
                steps_of(pe, SG, step)

            @block.scalar
            def _(act):
                act.wait_ge(eps_set, 1)

                def step(g, s, first):
                    act.wait_ge(loaded[s], 48 if first else (g - s) * 24 + 48)
                    nc.scalar.activation(z[s][:], z[s][:], ACT.Silu).then_inc(silu_ready, 1)
                    act.wait_ge(gated_ready, T * g + T)
                    if not first:
                        act.wait_ge(summed, g - 1)
                    nc.scalar.activation(square[s][:], gated[s][:], ACT.Square).then_inc(squared, 1)
                    act.wait_ge(summed, g + 1)
                    if not first:
                        act.wait_ge(ready, g - 1)
                    nc.scalar.activation(std[s][:], total[s][:], ACT.Sqrt, bias=eps[:, 0:1], scale=1.0 / GW).then_inc(std_ready, 1)
                steps_of(act, SG, step)

            @block.vector
            def _(dve):
                nc.vector.memset(eps[:], EPS).then_inc(eps_set, 1)

                def step(g, s, first):
                    dve.wait_ge(loaded[s], 48 if first else (g - s) * 24 + 48)
                    nc.vector.tensor_tensor(y0[s][:], y0[s][:], y1[s][:], ALU.add).then_inc(sum_ready, 1)
                    dve.wait_ge(silu_ready, g + 1)
                    if not first:
                        dve.wait_ge(ready, g - 1)
                    for k in range(T):
                        dve.wait_ge(turned_ready, T * g + (k + 1))
                        nc.vector.tensor_tensor(gated[s][:, k, :], turned[k][:], z[s][:, k, :], ALU.mult).then_inc(gated_ready, 1)
                    dve.wait_ge(std_ready, g + 1)
                    nc.vector.reciprocal(std[s][:], std[s][:]).then_inc(rstd_ready, 1)
                    dve.wait_ge(rstd_ready, g + 1)
                    for k in range(T):
                        nc.vector.scalar_tensor_tensor(
                            out=row_order(scaled_rows[:, k, :]), in0=gated[s][:, k, :].rearrange("p (c r) -> p c r", r=8),
                            scalar=gain[:, bass.ds(T * g + k, 1)], in1=std[s][:].rearrange("p (c r) -> p c r", r=8),
                            op0=ALU.mult, op1=ALU.mult).then_inc(scaled, 1)
                    dve.wait_ge(scaled, T * g + T)
                    hi = out.hi[:, bass.ds(T * g, T), :]
                    nc.vector.tensor_copy(hi, scaled_rows[:]).then_inc(hi_ready, 1)
                    dve.wait_ge(hi_ready, g + 1)
                    nc.vector.tensor_tensor(out.lo[:, bass.ds(T * g, T), :], scaled_rows[:], hi.bitcast(F32), ALU.subtract
                                            ).then_inc(ready, 1)
                    dve.wait_ge(ready, g + 1)
                steps_of(dve, SG, step)


LAYERS = 2
GATE_MIX, GATE_FFN = 2, 5
SHIFT_MIX, SCALE_MIX, SHIFT_FFN, SCALE_FFN = 0, 1, 3, 4


def gates_of(modT, which):
    return modT[:, KD * which:KD * (which + 1), :]


def load_tables(nc, jobs):
    with stage(nc, "loaded") as (block, loaded):
        @block.sync
        def _(sp):
            for dst, src in jobs:
                sp.dma_start(dst[:], src).then_inc(loaded, 16)
            sp.wait_ge(loaded, 16 * len(jobs))


def on_lanes(vec, n):
    return vec.rearrange("(o n) -> o n", o=1).to_broadcast([P, n])


def build(nc, a, out):
    def dram(name, shape):
        return nc.dram_tensor(name, shape, F32, kind="Internal").ap()

    proj = dram("proj", (5184, TOK))
    mix = dram("mix", (D, TOK))
    rot = dram("rot", (1536, TOK))
    mixed = dram("mixed", (1792, TOK))
    rwkv_arrays = dram("rwkv_arrays", (2, 4, RW, TOK))
    rwkv_dec = dram("rwkv_dec", (2, RW, NCH))
    bonus, gate = dram("bonus", (RW, LAT)), dram("gate", (RW, LAT))
    rwkv_ch = dram("rwkv_ch", (2, NCH, P, 4, RW // 2))
    rwkv_ys = dram("rwkv_ys", (2, RW, LAT))
    gla_arrays = dram("gla_arrays", (2, 3, GKW, TOK))
    gla_dec = dram("gla_dec", (2, GKW, NCH))
    gla_ys = dram("gla_ys", (2, GVW, TOK))
    xbc, acum = dram("xbc", (3072, TOK)), dram("acum", (2 * SG * SH, TOK))
    ssd_ys = dram("ssd_ys", (2, LAT, SI))

    with ExitStack() as ctx:
        sb, _ = memory(nc, ctx)
        xT = sb("xT", [P, KD, TOK])
        ident, ones, block_ones = sb("ident", [P, P]), sb("ones", [P, P]), sb("block_ones", [P, P])
        load_tables(nc, [(ident, a["identity"]), (ones, a["all_ones"]), (block_ones, a["block_ones"])])

        def conditions(c, c_ctx, w_mod, b_mod, gains, final):
            cond_cols, cond = sb("cond_cols", [P, 2 * KD]), sb("cond", [P, KD, 2])
            last_gain = sb("last_gain", [P, KD])
            gain = [sb(f"gain{i}", [P, KD]) for i in range(2 * LAYERS)]
            b_cols = [sb(f"b_cols{i}", [P, 6 * KD]) for i in range(LAYERS)]
            modT = [sb(f"modT{i}", [P, 6 * KD, 2]) for i in range(LAYERS)]
            columns(nc, ident, [(cond_cols[:, 0:KD], c), (cond_cols[:, KD:2 * KD], c_ctx), (last_gain, final)]
                    + list(zip(gain, gains)) + [(b_cols[i], b_mod[i]) for i in range(LAYERS)])
            with stage(nc, "silu_done") as (block, silu_done):
                @block.scalar
                def _(act):
                    for b in range(2):
                        nc.scalar.activation(cond[:, :, b], cond_cols[:, KD * b:KD * (b + 1)], ACT.Silu)
            return gain, last_gain, [(w_mod[i], cond, dram(f"mod_rows_{nc.next_id()}", (2, 6 * D)), b_cols[i], modT[i])
                                     for i in range(LAYERS)]

        def block_of(x_parts, kept, mixers, w_ffn_in, w_ffn_out):
            load_tokens(nc, xT, ident, x_parts)
            gain, last_gain, mods = kept
            for i in range(LAYERS):
                _, _, rows, b_cols, modT = mods[i]
                modulation_columns(nc, ident, rows, b_cols, modT)
                spans = SPANS if i < LAYERS - 1 else SPANS[:1]
                mixers[i](modT, gain[2 * i])
                with ExitStack() as ffn:
                    h = Halves(memory(nc, ffn)[0], "h", [P, KD, TOK])
                    rms_modulate(nc, xT, h, ones, gain[2 * i + 1], modT, SHIFT_FFN, SCALE_FFN, spans)
                    swiglu(nc, xT, h, w_ffn_in[i], w_ffn_out[i], gates_of(modT, GATE_FFN), spans)
            rms_modulate(nc, xT, xT, ones, last_gain, spans=SPANS[:1])

        def project(modT, gain, jobs, by_column=False):
            with ExitStack() as inner:
                h = Halves(memory(nc, inner)[0], "h", [P, KD, TOK])
                rms_modulate(nc, xT, h, ones, gain, modT, SHIFT_MIX, SCALE_MIX, by_column=by_column)
                for w, col0, n, spans in jobs:
                    if n < 256:
                        linear_narrow(nc, h, w, col0, n, proj, col0, spans)
                    else:
                        linear(nc, h, w, col0, n, ("store", proj, col0), spans)

        def add_out(modT, w, spans):
            with ExitStack() as inner:
                h = Halves(memory(nc, inner)[0], "h", [P, KD, TOK])
                load_columns(nc, h, mix, min(t0 for t0, _ in spans))
                linear(nc, h, w, 0, D, ("residual", xT, gates_of(modT, GATE_MIX)), spans)

        def attention_layer(modT, gain):
            project(modT, gain, [(a["w_in_even"][0], 0, 1536, SPANS)])
            with ExitStack() as inner:
                sb, _ = memory(nc, inner)
                cos, sin, gains = sb("cos", [P, TOK]), sb("sin", [P, TOK]), sb("gains", [P, 10])
                window, sinks = sb("window", [P, 4, TOK]), sb("sinks", [P, 8])
                load_tables(nc, [(cos, a["rope_cos"]), (sin, a["rope_sin"]), (window, a["window_mask"]),
                                 (sinks, on_lanes(a["sink_b"][0], 8))])
                columns(nc, ident, [(gains, a["qk_gains"])])
                with stage(nc, "negated") as (block, negated):
                    @block.vector
                    def _(dve):
                        nc.vector.tensor_scalar(sinks[:], sinks[:], -1.0, None, ALU.mult)
                even_mixer(nc, ident, proj, rot, mix, (block_ones, cos, sin), gains[:].rearrange("p (n t) -> p t n", n=2),
                           window, sinks, beside=(first[2][1][0:3], second[2][0][0:3]))
            add_out(modT, a["w_out_even"][0], SPANS)

        def rwkv_layer(modT, gain):
            w = a["w_in_odd"][0]
            project(modT, gain, [(w, 0, 512, SPANS[:1]), (w, 512, 2816, SPANS)])
            with ExitStack() as inner:
                sb, _ = memory(nc, inner)
                mask, exchange = sb("mask", [P, 4, TOK]), sb("exchange", [P, P])
                load_tables(nc, [(mask, a["neighbour_mask"]), (exchange, a["exchange"])])
                attention(nc, ident, 8, proj, 0, 512, 1, proj, 1024, mix, 0, QUERIES_MASKED, HD ** -0.5, mask=mask,
                          rpb=(a["rpb_padded"], exchange), q_from=CTX, beside=second[2][1][0:3])
            with ExitStack() as inner:
                sb, _ = memory(nc, inner)
                mu, kk, ka, rk, w0, a0, ln_w, ln_b = (sb(n, [P, k]) for n, k in (
                    ("mu", 14), ("kk", 4), ("ka", 4), ("rk", 4), ("w0", 8), ("a0", 8), ("ln_w", 4), ("ln_b", 4)))
                reset, masks = sb("reset", [P, TOK]), sb("masks", [P, 2, 10, CH])
                load_tables(nc, [(reset, a["scan_reset"]), (masks, a["chunk_masks"])])
                columns(nc, ident, [(mu, a["shift_mu"][0]), (kk, a["k_k"][0]), (ka, a["k_a"][0]),
                                    (rk, a["r_k"][0].rearrange("h n -> (h n)")), (w0, a["decay_w0"][0].rearrange("d n -> (d n)")),
                                    (a0, a["iclr_a0"][0].rearrange("d n -> (d n)")), (ln_w, a["ln_x_w"][0]), (ln_b, a["ln_x_b"][0])])
                shift_mix(nc, proj, 1536, 14, mu, mixed)
                rwkv_features(nc, mixed, a["decay_w2"][0], a["iclr_a2"][0], a["gate_g2"][0], (kk, ka, rk, w0, a0), block_ones,
                              reset, rwkv_arrays, rwkv_dec, bonus, gate)
                rwkv_chunks(nc, ident, masks, rwkv_arrays, mixed, rwkv_ch)
                rwkv_recurrence(nc, rwkv_ch, rwkv_dec, rwkv_ys)
                rwkv_readout(nc, rwkv_ys, block_ones, ln_w, ln_b, bonus, gate, mix, RW)
            add_out(modT, a["w_out_odd"][0], SPANS[:1])

        def gla_layer(modT, gain):
            w = a["ab_w_in_2"][0]
            project(modT, gain, [(w, 0, 768, SPANS), (w, AB_LR, 32, SPANS), (w, AB_Q, 1792, SPANS)])
            with ExitStack() as inner:
                sb, _ = memory(nc, inner)
                gate_b, gla_gain, v_gain = sb("gate_b", [P, 4]), sb("gla_gain", [P, 4]), sb("v_gain", [P, 4])
                reset, masks = sb("reset", [P, TOK]), sb("masks", [P, 2, 10, CH])
                load_tables(nc, [(reset, a["scan_reset"]), (masks, a["chunk_masks"])])
                columns(nc, ident, [(gate_b, a["ab_gate_b_2"][0].rearrange("d n -> (d n)")), (gla_gain, a["ab_gla_norm_g_2"][0]),
                                    (v_gain, a["ab_vnorm_g_2"][0])])
                gla_features(nc, proj, a["ab_gate_w_2"][0], gate_b, reset, gla_arrays, gla_dec)
                gla_chunks(nc, ident, masks, gla_arrays, proj, gla_dec, gla_ys)
                gla_readout(nc, gla_ys, ones, gla_gain, proj, mix)
                gmlp(nc, ident, ones, proj, a["ab_spatial_w_2"][0], a["ab_spatial_b_2"][0], v_gain, mix)
            add_out(modT, a["ab_w_out_2"][0], SPANS)

        def ssd_layer(modT, gain):
            w = a["ssd_w_in_2"][0]
            project(modT, gain, [(w, 0, 3072, SPANS), (w, SSD_DT, 64, SPANS), (w, SSD_Z, SI, SPANS[:1])], by_column=True)
            with ExitStack() as inner:
                sb, _ = memory(nc, inner)
                ssd_gain = sb("ssd_gain", [P, 16])
                with ExitStack() as scan:
                    sb, _ = memory(nc, scan)
                    taps, bias, skip = sb("taps", [P, 5 * 24]), sb("bias", [P, 24]), sb("skip", [P, SG * SH])
                    reset, mask = sb("reset", [P, TOK]), sb("mask", [P, 2, SC])
                    by_token = [sb(f"by_token{n}", [P, NSC, 2 * SG * SH]) for n in range(4)]
                    load_tables(nc, [(reset, a["scan_reset_ssd"]), (mask, a["ssd_mask"]),
                                     (skip, on_lanes(a["ssd_d_2"][0], SG * SH))])
                    columns(nc, ident, [(taps[:, 24 * j:24 * (j + 1)], a["ssd_conv_w_2"][0, j]) for j in range(5)]
                            + [(bias, a["ssd_conv_b_2"][0]), (ssd_gain, a["ssd_norm_g_2"][0])])
                    conv_silu(nc, proj, 24, taps, bias, xbc)
                    ssd_steps(nc, ident, proj, a["ssd_dt_bias_2"][0], a["ssd_a_log_2"][0], reset, by_token, acum)
                    ssd_groups(nc, ident, mask, by_token, acum, xbc, skip, ssd_ys)
                wide = Halves(memory(nc, inner)[0], "wide", [P, SI // P, LAT])
                ssd_readout(nc, ident, ones, ssd_ys, proj, ssd_gain, wide)
                linear(nc, wide, a["ssd_w_out_2"][0], 0, D, ("residual", xT, gates_of(modT, GATE_MIX)), SPANS[:1], x0=CTX)

        first = conditions(a["c"][0], a["c_ctx"], a["w_mod"], a["b_mod"],
                           [a["norm_mix"][0], a["norm_ffn"][0], a["norm_mix"][1], a["norm_ffn"][1]], a["norm_out"])
        second = conditions(a["c_2"][0], a["c_ctx_2"], a["mod_w_2"], a["mod_b_2"],
                            [a["norm_g_2"][0, 0], a["norm_g_2"][0, 1], a["norm_g_2"][1, 0], a["norm_g_2"][1, 1]],
                            a["final_norm_g_2"])
        modulation_rows(nc, *first[2][0][0:3])
        block_of([(a["ctx"][0], 0), (a["x"][0], CTX)], first, (attention_layer, rwkv_layer), a["w_ffn_in"], a["w_ffn_out"])
        block_of([(a["ctx_2"][0], 0)], second, (gla_layer, ssd_layer), a["ffn_w_in_2"], a["ffn_w_out_2"])
        store_tokens(nc, xT, ident, out)



def rope_tables():
    t = np.arange(LAT)
    inv = 10000.0 ** (-np.arange(16) / 16)
    ang = np.concatenate([(t // 64)[:, None] * inv, (t % 64)[:, None] * inv], -1).T
    cos, sin = np.ones((P, TOK), np.float32), np.zeros((P, TOK), np.float32)
    for h in range(4):
        cos[32 * h:32 * h + 32, CTX:] = np.cos(ang)
        sin[32 * h:32 * h + 32, CTX:] = np.sin(ang) * (1 if h % 2 else -1)
    return cos, sin


def window_mask():
    q, k = np.arange(LAT)[:, None], np.arange(LAT)[None]
    m = np.zeros((LAT, TOK), np.float32)
    m[:, CTX:] = np.where(np.abs(q - k) <= 128, 0, NEG)
    return np.ascontiguousarray(m.reshape(4, P, TOK).transpose(1, 0, 2))


def neighbour_mask():
    q, k = np.arange(LAT)[:, None] % 64, np.arange(LAT)[None] % 64
    start = np.clip(q - 8, 0, 48)
    m = np.zeros((LAT, TOK), np.float32)
    m[:, CTX:] = np.where((k >= start) & (k < start + 16), 0, NEG)
    return np.ascontiguousarray(m.reshape(4, P, TOK).transpose(1, 0, 2))


def chunk_masks():
    j, t = np.arange(64)[:, None], np.arange(64)[None]
    out = np.zeros((64, 2, 10, 64), np.float32)
    for d in range(2):
        before, pos = (j < t, t) if d == 0 else (j > t, 63 - t)
        out[:, d, 0], out[:, d, 1], out[:, d, 2] = before, before | (j == t), -1.0 * (before | (j == t))
        for n in range(6):
            s = 1 << n
            out[:, d, 3 + n] = -1.0 * (before & (j // (2 * s) == t // (2 * s)) & (j // s != t // s))
        out[:, d, 9] = j == t
    return np.concatenate([out, out])


def scan_reset():
    m = np.ones((P, TOK), np.float32)
    m[:, ::64] = 0
    return m


def scan_reset_ssd():
    m = np.ones((P, TOK), np.float32)
    m[:, ::128] = 0
    return m


def ssd_mask():
    s, l = np.arange(128)[:, None], np.arange(128)[None]
    out = np.zeros((128, 2, 128), np.float32)
    out[:, 0], out[:, 1] = np.where(s <= l, 0, NEG), np.where(s >= l, 0, NEG)
    return out


def tables():
    cos, sin = rope_tables()
    exchange = np.zeros((P, P), np.float32)
    for p in range(P):
        exchange[p, p // 64 * 64 + 63 - p % 64] = HD ** 0.5
    return {"identity": np.eye(P, dtype=np.float32), "all_ones": np.ones((P, P), np.float32),
            "block_ones": np.kron(np.eye(2), np.ones((HD, HD))).astype(np.float32),
            "rope_cos": cos, "rope_sin": sin, "window_mask": window_mask(), "neighbour_mask": neighbour_mask(),
            "exchange": exchange, "scan_reset": scan_reset(), "scan_reset_ssd": scan_reset_ssd(),
            "chunk_masks": chunk_masks(), "ssd_mask": ssd_mask()}


def kernel(**inputs):
    import concourse.bacc as bacc
    from concourse.bass_utils import run_bass_kernel_spmd

    arrays = {n: np.ascontiguousarray(v) for n, v in inputs.items()}
    rpb = arrays.pop("rpb_c")
    padded = np.zeros((8, 15, 127), rpb.dtype)
    padded[:, :, 48:79] = rpb[0]
    arrays["rpb_padded"] = padded
    q, k = arrays.pop("q_norm_a")[0], arrays.pop("k_norm_a")[0]
    swap = lambda g: np.concatenate([g[32:], g[:32]])
    arrays["qk_gains"] = np.concatenate([g for turn in (lambda g: g, swap) for g in [turn(q)] * 8 + [turn(k)] * 2])
    arrays.update(tables())

    nc = bacc.Bacc("TRN2", target_bir_lowering=False, num_devices=1)
    aps = {n: nc.dram_tensor(f"in_{n}", v.shape, mybir.dt.from_np(v.dtype), kind="ExternalInput").ap()
           for n, v in arrays.items()}
    out = nc.dram_tensor("out_0", (LAT, D), F32, kind="ExternalOutput").ap()
    build(nc, aps, out)
    got = run_bass_kernel_spmd(nc, [{f"in_{n}": v for n, v in arrays.items()}], core_ids=[0])
    return got.results[0]["out_0"].reshape(1, LAT, D)
```
